# Optimizing a Trainium2 kernel written in Bass

```python
import math
import functools
import jax
import jax.numpy as jnp
from jax import lax
import numpy as np

D_MODEL = 1024
BATCH = 1
SEQ = 256
DEPTH = 2

HEAD_DIM = 64
D_FF = 2816
MACARON_WEIGHT = 0.5
NORM_EPS = 1e-6
QBLK = 128
GATHER_QBLK = 16
NEG_INF = -1e30
FORCE_SCORE = 1e9

REL_BUCKETS = 32
REL_MAX_DIST = 1024
A_SLOT = 0
C_SLOT = 8
D_SLOT = 16
REL_SLOTS = 24

A_HEADS = 8
A_KV_HEADS = 2
A_WINDOW = 128

B_HEADS = 8
MLA_Q_RANK = 256
MLA_KV_RANK = 128
MLA_NOPE = 64
MLA_ROPE = 32
MLA_V = 64
ROPE_THETA = 10000.0

C_HEADS = 8
C_KV_HEADS = 2
CMP_BLOCK = 32
CMP_STRIDE = 16
CMP_HIDDEN = 256
SEL_BLOCK = 64
SEL_TOPK = 8
NSA_WINDOW = 256

D_HEADS = 8
MOBA_BLOCK = 256
MOBA_TOPK = 3

AB_COLS = (A_HEADS * HEAD_DIM, A_KV_HEADS * HEAD_DIM, A_KV_HEADS * HEAD_DIM, MLA_Q_RANK, MLA_KV_RANK, MLA_ROPE)
CD_COLS = (C_HEADS * HEAD_DIM,) + (C_KV_HEADS * HEAD_DIM,) * 6 + (3 * C_HEADS,) + (D_HEADS * HEAD_DIM,) * 3
AB_OUT = A_HEADS * HEAD_DIM + B_HEADS * MLA_V
CD_OUT = C_HEADS * HEAD_DIM + D_HEADS * HEAD_DIM

kernel_name = 'hybrid_swa_mla_nsa_moba_macaron'

def split_cols(z, sizes):
    return jnp.split(z, np.cumsum(sizes)[:-1].tolist(), axis=-1)

def rms_norm(x, g):
    xf = x.astype(jnp.float32)
    y = xf * lax.rsqrt(jnp.mean(xf * xf, axis=-1, keepdims=True) + NORM_EPS)
    return (y * g.astype(jnp.float32)).astype(x.dtype)

def swiglu(h, wg, wu, wd):
    return (jax.nn.silu(h @ wg) * (h @ wu)) @ wd

def sandwich(x, pre, post, fn, weight):
    return x + weight * rms_norm(fn(rms_norm(x, pre)), post)

def t5_bucket(dist):
    n = jnp.maximum(dist, 0)
    exact = REL_BUCKETS // 2
    nf = jnp.maximum(n, 1).astype(jnp.float32)
    large = exact + (jnp.log(nf / exact) / math.log(REL_MAX_DIST / exact) * (REL_BUCKETS - exact)).astype(jnp.int32)
    return jnp.where(n < exact, n, jnp.minimum(large, REL_BUCKETS - 1))

def rope_tables(S):
    inv = ROPE_THETA ** (-jnp.arange(0, MLA_ROPE, 2, dtype=jnp.float32) / MLA_ROPE)
    ang = jnp.arange(S, dtype=jnp.float32)[:, None] * inv[None, :]
    return jnp.cos(ang), jnp.sin(ang)

def apply_rope(x, cos, sin):
    x1, x2 = jnp.split(x, 2, axis=-1)
    return jnp.concatenate([x1 * cos - x2 * sin, x2 * cos + x1 * sin], axis=-1).astype(x.dtype)

def band_blocks(t, window):
    B, S = t.shape[:2]
    nb = S // QBLK
    tp = jnp.pad(t, [(0, 0), (window, 0)] + [(0, 0)] * (t.ndim - 2))
    parts = [tp[:, j * QBLK:j * QBLK + S].reshape((B, nb, QBLK) + t.shape[2:]) for j in range(window // QBLK + 1)]
    return jnp.concatenate(parts, axis=2)

def band_attention(q, k, v, window, bias_cols, sinks=None):
    B, S, Hkv, G, Dh = q.shape
    nb = S // QBLK
    span = window + QBLK
    qb = q.reshape(B, nb, QBLK, Hkv, G, Dh)
    kb = band_blocks(k, window)
    vb = band_blocks(v, window)
    kk = jnp.arange(span)[None, :]
    dist = jnp.arange(QBLK)[:, None] + window - kk
    kpos = jnp.arange(nb)[:, None, None] * QBLK - window + kk[None]
    valid = (dist >= 0) & (dist < window) & (kpos >= 0)
    bias = bias_cols.astype(jnp.float32)[t5_bucket(dist)].reshape(QBLK, span, Hkv, G).transpose(2, 3, 0, 1)
    s = jnp.einsum('bnqhgd,bnkhd->bnhgqk', qb, kb).astype(jnp.float32) * Dh ** -0.5 + bias
    s = jnp.where(valid[None, :, None, None], s, NEG_INF)
    if sinks is not None:
        sink = jnp.broadcast_to(sinks.astype(jnp.float32).reshape(Hkv, G, 1, 1), s.shape[:-1] + (1,))
        p = jax.nn.softmax(jnp.concatenate([s, sink], axis=-1), axis=-1)[..., :-1]
    else:
        p = jax.nn.softmax(s, axis=-1)
    o = jnp.einsum('bnhgqk,bnkhd->bnqhgd', p.astype(v.dtype), vb)
    return o.reshape(B, S, Hkv, G, -1)

def causal_block_attention(q, k, v):
    B, S, H, Dk = q.shape
    nb = S // QBLK
    kpos = jnp.arange(S)

    def block(args):
        qb, i = args
        qpos = i * QBLK + jnp.arange(QBLK)
        s = jnp.einsum('bqhd,bkhd->bhqk', qb, k).astype(jnp.float32) * Dk ** -0.5
        s = jnp.where(kpos[None, :] <= qpos[:, None], s, NEG_INF)
        p = jax.nn.softmax(s, axis=-1).astype(v.dtype)
        return jnp.einsum('bhqk,bkhd->bqhd', p, v)

    qs = q.reshape(B, nb, QBLK, H, Dk).swapaxes(0, 1)
    o = lax.map(block, (qs, jnp.arange(nb)))
    return o.swapaxes(0, 1).reshape(B, S, H, -1)

def gather_blocks(blocks, idx):
    return jax.vmap(jax.vmap(lambda b, i: b[i]))(blocks, idx)

def nsa_compressed(q, k, v, pe_k, pe_v, wk1, wk2, wv1, wv2):
    B, S, Hkv, G, Dh = q.shape
    n_c = (S - CMP_BLOCK) // CMP_STRIDE + 1
    starts = jnp.arange(n_c) * CMP_STRIDE
    cidx = starts[:, None] + jnp.arange(CMP_BLOCK)[None, :]

    def compress(t, pe, w1, w2):
        blk = t[:, cidx] + pe[None, None, :, None, :]
        blk = blk.transpose(0, 1, 3, 2, 4).reshape(B, n_c, Hkv, CMP_BLOCK * Dh)
        return jax.nn.silu(blk @ w1) @ w2

    k_cmp = compress(k, pe_k, wk1, wk2)
    v_cmp = compress(v, pe_v, wv1, wv2)
    valid = (starts + CMP_BLOCK - 1)[None, :] <= jnp.arange(S)[:, None]
    s = jnp.einsum('bshgd,bchd->bhgsc', q, k_cmp).astype(jnp.float32) * Dh ** -0.5
    p = jax.nn.softmax(jnp.where(valid, s, NEG_INF), axis=-1) * valid
    o = jnp.einsum('bhgsc,bchd->bshgd', p.astype(v_cmp.dtype), v_cmp)
    return o, p

def nsa_select(p_cmp, S):
    n_c = p_cmp.shape[-1]
    n_s = S // SEL_BLOCK
    c_start = jnp.arange(n_c)[:, None] * CMP_STRIDE
    j_start = jnp.arange(n_s)[None, :] * SEL_BLOCK
    overlap = ((c_start < j_start + SEL_BLOCK) & (c_start + CMP_BLOCK > j_start)).astype(jnp.float32)
    imp = jnp.einsum('bhgsc,cj->bhsj', p_cmp, overlap)
    cur = (jnp.arange(S) // SEL_BLOCK)[:, None]
    j = jnp.arange(n_s)[None, :]
    forced = (j == 0) | (j == cur) | (j == cur - 1)
    imp = jnp.where(forced, FORCE_SCORE, jnp.where(j <= cur, imp, NEG_INF))
    _, idx = lax.top_k(imp, min(SEL_TOPK, n_s))
    return idx

def nsa_selected(q, k, v, idx, bias_cols):
    B, S, Hkv, G, Dh = q.shape
    n_s = S // SEL_BLOCK
    top = idx.shape[-1]
    nq = S // GATHER_QBLK
    k_blk = k.reshape(B, n_s, SEL_BLOCK, Hkv, Dh).transpose(0, 3, 1, 2, 4)
    v_blk = v.reshape(B, n_s, SEL_BLOCK, Hkv, Dh).transpose(0, 3, 1, 2, 4)
    tab = bias_cols.astype(jnp.float32).reshape(REL_BUCKETS, Hkv, G).transpose(1, 0, 2)
    h_ix = jnp.arange(Hkv)[None, :, None, None, None]

    def block(args):
        qb, ib, i = args
        qpos = i * GATHER_QBLK + jnp.arange(GATHER_QBLK)
        kg = gather_blocks(k_blk, ib)
        vg = gather_blocks(v_blk, ib)
        dist = qpos[None, None, :, None, None] - (ib[..., None] * SEL_BLOCK + jnp.arange(SEL_BLOCK))
        bias = jnp.moveaxis(tab[h_ix, t5_bucket(dist)], -1, 2)
        s = jnp.einsum('bqhgd,bhqkld->bhgqkl', qb, kg).astype(jnp.float32) * Dh ** -0.5 + bias
        s = jnp.where(dist[:, :, None] >= 0, s, NEG_INF).reshape(B, Hkv, G, GATHER_QBLK, top * SEL_BLOCK)
        p = jax.nn.softmax(s, axis=-1).astype(vg.dtype).reshape(B, Hkv, G, GATHER_QBLK, top, SEL_BLOCK)
        return jnp.einsum('bhgqkl,bhqkld->bqhgd', p, vg)

    qs = q.reshape(B, nq, GATHER_QBLK, Hkv, G, Dh).swapaxes(0, 1)
    ids = idx.reshape(B, Hkv, nq, GATHER_QBLK, top).transpose(2, 0, 1, 3, 4)
    o = lax.map(block, (qs, ids, jnp.arange(nq)))
    return o.swapaxes(0, 1).reshape(B, S, Hkv, G, Dh)

def moba_attention(q, k, v, bias_cols):
    B, S, H, Dh = q.shape
    n_b = -(-S // MOBA_BLOCK)
    pad = n_b * MOBA_BLOCK - S
    kp = jnp.pad(k, ((0, 0), (0, pad), (0, 0), (0, 0)))
    vp = jnp.pad(v, ((0, 0), (0, pad), (0, 0), (0, 0)))
    k_blk = kp.reshape(B, n_b, MOBA_BLOCK, H, Dh)
    k_mean = jnp.mean(k_blk.astype(jnp.float32), axis=2)
    cur = (jnp.arange(S) // MOBA_BLOCK)[:, None]
    past = jnp.arange(n_b)[None, :] < cur
    gate = jnp.einsum('bshd,bnhd->bhsn', q.astype(jnp.float32), k_mean)
    top = min(MOBA_TOPK, n_b)
    _, idx = lax.top_k(jnp.where(past, gate, NEG_INF), top)
    k_bh = k_blk.transpose(0, 3, 1, 2, 4)
    v_bh = vp.reshape(B, n_b, MOBA_BLOCK, H, Dh).transpose(0, 3, 1, 2, 4)
    tab = bias_cols.astype(jnp.float32)
    tab_h = tab.T
    h_ix = jnp.arange(H)[None, :, None, None, None]
    nq = S // GATHER_QBLK
    scale = Dh ** -0.5

    def block(args):
        qb, ib, i = args
        qpos = i * GATHER_QBLK + jnp.arange(GATHER_QBLK)
        own = (i * GATHER_QBLK) // MOBA_BLOCK
        kg = gather_blocks(k_bh, ib)
        vg = gather_blocks(v_bh, ib)
        dist_sel = qpos[None, None, :, None, None] - (ib[..., None] * MOBA_BLOCK + jnp.arange(MOBA_BLOCK))
        s_sel = jnp.einsum('bqhd,bhqjld->bhqjl', qb, kg).astype(jnp.float32) * scale + tab_h[h_ix, t5_bucket(dist_sel)]
        s_sel = jnp.where((ib < own)[..., None], s_sel, NEG_INF).reshape(B, H, GATHER_QBLK, top * MOBA_BLOCK)
        k_own = lax.dynamic_slice_in_dim(kp, own * MOBA_BLOCK, MOBA_BLOCK, axis=1)
        v_own = lax.dynamic_slice_in_dim(vp, own * MOBA_BLOCK, MOBA_BLOCK, axis=1)
        dist_own = qpos[:, None] - (own * MOBA_BLOCK + jnp.arange(MOBA_BLOCK))[None, :]
        s_own = jnp.einsum('bqhd,bkhd->bhqk', qb, k_own).astype(jnp.float32) * scale + jnp.moveaxis(tab[t5_bucket(dist_own)], -1, 0)
        s_own = jnp.where(dist_own >= 0, s_own, NEG_INF)
        p = jax.nn.softmax(jnp.concatenate([s_sel, s_own], axis=-1), axis=-1).astype(v.dtype)
        p_sel = p[..., :top * MOBA_BLOCK].reshape(B, H, GATHER_QBLK, top, MOBA_BLOCK)
        p_own = p[..., top * MOBA_BLOCK:]
        return jnp.einsum('bhqjl,bhqjld->bqhd', p_sel, vg) + jnp.einsum('bhqk,bkhd->bqhd', p_own, v_own)

    qs = q.reshape(B, nq, GATHER_QBLK, H, Dh).swapaxes(0, 1)
    ids = idx.reshape(B, H, nq, GATHER_QBLK, top).transpose(2, 0, 1, 3, 4)
    o = lax.map(block, (qs, ids, jnp.arange(nq)))
    return o.swapaxes(0, 1).reshape(B, S, H, Dh)

def mixer_swa_mla(h, w_in, sinks, q_norm, w_uq, kv_norm, w_ukv, w_out, rel_table):
    B, S, _ = h.shape
    qa, ka, va, cq, ckv, kr = split_cols(h @ w_in, AB_COLS)
    kv_shape = (B, S, A_KV_HEADS, HEAD_DIM)
    qa = qa.reshape(B, S, A_KV_HEADS, A_HEADS // A_KV_HEADS, HEAD_DIM)
    o_a = band_attention(qa, ka.reshape(kv_shape), va.reshape(kv_shape), A_WINDOW,
                         rel_table[:, A_SLOT:A_SLOT + A_HEADS], sinks)
    q = (rms_norm(cq, q_norm) @ w_uq).reshape(B, S, B_HEADS, MLA_NOPE + MLA_ROPE)
    kv = (rms_norm(ckv, kv_norm) @ w_ukv).reshape(B, S, B_HEADS, MLA_NOPE + MLA_V)
    cos, sin = rope_tables(S)
    q = jnp.concatenate([q[..., :MLA_NOPE], apply_rope(q[..., MLA_NOPE:], cos[:, None], sin[:, None])], axis=-1)
    kr = apply_rope(kr, cos, sin)
    k = jnp.concatenate([kv[..., :MLA_NOPE], jnp.broadcast_to(kr[:, :, None, :], (B, S, B_HEADS, MLA_ROPE))], axis=-1)
    o_b = causal_block_attention(q, k, kv[..., MLA_NOPE:])
    o = jnp.concatenate([o_a.reshape(B, S, -1), o_b.reshape(B, S, -1)], axis=-1)
    return o @ w_out

def mixer_nsa_moba(h, w_in, pe_k, pe_v, wk1, wk2, wv1, wv2, w_out, rel_table):
    B, S, _ = h.shape
    G = C_HEADS // C_KV_HEADS
    qc, kc, vc, ks, vs, kw, vw, gl, qd, kd, vd = split_cols(h @ w_in, CD_COLS)
    kv_shape = (B, S, C_KV_HEADS, HEAD_DIM)
    qc = qc.reshape(B, S, C_KV_HEADS, G, HEAD_DIM)
    c_cols = rel_table[:, C_SLOT:C_SLOT + C_HEADS]
    o_cmp, p_cmp = nsa_compressed(qc, kc.reshape(kv_shape), vc.reshape(kv_shape), pe_k, pe_v, wk1, wk2, wv1, wv2)
    sel_idx = nsa_select(p_cmp, S)
    o_slc = nsa_selected(qc, ks.reshape(kv_shape), vs.reshape(kv_shape), sel_idx, c_cols)
    o_win = band_attention(qc, kw.reshape(kv_shape), vw.reshape(kv_shape), NSA_WINDOW, c_cols)
    g = jax.nn.sigmoid(gl).reshape(B, S, 3, C_KV_HEADS, G, 1)
    o_c = g[:, :, 0] * o_cmp + g[:, :, 1] * o_slc + g[:, :, 2] * o_win
    d_shape = (B, S, D_HEADS, HEAD_DIM)
    o_d = moba_attention(qd.reshape(d_shape), kd.reshape(d_shape), vd.reshape(d_shape),
                         rel_table[:, D_SLOT:D_SLOT + D_HEADS])
    o = jnp.concatenate([o_c.reshape(B, S, -1), o_d.reshape(B, S, -1)], axis=-1)
    return o @ w_out

def setup_inputs(seed: int = 0) -> dict:
    key = jax.random.key(seed)
    keys = iter(jax.random.split(key, 64))

    def normal(shape, scale):
        return scale * jax.random.normal(next(keys), shape, jnp.float32)

    def dense(fan_in, fan_out):
        return normal((fan_in, fan_out), fan_in ** -0.5)

    def gain(n):
        return 1.0 + normal((n,), 0.05)

    def add_ffn(d, prefix):
        d[prefix + '_pre'] = gain(D_MODEL)
        d[prefix + '_post'] = gain(D_MODEL)
        d[prefix + '_wg'] = dense(D_MODEL, D_FF)
        d[prefix + '_wu'] = dense(D_MODEL, D_FF)
        d[prefix + '_wd'] = dense(D_FF, D_MODEL)

    d = {}
    d['x'] = normal((BATCH, SEQ, D_MODEL), 1.0)
    d['rel_bias_table'] = normal((REL_BUCKETS, REL_SLOTS), 0.3)
    add_ffn(d, 'l0_ffn1')
    d['l0_mix_pre'] = gain(D_MODEL)
    d['l0_mix_post'] = gain(D_MODEL)
    d['l0_w_in'] = dense(D_MODEL, sum(AB_COLS))
    d['l0_sinks'] = normal((A_HEADS,), 0.5)
    d['l0_mla_q_norm'] = gain(MLA_Q_RANK)
    d['l0_mla_w_uq'] = dense(MLA_Q_RANK, B_HEADS * (MLA_NOPE + MLA_ROPE))
    d['l0_mla_kv_norm'] = gain(MLA_KV_RANK)
    d['l0_mla_w_ukv'] = dense(MLA_KV_RANK, B_HEADS * (MLA_NOPE + MLA_V))
    d['l0_w_out'] = dense(AB_OUT, D_MODEL)
    add_ffn(d, 'l0_ffn2')
    add_ffn(d, 'l1_ffn1')
    d['l1_mix_pre'] = gain(D_MODEL)
    d['l1_mix_post'] = gain(D_MODEL)
    d['l1_w_in'] = dense(D_MODEL, sum(CD_COLS))
    d['l1_nsa_pe_k'] = normal((CMP_BLOCK, HEAD_DIM), 0.3)
    d['l1_nsa_pe_v'] = normal((CMP_BLOCK, HEAD_DIM), 0.3)
    d['l1_nsa_wk1'] = dense(CMP_BLOCK * HEAD_DIM, CMP_HIDDEN)
    d['l1_nsa_wk2'] = dense(CMP_HIDDEN, HEAD_DIM)
    d['l1_nsa_wv1'] = dense(CMP_BLOCK * HEAD_DIM, CMP_HIDDEN)
    d['l1_nsa_wv2'] = dense(CMP_HIDDEN, HEAD_DIM)
    d['l1_w_out'] = dense(CD_OUT, D_MODEL)
    add_ffn(d, 'l1_ffn2')
    return d

def reference(x, rel_bias_table,
              l0_ffn1_pre, l0_ffn1_post, l0_ffn1_wg, l0_ffn1_wu, l0_ffn1_wd,
              l0_mix_pre, l0_mix_post, l0_w_in, l0_sinks, l0_mla_q_norm, l0_mla_w_uq,
              l0_mla_kv_norm, l0_mla_w_ukv, l0_w_out,
              l0_ffn2_pre, l0_ffn2_post, l0_ffn2_wg, l0_ffn2_wu, l0_ffn2_wd,
              l1_ffn1_pre, l1_ffn1_post, l1_ffn1_wg, l1_ffn1_wu, l1_ffn1_wd,
              l1_mix_pre, l1_mix_post, l1_w_in, l1_nsa_pe_k, l1_nsa_pe_v,
              l1_nsa_wk1, l1_nsa_wk2, l1_nsa_wv1, l1_nsa_wv2, l1_w_out,
              l1_ffn2_pre, l1_ffn2_post, l1_ffn2_wg, l1_ffn2_wu, l1_ffn2_wd):
    mixer0 = functools.partial(mixer_swa_mla, w_in=l0_w_in, sinks=l0_sinks, q_norm=l0_mla_q_norm,
                               w_uq=l0_mla_w_uq, kv_norm=l0_mla_kv_norm, w_ukv=l0_mla_w_ukv,
                               w_out=l0_w_out, rel_table=rel_bias_table)
    mixer1 = functools.partial(mixer_nsa_moba, w_in=l1_w_in, pe_k=l1_nsa_pe_k, pe_v=l1_nsa_pe_v,
                               wk1=l1_nsa_wk1, wk2=l1_nsa_wk2, wv1=l1_nsa_wv1, wv2=l1_nsa_wv2,
                               w_out=l1_w_out, rel_table=rel_bias_table)
    layers = (
        ((l0_ffn1_pre, l0_ffn1_post, l0_ffn1_wg, l0_ffn1_wu, l0_ffn1_wd), (l0_mix_pre, l0_mix_post), mixer0,
         (l0_ffn2_pre, l0_ffn2_post, l0_ffn2_wg, l0_ffn2_wu, l0_ffn2_wd)),
        ((l1_ffn1_pre, l1_ffn1_post, l1_ffn1_wg, l1_ffn1_wu, l1_ffn1_wd), (l1_mix_pre, l1_mix_post), mixer1,
         (l1_ffn2_pre, l1_ffn2_post, l1_ffn2_wg, l1_ffn2_wu, l1_ffn2_wd)),
    )
    for layer in range(DEPTH):
        ffn1, mix_norms, mixer, ffn2 = layers[layer]
        x = sandwich(x, ffn1[0], ffn1[1], functools.partial(swiglu, wg=ffn1[2], wu=ffn1[3], wd=ffn1[4]), MACARON_WEIGHT)
        x = sandwich(x, mix_norms[0], mix_norms[1], mixer, 1.0)
        x = sandwich(x, ffn2[0], ffn2[1], functools.partial(swiglu, wg=ffn2[2], wu=ffn2[3], wd=ffn2[4]), MACARON_WEIGHT)
    return x


_drawn_inputs = setup_inputs


def setup_inputs(seed=0):
    import zlib

    import numpy as np

    out = dict(_drawn_inputs(seed))
    spreads = {}
    factors = {'l0_sinks': 7.022,
     'l0_ffn2_post': 3.419,
     'l1_ffn1_post': 3.712,
     'l1_nsa_pe_k': 5.097,
     'l1_ffn2_pre': 2.966,
     'l1_ffn2_post': 4.397,
     'l1_mix_post': 3.24}
    for name, (base, spread) in spreads.items():
        noise = np.random.default_rng([zlib.crc32(name.encode()), seed]).standard_normal(out[name].shape)
        drawn = base * np.exp(spread * noise) if base else spread * noise
        out[name] = jnp.asarray(drawn.astype(out[name].dtype))
    for name, factor in factors.items():
        out[name] = (out[name] * factor).astype(out[name].dtype)
    return out
```

```python
import math
from contextlib import ExitStack

import numpy as np

import concourse.bass as bass
from concourse import mybir

F32 = mybir.dt.float32
F32R = mybir.dt.float32r
ALU = mybir.AluOpType
ACT = mybir.ActivationFunctionType
AX = mybir.AxisListType.X

P = 128
SEQ = 256
TILES = SEQ // P
D = 1024
KD = D // P
DFF = 2816
EPS = 1e-6
BIG = 1e30

HEAD = 64
HEADS = 8
BUCKETS, SLOTS, MAX_DIST = 32, 24, 1024
MLA_Q, MLA_KV, NOPE, ROPE = 256, 128, 64, 32
MLA_K = NOPE + ROPE
CMP_BLOCK, CMP_STRIDE, CMP_HID = 32, 16, 256
NCMP = (SEQ - CMP_BLOCK) // CMP_STRIDE + 1
CPAD = 16
CROW = 32

FB = 256
FBLOCKS = DFF // FB
FC = FB // P
PEEL = 3
MAIN = KD * 512
DOWN = FC * D

FFNS = ("l0_ffn1", "l0_ffn2", "l1_ffn1", "l1_ffn2")
STAGES = ("l0_ffn1", "l0_mix", "l0_ffn2", "l1_ffn1", "l1_mix", "l1_ffn2")
MIX0_BLOCKS = ((0, 512), (512, 512), (1024, 160))
MIX1_BLOCKS = ((0, 512), (512, 512), (1024, 280), (1304, 512), (1816, 512), (2328, 512))


def bucket_ranges():
    n = np.arange(SEQ)
    nf = np.maximum(n, 1).astype(np.float32)
    exact = BUCKETS // 2
    large = exact + (np.log(nf / np.float32(exact)) / np.float32(math.log(MAX_DIST / exact))
                     * np.float32(BUCKETS - exact)).astype(np.int32)
    bucket = np.where(n < exact, n, np.minimum(large, BUCKETS - 1))
    return [(int(b), int(np.flatnonzero(bucket == b)[0]), int(np.flatnonzero(bucket == b)[-1]))
            for b in np.unique(bucket)]


BUCKET_RANGES = bucket_ranges()


def trunk(nc, a, out):
    n_mix0 = len(MIX0_BLOCKS) + 3
    n_mix1 = len(MIX1_BLOCKS) + 4
    counts = {"l0_mix": n_mix0, "l1_mix": n_mix1}
    first_block, n = {}, 0
    for s in STAGES:
        first_block[s] = n
        n += counts.get(s, FBLOCKS)
    total_blocks = n

    def main_dmas(n):
        for s in STAGES:
            if s in FFNS and first_block[s] <= n < first_block[s] + FBLOCKS:
                return 2
        return 2 if n == first_block["l0_mix"] + len(MIX0_BLOCKS) else 1

    def landed_value(n):
        return 16 * sum(main_dmas(m) for m in range(n % 2, n + 1, 2))

    job_counts = [("prep", 2), ("norm0", 8), ("norm1", 8), ("qa", 4), ("ka", 1), ("lat", 3), ("mla", 16),
                  ("out0", 8), ("norm2", 8), ("norm3", 8), ("norm4", 8), ("qc", 4), ("kvc", 2), ("ks", 1),
                  ("kw", 1), ("qd", 4), ("kd", 4), ("out1", 8), ("norm5", 8)]
    job_base, n = {}, 0
    for name, k in job_counts:
        job_base[name] = n
        n += k

    hi_base, n = {}, 0
    for name, k in job_counts:
        if name.startswith(("norm", "out", "lat")):
            hi_base[name] = n
            n += k

    proj_base = {"w_in0": 0, "up": 2 * len(MIX0_BLOCKS), "w_in1": 2 * len(MIX0_BLOCKS) + 4}
    rstd_base, n = {}, 0
    for name, k in [("pre0", 2), ("post0", 2), ("pre1", 2), ("lat", 4), ("post1", 2), ("pre2", 2), ("post2", 2),
                    ("pre3", 2), ("post3", 2), ("pre4", 2), ("post4", 2), ("pre5", 2), ("post5", 2)]:
        rstd_base[name] = n
        n += k
    n_rstd = n
    OUT = {"w_in0": [2, 4, 6], "up": [10, 18], "w_in1": [20, 24, 30, 32, 34, 36]}
    ATT = {"swa": 0, "mla": 1, "slc": 2, "win": 3, "moba": 4}
    UNITS = TILES * HEADS
    OUT_BEFORE = {"swa": 0, "mla": 2, "slc0": 4, "slc": 6, "win": 8, "moba": 10, "end": 12}

    G_PRE, G_Q, G_KV, G_PEK, G_PEV, G_ROWS = 0, 48, 50, 51, 67, 83

    with ExitStack() as ctx:
        def sb(name, shape, dt=F32):
            return ctx.enter_context(nc.sbuf_tensor(name, shape, dt))

        def sem(name):
            return ctx.enter_context(nc.semaphore(name))

        ps = ctx.enter_context(nc.psum_tensor("ps", [P, 8, 512], F32))

        raw = sb("raw", [P, 2, MAIN])
        w_hi = sb("w_hi", [P, 2, MAIN], F32R)
        w_lo = sb("w_lo", [P, 2, MAIN], F32R)
        raw_down = sb("raw_down", [P, DOWN])
        down_hi = sb("down_hi", [P, DOWN], F32R)
        down_lo = sb("down_lo", [P, DOWN], F32R)
        x = sb("x", [P, TILES, D])
        xn = sb("xn", [P, TILES, D])
        xt_hi = sb("xt_hi", [P, KD, SEQ], F32R)
        xt_lo = sb("xt_lo", [P, KD, SEQ], F32R)
        gpost = sb("gpost", [P, D])
        h = sb("h", [P, TILES, FB])
        ht_hi = sb("ht_hi", [P, FC, SEQ], F32R)
        ht_lo = sb("ht_lo", [P, FC, SEQ], F32R)
        bias = sb("bias", [P, 2 * HEADS, SEQ])
        qk = sb("qk", [P, 8, SEQ])
        val = sb("val", [P, TILES, 512])
        val2 = sb("val2", [P, TILES, 2, P])
        logit = sb("logit", [P, 3, SEQ])
        probt = sb("probt", [P, 3, SEQ])
        ident = sb("ident", [P, P])
        flip = sb("flip", [P, P])
        causal = sb("causal", [P, SEQ])
        cmp_off = sb("cmp_off", [P, TILES, CPAD])
        cmp_ok = sb("cmp_ok", [P, TILES, CPAD])
        grows = sb("grows", [G_ROWS, P])
        gcol = sb("gcol", [P, G_ROWS])
        table = sb("table", [BUCKETS, SLOTS])
        neg_table = sb("neg_table", [SLOTS, BUCKETS])
        half = sb("half", [P, 1])
        sumsq = sb("sumsq", [P, n_rstd])
        meansq = sb("meansq", [P, n_rstd])
        rstd = sb("rstd", [P, n_rstd])
        low = sb("low", [P, len(ATT) * UNITS])
        total = sb("total", [P, len(ATT) * UNITS])
        share = sb("share", [P, len(ATT) * UNITS])
        cmp_low = sb("cmp_low", [P, TILES, HEADS])
        cmp_sum = sb("cmp_sum", [P, TILES, HEADS])
        neg_sinks = sb("neg_sinks", [P, HEADS])
        sinks = sb("sinks", [P, HEADS])
        sink_exp = sb("sink_exp", [P, UNITS])
        gate = sb("gate", [P, TILES, 3 * HEADS])
        rope = sb("rope", [P, TILES, ROPE])
        w2k = sb("w2k", [P, 2, 2, HEAD])
        w2v = sb("w2v", [P, 2, HEAD])
        hid = sb("hid", [P, 2, 2, 2 * NCMP])
        hid_rows = sb("hid_rows", [P, 2, 2, 4, CROW])
        kcmp = sb("kcmp", [P, 2, CPAD])
        rows_dram = nc.dram_tensor("bias_rows", [SLOTS, SEQ + P], F32, kind="Internal").ap()

        stage = xn
        bias_rows = h[0:SLOTS, :, :].rearrange("p t c -> p (t c)")[:, 0:SEQ + P]
        hankel = [val[:, :, :].rearrange("p t (h c) -> p (t h) c", h=2), qk[:, 0:4, :], qk[:, 4:8, :]]
        attn = raw_down[:, :].rearrange("p (t c) -> p t c", t=TILES)
        latent = val2[:, :, :, :].rearrange("p t a c -> p t (a c)")[:, :, 0:MLA_KV + ROPE]
        mla_qt = bias[:, HEADS:2 * HEADS, :]
        mla_kt = qk
        mla_q = xn[:, :, 0:HEADS * MLA_K].rearrange("p t (h c) -> p t h c", h=HEADS)
        mla_k = bias[:, 0:6, :].rearrange("p a b -> p (a b)").rearrange("p (t h c) -> p t h c", t=TILES, h=HEADS)
        zk = logit[:, :, :].rearrange("p a b -> p (a b)")[:, 0:480].rearrange("p (m g c) -> p m g c", m=16, g=2)
        zv = probt[:, :, :].rearrange("p a b -> p (a b)")[:, 0:480].rearrange("p (m g c) -> p m g c", m=16, g=2)
        vcmp = h[:, :, :].rearrange("p g (a d) -> p g a d", a=4)
        branch = h[:, :, :].rearrange("p t c -> p (t c)").rearrange("p (h d) -> p h d", h=HEADS)

        x_landed, small_landed, table_landed = sem("x_landed"), sem("small_landed"), sem("table_landed")
        main_landed = [sem("main_landed0"), sem("main_landed1")]
        down_landed = sem("down_landed")
        gpost_landed = sem("gpost_landed")
        rows_stored = sem("rows_stored")
        hankel_landed = sem("hankel_landed")
        main_hi, main_lo = sem("main_hi"), sem("main_lo")
        d_hi, d_lo, down_used = sem("d_hi"), sem("d_lo"), sem("down_used")
        const_step = sem("const_step")
        ss_ready, ms_ready, rstd_ready = sem("ss_ready"), sem("ms_ready"), sem("rstd_ready")
        w_out_ready = sem("w_out_ready")
        y_scaled, x_new, xn_ready = sem("y_scaled"), sem("x_new"), sem("xn_ready")
        t_ready, t_hi, t_done = sem("t_ready"), sem("t_hi"), sem("t_done")
        gu_ready, silu_done, h_ready = sem("gu_ready"), sem("silu_done"), sem("h_ready")
        ht_ready, ht_h, ht_l = sem("ht_ready"), sem("ht_h"), sem("ht_l")
        rows_step = sem("rows_step")
        flip_ready, flip_done = sem("flip_ready"), sem("flip_done")
        proj_ready, proj_out = sem("proj_ready"), sem("proj_out")
        rope_step, rope_done = sem("rope_step"), sem("rope_done")
        kr_done, q_rotated, lat_ready = sem("kr_done"), sem("q_rotated"), sem("lat_ready")
        scores_ready, logits_ready, probs_ready = sem("scores_ready"), sem("logits_ready"), sem("probs_ready")
        pt_ready, pt_copied = sem("pt_ready"), sem("pt_copied")
        pv_ready, head_out, share_step = sem("pv_ready"), sem("head_out"), sem("share_step")
        sink_added, sink_done = sem("sink_added"), sem("sink_done")
        z_hi, z_lo = sem("z_hi"), sem("z_lo")
        hid_ready, hid_done, hid_spread, hid_zero = sem("hid_ready"), sem("hid_done"), sem("hid_spread"), sem("hid_zero")
        cmp_kv_ready, cmp_kv_done = sem("cmp_kv_ready"), sem("cmp_kv_done")
        cmp_s_ready, cmp_step, cmp_e, cmp_p_ready = sem("cmp_s_ready"), sem("cmp_step"), sem("cmp_e"), sem("cmp_p_ready")
        neg_sinks_ready = sem("neg_sinks_ready")
        cmp_t_ready, cmp_t_done, cmp_o_ready, cmp_out = sem("cmp_t_ready"), sem("cmp_t_done"), sem("cmp_o_ready"), sem("cmp_out")
        gate_exp, gate_done = sem("gate_exp"), sem("gate_done")
        stored = sem("stored")
        block = ctx.enter_context(nc.Block())

        N_CONST = 11
        N_SMALL = len(STAGES) + 9
        N_ROWS = len(BUCKET_RANGES) + 2

        def main_view(buf, n, k, width):
            return buf[:, n % 2, k * 512:k * 512 + width]

        def wait_block_used(eng, n, g=lambda c, k: c):
            if n < 0:
                return
            s = next(s for s in reversed(STAGES) if first_block[s] <= n)
            m = n - first_block[s]
            if s in FFNS:
                eng.wait_ge(gu_ready, g(2 * (FFNS.index(s) * FBLOCKS + m + 1), 2))
            elif s == "l0_mix":
                if m <= len(MIX0_BLOCKS):
                    eng.wait_ge(proj_ready, 2 * (m + 1) + (2 if m == len(MIX0_BLOCKS) else 0))
                else:
                    eng.wait_ge(w_out_ready, m - len(MIX0_BLOCKS))
            elif m < len(MIX1_BLOCKS):
                eng.wait_ge(proj_ready, proj_base["w_in1"] + 2 * (m + 1))
            elif m < len(MIX1_BLOCKS) + 2:
                eng.wait_ge(hid_ready, m - len(MIX1_BLOCKS) + 1)
            else:
                eng.wait_ge(w_out_ready, 2 + m - len(MIX1_BLOCKS) - 1)

        def wait_y(eng, s_no):
            s = STAGES[s_no]
            if s in FFNS:
                eng.wait_ge(down_used, (FFNS.index(s) + 1) * FBLOCKS)
            else:
                eng.wait_ge(w_out_ready, 2 if s == "l0_mix" else 4)

        def pieces(n):
            m = n - first_block["l0_mix"]
            if m == len(MIX0_BLOCKS):
                return [lambda b: b[:, n % 2, 0:1536], lambda b: b[:, n % 2, 1536:2560]]
            width = 512
            if 0 <= m < len(MIX0_BLOCKS):
                width = MIX0_BLOCKS[m][1]
            m = n - first_block["l1_mix"]
            if 0 <= m < len(MIX1_BLOCKS):
                width = MIX1_BLOCKS[m][1]

            def part(half_no):
                lo, hi = half_no * MAIN // 2, (half_no + 1) * MAIN // 2
                return lambda b: b[:, n % 2, lo:hi].rearrange("p (k c) -> p k c", c=512)[:, :, 0:width]
            return [part(0), part(1)]

        def z_part(buf, i):
            flat = buf[:, :, :].rearrange("p k t -> p (k t)")
            return flat[:, 512 * i:512 * i + 480].rearrange("p (m g c) -> p m g c", m=16, g=2)

        def cmp_view(t, width=CPAD):
            return hid_rows[:, t, :, :, 0:width].rearrange("p g a c -> p (g a) c")

        def spread(ap, shape):
            return ap.unsqueeze(len(ap.shape)).to_broadcast(shape)

        def y_bank(t):
            return ps[:, 2 * t:2 * t + 2, :].rearrange("p a b -> p (a b)")

        def t_bank(job):
            return ps[:, 6 + job % 2, 0:SEQ]

        @block.sync
        def _(sp):
            def ffn_main(w, j, n):
                cols = bass.ds(j * FB, FB) if not isinstance(j, int) else slice(j * FB, (j + 1) * FB)
                dst = raw[:, n % 2, :].rearrange("p (k two c) -> p k two c", two=2, c=FB)
                for i, part in enumerate(("wg", "wu")):
                    src = a[f"{w}_{part}"].rearrange("(k p) n -> p k n", p=P)[:, :, cols]
                    sp.dma_start(dst[:, :, i, :], src).then_inc(main_landed[n % 2], 16)

            def ffn_down(w, j):
                rows = a[f"{w}_wd"].rearrange("(j c p) n -> j p c n", p=P, c=FC)
                src = rows[j] if isinstance(j, int) else rows[bass.ds(j, 1)].rearrange("o p c n -> (o p) c n")
                sp.dma_start(raw_down[:, :].rearrange("p (c n) -> p c n", c=FC), src).then_inc(down_landed, 16)

            def ring_wait(n):
                if n >= 2:
                    sp.wait_ge(main_lo, 2 * (n - 1))

            def down_wait(d):
                if d >= 1:
                    sp.wait_ge(d_lo, d)

            sp.dma_start(x[:, :, :], a["x"].rearrange("b (t p) d -> p (b t) d", p=P)).then_inc(x_landed, 16)
            late_down = None
            for s_no, s in enumerate(STAGES):
                n0 = first_block[s]
                if s in FFNS:
                    d0 = FFNS.index(s) * FBLOCKS
                    for j in range(PEEL):
                        ring_wait(n0 + j)
                        ffn_main(s, j, n0 + j)
                        if j == 0 and late_down:
                            late_down()
                        if j == 1 and s_no > 0 and STAGES[s_no - 1] not in FFNS:
                            sp.wait_ge(t_ready, job_base["out0" if s_no == 2 else "out1"] + 8)
                        if j >= 1:
                            down_wait(d0 + j - 1)
                            ffn_down(s, j - 1)
                    with sp.Fori(0, (FBLOCKS - PEEL) // 2) as i:
                        for q in range(2):
                            j = PEEL + q
                            sp.wait_ge(main_lo, 4 * i + 2 * (n0 + j - 1))
                            ffn_main(s, 2 * i + j, n0 + j)
                            sp.wait_ge(d_lo, 2 * i + d0 + j - 1)
                            ffn_down(s, 2 * i + (j - 1))

                    def late_down(s=s, d=d0 + FBLOCKS - 1):
                        down_wait(d)
                        ffn_down(s, FBLOCKS - 1)
                    if s == STAGES[-1]:
                        late_down()
                    continue
                if s == "l0_mix":
                    for b, (c0, width) in enumerate(MIX0_BLOCKS):
                        ring_wait(n0 + b)
                        dst = raw[:, (n0 + b) % 2, :].rearrange("p (k c) -> p k c", c=512)[:, :, 0:width]
                        sp.dma_start(dst, a["l0_w_in"].rearrange("(k p) n -> p k n", p=P)[:, :, c0:c0 + width])\
                          .then_inc(main_landed[(n0 + b) % 2], 16)
                        if b == 0:
                            late_down()
                            late_down = None
                    n = n0 + len(MIX0_BLOCKS)
                    ring_wait(n)
                    sp.dma_start(raw[:, n % 2, 0:1536].rearrange("p (k c) -> p k c", k=2),
                                 a["l0_mla_w_uq"].rearrange("(k p) n -> p k n", p=P)).then_inc(main_landed[n % 2], 16)
                    sp.dma_start(raw[:, n % 2, 1536:2560], a["l0_mla_w_ukv"]).then_inc(main_landed[n % 2], 16)
                    n += 1
                else:
                    for b, (c0, width) in enumerate(MIX1_BLOCKS):
                        ring_wait(n0 + b)
                        dst = raw[:, (n0 + b) % 2, :].rearrange("p (k c) -> p k c", c=512)[:, :, 0:width]
                        sp.dma_start(dst, a["l1_w_in"].rearrange("(k p) n -> p k n", p=P)[:, :, c0:c0 + width])\
                          .then_inc(main_landed[(n0 + b) % 2], 16)
                        if b == 0:
                            late_down()
                            late_down = None
                    n = n0 + len(MIX1_BLOCKS)
                    for w in ("l1_nsa_wk1", "l1_nsa_wv1"):
                        ring_wait(n)
                        sp.dma_start(raw[:, n % 2, :].rearrange("p (m c) -> p m c", c=CMP_HID),
                                     a[w].rearrange("(m p) n -> p m n", p=P)).then_inc(main_landed[n % 2], 16)
                        n += 1
                w_out = a["l0_w_out" if s == "l0_mix" else "l1_w_out"].rearrange("(k p) n -> p k n", p=P)
                for half_no in range(2):
                    ring_wait(n)
                    sp.dma_start(raw[:, n % 2, :].rearrange("p (k c) -> p k c", c=512),
                                 w_out[:, :, half_no * 512:(half_no + 1) * 512]).then_inc(main_landed[n % 2], 16)
                    n += 1
            for t in range(TILES):
                sp.wait_ge(x_new, 2 * len(STAGES) - 1 + t)
                sp.dma_start(out[0, t * P:(t + 1) * P, :], x[:, t, :]).then_inc(stored, 16)
            sp.wait_ge(stored, 16 * TILES)

        @block.gpsimd
        def _(pool):
            steps = [0]

            def step(ins):
                steps[0] += 1
                ins.then_inc(const_step, 1)
                pool.wait_ge(const_step, steps[0])

            for m in (ident, flip, causal):
                step(pool.memset(m[:, :], 0.0))
            step(pool.memset(cmp_off[:, :, :], 0.0))
            step(pool.memset(cmp_ok[:, :, :], 1.0))
            step(pool.memset(half[:, :], -0.5))
            step(pool.affine_select(out=ident[:, :], in_=ident[:, :], compare_op=ALU.not_equal, fill=1.0,
                                    base=0, pattern=[[-1, P]], channel_multiplier=1))
            step(pool.affine_select(out=flip[:, :], in_=flip[:, :], compare_op=ALU.not_equal, fill=1.0,
                                    base=1 - P, pattern=[[1, P]], channel_multiplier=1))
            step(pool.affine_select(out=causal[:, P:SEQ], in_=causal[:, P:SEQ], compare_op=ALU.is_ge, fill=BIG,
                                    base=0, pattern=[[-1, P]], channel_multiplier=1))
            for m, fill in ((cmp_off, BIG), (cmp_ok, 0.0)):
                step(pool.affine_select(out=m[:, :, :], in_=m[:, :, :], compare_op=ALU.is_ge, fill=fill,
                                        base=1 - CMP_BLOCK, pattern=[[P, TILES], [-CMP_STRIDE, CPAD]],
                                        channel_multiplier=1))
            pool.memset(hid_rows[:, :, :, :, :], 0.0).then_inc(hid_zero, 1)
            pool.memset(kcmp[:, :, :], 0.0).then_inc(hid_zero, 1)
            lat = rstd_base["lat"]
            for r in range(n_rstd):
                size = D if not lat <= r < lat + 4 else (MLA_Q if r < lat + 2 else MLA_KV)
                pool.wait_ge(ss_ready, r + 1)
                pool.tensor_scalar(meansq[:, r:r + 1], sumsq[:, r:r + 1], 1.0 / size, EPS, ALU.mult, ALU.add)\
                    .then_inc(ms_ready, 1)
                pool.wait_ge(ms_ready, r + 1)
                pool.tensor_tensor(rstd[:, r:r + 1], meansq[:, r:r + 1], half[:, :], ALU.pow).then_inc(rstd_ready, 1)

        @block.scalar
        def _(act):
            act.dma_start(table[:, :], a["rel_bias_table"]).then_inc(table_landed, 16)
            loads = []
            for s_no, s in enumerate(STAGES):
                loads.append((grows[8 * s_no:8 * s_no + 8, :], a[f"{s}_pre"].rearrange("(c p) -> c p", p=P)))
            loads += [(grows[G_Q:G_Q + 2, :], a["l0_mla_q_norm"].rearrange("(c p) -> c p", p=P)),
                      (grows[G_KV:G_KV + 1, :], a["l0_mla_kv_norm"].rearrange("(c p) -> c p", p=P)),
                      (grows[G_PEK:G_PEK + 16, :], a["l1_nsa_pe_k"].rearrange("(m a) d -> m (a d)", a=2)),
                      (grows[G_PEV:G_PEV + 16, :], a["l1_nsa_pe_v"].rearrange("(m a) d -> m (a d)", a=2)),
                      (w2v[:, :, :], a["l1_nsa_wv2"].rearrange("(k p) d -> p k d", p=P)),
                      (w2k[:, :, 0, :], a["l1_nsa_wk2"].rearrange("(k p) d -> p k d", p=P)),
                      (w2k[:, :, 1, :], a["l1_nsa_wk2"].rearrange("(k p) d -> p k d", p=P)),
                      (rope[:, :, :], a["rope_tables"].rearrange("(t p) c -> p t c", p=P)),
                      (sinks[:, :], bass.AP(tensor=a["l0_sinks"].tensor, offset=0, ap=[[0, P], [1, HEADS]]))]
            assert len(loads) == N_SMALL
            for dst, src in loads:
                act.dma_start(dst, src).then_inc(small_landed, 16)

            def load_hankel(quartet, slot):
                src = bass.AP(tensor=rows_dram.tensor, offset=quartet * 4 * (SEQ + P),
                              ap=[[1, P], [SEQ + P, 4], [1, SEQ]])
                act.dma_start(hankel[slot], src).then_inc(hankel_landed, 16)

            def copy_bias(f0, count):
                for f in range(f0, f0 + count):
                    pair = f if f < 4 else f - 4
                    act.wait_ge(flip_ready, f + 1)
                    act.activation(bias[:, 2 * pair:2 * pair + 2, :],
                                   ps[:, 4 + f % 2, :].rearrange("p (h c) -> p h c", h=2), ACT.Copy).then_inc(flip_done, 1)

            def load_gpost(s):
                act.dma_start(gpost[:, :], bass.AP(tensor=a[f"{s}_post"].tensor, offset=0, ap=[[0, P], [1, D]]))\
                   .then_inc(gpost_landed, 16)

            def split_main(n, g=lambda c, k: c):
                act.wait_ge(main_landed[n % 2], g(landed_value(n), 32))
                wait_block_used(act, n - 2, g)
                for part in pieces(n):
                    act.activation(part(w_hi), part(raw), ACT.Copy).then_inc(main_hi, 1)

            def squares(src, width, r):
                act.activation(xn[:, r % 2, 0:width], src, ACT.Square, accum_out=sumsq[:, r:r + 1]).then_inc(ss_ready, 1)

            def turned_hi(name, dst, gain=None, banks=8):
                for k in range(banks):
                    job = job_base[name] + k
                    act.wait_ge(t_ready, job + 1)
                    kw = {} if gain is None else {"scale": gcol[:, gain + k:gain + k + 1]}
                    act.activation(dst[:, k, :], t_bank(job), ACT.Copy, **kw).then_inc(t_hi, 1)

            def pre_norm(s_no):
                for t in range(TILES):
                    if s_no == 0:
                        act.wait_ge(x_landed, 16)
                    else:
                        act.wait_ge(x_new, 2 * (s_no - 1) + t + 1)
                    squares(x[:, t, :], D, rstd_base[f"pre{s_no}"] + t)
                load_gpost(STAGES[s_no])
                if s_no == 0:
                    act.wait_ge(t_done, 1)
                turned_hi(f"norm{s_no}", xt_hi, gain=8 * s_no)

            def post_squares(s_no):
                wait_y(act, s_no)
                for t in range(TILES):
                    squares(y_bank(t), D, rstd_base[f"post{s_no}"] + t)

            def ffn(u, s_no):
                n0, d0 = first_block[STAGES[s_no]], u * FBLOCKS

                def silu(jc, t, g):
                    act.wait_ge(gu_ready, g(2 * (d0 + jc) + t + 1, 2))
                    if d0 + jc >= 1:
                        act.wait_ge(ht_ready, g(d0 + jc, 1))
                    act.activation(h[:, t, :], ps[:, 4 + t, 0:FB], ACT.Silu).then_inc(silu_done, 1)

                def behind(jc, g):
                    act.wait_ge(ht_ready, g(d0 + jc + 1, 1))
                    if d0 + jc >= 1:
                        act.wait_ge(down_used, g(d0 + jc, 1))
                    act.activation(ht_hi[:, :, :], ps[:, 6, :].rearrange("p (c t) -> p c t", c=FC), ACT.Copy)\
                       .then_inc(ht_h, 1)
                    act.wait_ge(down_landed, g(16 * (d0 + jc + 1), 16))
                    act.activation(down_hi[:, :], raw_down[:, :], ACT.Copy).then_inc(d_hi, 1)

                def step(jc, g, ahead):
                    if jc >= 1:
                        behind(jc - 1, g)
                    silu(jc, 0, g)
                    if ahead:
                        split_main(n0 + jc + 1, g)
                    silu(jc, 1, g)

                def fixed(c, k):
                    return c
                step(0, fixed, True)
                step(1, fixed, True)
                with act.Fori(0, (FBLOCKS - PEEL) // 2) as i:
                    for q in range(2):
                        step(2 + q, lambda c, k, i=i: c + (2 * k if k != 32 else 32) * i, True)
                step(FBLOCKS - 1, fixed, n0 + FBLOCKS < total_blocks)
                behind(FBLOCKS - 1, fixed)

            def project_out(j0, copies):
                for t in range(TILES):
                    act.wait_ge(proj_ready, j0 + t + 1)
                    for dst, src, scale in copies(t):
                        act.activation(dst, src, ACT.Copy, scale=scale).then_inc(proj_out, 1)

            def exps(name):
                base = UNITS * ATT[name]
                for n in range(UNITS):
                    t = n // HEADS
                    keys = P * (t + 1)
                    act.wait_ge(logits_ready, base + n + 1)
                    act.activation(logit[:, n % 3, 0:keys], logit[:, n % 3, 0:keys], ACT.Exp,
                                   bias=low[:, base + n:base + n + 1], scale=-1.0,
                                   accum_out=total[:, base + n:base + n + 1]).then_inc(probs_ready, 1)
                    if name == "swa" and n % HEADS == HEADS - 1:
                        act.wait_ge(sink_added, t + 1)
                        cols = slice(HEADS * t, HEADS * (t + 1))
                        act.activation(sink_exp[:, cols], sink_exp[:, cols], ACT.Exp).then_inc(sink_done, 1)

            split_main(0)
            act.wait_ge(rows_step, N_ROWS)
            act.dma_start(rows_dram, bias_rows).then_inc(rows_stored, 16)
            pre_norm(0)
            act.wait_ge(rows_stored, 16)
            for k in range(2):
                load_hankel(k, k)
            ffn(0, 0)
            post_squares(0)

            n0 = first_block["l0_mix"]
            pre_norm(1)
            copy_bias(0, 2)
            j0 = proj_base["w_in0"]
            scale_a = -HEAD ** -0.5
            split_main(n0 + 1)
            project_out(j0, lambda t: [(stage[:, t, 0:512], ps[:, t, :], scale_a)])
            copy_bias(2, 2)
            split_main(n0 + 2)
            project_out(j0 + 2, lambda t: [(stage[:, t, 512:1024], ps[:, 2 + t, :], 1.0)])
            split_main(n0 + 3)
            project_out(j0 + 4, lambda t: [(latent[:, t, :], ps[:, t, 0:160], 1.0)])
            split_main(n0 + 4)
            lat = rstd_base["lat"]
            for r, (src, width, need) in enumerate(
                    [(stage[:, 0, 768:1024], MLA_Q, 4), (stage[:, 1, 768:1024], MLA_Q, 4),
                     (latent[:, 0, 0:MLA_KV], MLA_KV, 6), (latent[:, 1, 0:MLA_KV], MLA_KV, 6)]):
                act.wait_ge(proj_out, need)
                act.activation(h[:, r % 2, 0:width], src, ACT.Square, accum_out=sumsq[:, lat + r:lat + r + 1])\
                   .then_inc(ss_ready, 1)
                act.wait_ge(ss_ready, lat + r + 1)
            for k in range(3):
                job = job_base["lat"] + k
                act.wait_ge(t_ready, job + 1)
                act.activation(xt_hi[:, k, :], t_bank(job), ACT.Copy, scale=gcol[:, G_Q + k:G_Q + k + 1])\
                   .then_inc(t_hi, 1)
            exps("swa")
            j0 = proj_base["up"]
            scale_b = -MLA_K ** -0.5
            act.wait_ge(pv_ready, UNITS * (ATT["swa"] + 1))
            for t in range(TILES):
                act.wait_ge(proj_ready, j0 + t + 1)
                for b in range(2):
                    act.activation(mla_q[:, t, 4 * b:4 * b + 4, :],
                                   ps[:, 2 * t + b, 0:384].rearrange("p (h c) -> p h c", h=4), ACT.Copy,
                                   scale=scale_b).then_inc(proj_out, 1)
            for t in range(TILES):
                act.wait_ge(proj_ready, j0 + 2 + t + 1)
                act.wait_ge(logits_ready, UNITS * (ATT["swa"] + 1))
                for b in range(2):
                    kv = ps[:, 2 * t + b, :].rearrange("p (h c) -> p h c", h=4)
                    act.activation(mla_k[:, t, 4 * b:4 * b + 4, 0:NOPE], kv[:, :, 0:NOPE], ACT.Copy).then_inc(proj_out, 1)
                    act.activation(val[:, t, 256 * b:256 * b + 256].rearrange("p (h c) -> p h c", h=4),
                                   kv[:, :, NOPE:2 * NOPE], ACT.Copy).then_inc(proj_out, 1)
            split_main(n0 + 5)
            exps("mla")
            turned_hi("out0", xt_hi)
            split_main(n0 + 6)
            post_squares(1)
            for k in range(3):
                load_hankel(2 + k, k)

            pre_norm(2)
            ffn(1, 2)
            post_squares(2)
            pre_norm(3)
            ffn(2, 3)
            post_squares(3)

            n0 = first_block["l1_mix"]
            pre_norm(4)
            copy_bias(4, 2)
            load_hankel(5, 0)
            j0 = proj_base["w_in1"]
            split_main(n0 + 1)
            project_out(j0, lambda t: [(stage[:, t, 0:512], ps[:, t, :], scale_a)])
            copy_bias(6, 4)
            split_main(n0 + 2)
            project_out(j0 + 2, lambda t: [(stage[:, t, 512:896], ps[:, 2 + t, 0:384], 1.0),
                                           (val2[:, t, 0, :], ps[:, 2 + t, 384:512], 1.0)])
            copy_bias(10, 2)
            split_main(n0 + 3)
            act.wait_ge(t_ready, job_base["qc"] + 4)
            project_out(j0 + 4, lambda t: [(stage[:, t, 0:P], ps[:, t, 0:P], 1.0),
                                           (val2[:, t, 1, :], ps[:, t, P:2 * P], 1.0),
                                           (gate[:, t, :], ps[:, t, 2 * P:2 * P + 24], -1.0)])
            for t in range(TILES):
                act.wait_ge(proj_out, OUT["w_in1"][2])
                act.activation(gate[:, t, :], gate[:, t, :], ACT.Exp).then_inc(gate_exp, 1)
            split_main(n0 + 4)
            act.wait_ge(t_ready, job_base["kw"] + 1)
            project_out(j0 + 6, lambda t: [(stage[:, t, 0:512], ps[:, 2 + t, :], scale_a)])
            split_main(n0 + 5)
            project_out(j0 + 8, lambda t: [(stage[:, t, 512:1024], ps[:, t, :], 1.0)])
            split_main(n0 + 6)
            project_out(j0 + 10, lambda t: [(val[:, t, :], ps[:, 2 + t, :], 1.0)])
            split_main(n0 + 7)
            for i, z in enumerate((zk, zv)):
                act.wait_ge(t_done, job_base["kvc"] + i + 1)
                act.wait_ge(proj_ready, j0 + 12)
                act.activation(z_part(xt_hi, i), z, ACT.Copy).then_inc(z_hi, 1)
            for i in range(2):
                act.wait_ge(hid_ready, i + 1)
                act.activation(hid[:, i, :, :], ps[:, i, 0:4 * NCMP].rearrange("p (k r) -> p k r", k=2), ACT.Silu)\
                   .then_inc(hid_done, 1)
            split_main(n0 + 8)
            split_main(n0 + 9)
            for t in range(TILES):
                act.wait_ge(cmp_step, 4 * t + 4)
                act.activation(cmp_view(t), cmp_view(t), ACT.Exp, scale=-1.0).then_inc(cmp_e, 1)
            exps("slc")
            exps("win")
            exps("moba")
            turned_hi("out1", xt_hi)
            split_main(n0 + 10)
            post_squares(4)
            pre_norm(5)
            ffn(3, 5)
            post_squares(5)

        @block.tensor
        def _(pe):
            def mm(dst, lhs, rhs, start, stop):
                return pe.matmul(dst, lhs, rhs, start=start, stop=stop, skip_group_check=True)

            def three(dst, lhs_hi, lhs_lo, rhs_hi, rhs_lo, start, stop):
                mm(dst, lhs_hi, rhs_hi, start, False)
                mm(dst, lhs_hi, rhs_lo, False, False)
                return mm(dst, lhs_lo, rhs_hi, False, stop)

            def turn(job, parts):
                if job >= 2:
                    pe.wait_ge(t_done, job - 1)
                for dst, src in parts:
                    ins = pe.transpose(dst, src, ident[0:src.shape[0], 0:src.shape[0]])
                ins.then_inc(t_ready, 1)

            def turn_pairs(name, source, count):
                for k in range(count):
                    bank = t_bank(job_base[name] + k)
                    turn(job_base[name] + k, [(bank[:, t * P:(t + 1) * P], source(t, k)) for t in range(TILES)])

            def norm(s_no):
                pe.wait_ge(xn_ready, 2 * (s_no + 1))
                turn_pairs(f"norm{s_no}", lambda t, k: xn[:, t, k * P:(k + 1) * P], KD)

            def product(n, t, width, bank, c0=0, cw=None, lo=None):
                for k in range(KD):
                    if k % (KD // 2) == 0:
                        half_no = k // (KD // 2)
                        pe.wait_ge(main_lo, (2 * n + 1 if lo is None else lo) + half_no)
                    ins = three(ps[:, bank, 0:width], xt_hi[:, k, t * P:(t + 1) * P], xt_lo[:, k, t * P:(t + 1) * P],
                                main_view(w_hi, n, k, width), main_view(w_lo, n, k, width), k == 0, k == KD - 1)
                return ins

            def ffn(u, s_no):
                n0, d0 = first_block[STAGES[s_no]], u * FBLOCKS
                pe.wait_ge(t_done, job_base[f"norm{s_no}"] + KD)

                def gate_up(jc, g):
                    n = n0 + jc
                    for t in range(TILES):
                        if d0 + jc >= 1:
                            pe.wait_ge(h_ready, g(2 * (d0 + jc - 1) + t + 1, 2))
                        product(n, t, 512, 4 + t, lo=g(2 * n + 1, 2)).then_inc(gu_ready, 1)

                def turn_h(jc, g):
                    pe.wait_ge(h_ready, g(2 * (d0 + jc) + 2, 2))
                    if d0 + jc >= 1:
                        pe.wait_ge(ht_l, g(d0 + jc, 1))
                    for c in range(FC):
                        for t in range(TILES):
                            at = c * SEQ + t * P
                            ins = pe.transpose(ps[:, 6, at:at + P], h[:, t, c * P:(c + 1) * P], ident[:, :])
                    ins.then_inc(ht_ready, 1)

                def down(jc, g):
                    pe.wait_ge(ht_l, g(d0 + jc + 1, 1))
                    pe.wait_ge(d_lo, g(d0 + jc + 1, 1))
                    for t in range(TILES):
                        for c in range(FC):
                            for part in range(2):
                                cols = slice(c * D + part * 512, c * D + part * 512 + 512)
                                ins = three(ps[:, 2 * t + part, :], ht_hi[:, c, t * P:(t + 1) * P],
                                            ht_lo[:, c, t * P:(t + 1) * P], down_hi[:, cols], down_lo[:, cols],
                                            jc == 0 and c == 0, jc == FBLOCKS - 1 and c == FC - 1)
                    ins.then_inc(down_used, 1)

                def fixed(c, k):
                    return c
                for jc in range(PEEL):
                    gate_up(jc, fixed)
                    if jc >= 1:
                        down(jc - 1, fixed)
                    turn_h(jc, fixed)
                with pe.Fori(0, (FBLOCKS - PEEL) // 2) as i:
                    for q in range(2):
                        def looped(c, k, i=i):
                            return c + 2 * k * i
                        gate_up(PEEL + q, looped)
                        down(PEEL + q - 1, looped)
                        turn_h(PEEL + q, looped)
                down(FBLOCKS - 1, fixed)

            def flips(f0, count):
                for f in range(f0, f0 + count):
                    quartet = f // 2 if f < 4 else (f - 4) // 2
                    slot = quartet if quartet < 3 else 0
                    pe.wait_ge(hankel_landed, 16 * (2 if f < 4 else (5 if quartet < 3 else 6)))
                    if f >= 2:
                        pe.wait_ge(flip_done, f - 1)
                    mm(ps[:, 4 + f % 2, :], flip[:, :], hankel[slot][:, 2 * (f % 2):2 * (f % 2) + 2, :].rearrange("p h c -> p (h c)"), True, True)\
                        .then_inc(flip_ready, 1)

            def project(n, job, width, bank):
                for t in range(TILES):
                    ins = product(n, t, width, bank + t)
                    ins.then_inc(proj_ready, 1)

            def attention(name, q_of, k_of, v_of):
                base = UNITS * ATT[name]

                def scores(n):
                    t, hh = n // HEADS, n % HEADS
                    if base + n >= 3:
                        pe.wait_ge(logits_ready, base + n - 2)
                    mm(ps[:, n % 3, 0:P * (t + 1)], q_of(hh)[:, t * P:(t + 1) * P], k_of(hh)[:, 0:P * (t + 1)], True, True)\
                        .then_inc(scores_ready, 1)

                def turn_probs(n):
                    t = n // HEADS
                    pe.wait_ge(probs_ready, base + n + 1)
                    if base + n >= 3:
                        pe.wait_ge(pt_copied, base + n - 2)
                    for kt in range(t + 1):
                        ins = pe.transpose(ps[:, 3 + n % 3, kt * P:(kt + 1) * P], logit[:, n % 3, kt * P:(kt + 1) * P],
                                           ident[:, :])
                    ins.then_inc(pt_ready, 1)

                def values(n):
                    t, hh = n // HEADS, n % HEADS
                    pe.wait_ge(pt_copied, base + n + 1)
                    if hh == 0 and OUT_BEFORE[name] > 0:
                        pe.wait_ge(head_out, OUT_BEFORE[name])
                    for kt in range(t + 1):
                        ins = mm(ps[:, 6 + t, hh * HEAD:(hh + 1) * HEAD], probt[:, n % 3, kt * P:(kt + 1) * P],
                                 v_of(kt, hh), kt == 0, kt == t)
                    ins.then_inc(pv_ready, 1)

                for n in range(UNITS + 3):
                    if n < UNITS:
                        scores(n)
                    if 2 <= n < UNITS + 2:
                        turn_probs(n - 2)
                    if n >= 3:
                        values(n - 3)

            def w_out(s_no, n):
                for part in range(2):
                    for t in range(TILES):
                        ins = product(n + part, t, 512, 2 * t + part)
                    ins.then_inc(w_out_ready, 1)

            pe.wait_ge(const_step, N_CONST)
            pe.wait_ge(small_landed, 16 * N_SMALL)
            pe.wait_ge(table_landed, 16)
            turn(0, [(ps[:, 6, 0:G_ROWS], grows[:, :])])
            turn(1, [(ps[0:SLOTS, 7, 0:BUCKETS], table[:, :])])
            norm(0)
            ffn(0, 0)

            n0 = first_block["l0_mix"]
            flips(0, 2)
            norm(1)
            pe.wait_ge(t_done, job_base["norm1"] + KD)
            project(n0, 0, 512, 0)
            flips(2, 2)
            project(n0 + 1, 2, 512, 2)
            pe.wait_ge(proj_out, OUT["w_in0"][0])
            project(n0 + 2, 4, 160, 0)
            turn_pairs("qa", lambda t, k: stage[:, t, k * P:(k + 1) * P], 4)
            pe.wait_ge(proj_out, OUT["w_in0"][1])
            turn_pairs("ka", lambda t, k: stage[:, t, 512:512 + P], 1)
            pe.wait_ge(lat_ready, 4)
            turn_pairs("lat", lambda t, k: stage[:, t, 768 + k * P:768 + (k + 1) * P] if k < 2 else latent[:, t, 0:P], 3)
            pe.wait_ge(t_done, job_base["lat"] + 3)
            pe.wait_ge(flip_done, 4)
            attention("swa", lambda hh: qk[64 * (hh % 2):64 * (hh % 2) + 64, hh // 2, :],
                      lambda hh: qk[64 * (hh % 2):64 * (hh % 2) + 64, 4 + hh // 4, :],
                      lambda kt, hh: stage[:, kt, 640 + HEAD * (hh // 4):640 + HEAD * (hh // 4) + HEAD])
            n = n0 + len(MIX0_BLOCKS)
            pe.wait_ge(main_lo, 2 * n + 2)
            pe.wait_ge(pt_copied, UNITS)
            pe.wait_ge(logits_ready, UNITS)
            for t in range(TILES):
                for b in range(2):
                    for k in range(2):
                        cols = slice(k * 768 + b * 384, k * 768 + b * 384 + 384)
                        ins = three(ps[:, 2 * t + b, 0:384], xt_hi[:, k, t * P:(t + 1) * P], xt_lo[:, k, t * P:(t + 1) * P],
                                    w_hi[:, n % 2, cols], w_lo[:, n % 2, cols], k == 0, k == 1)
                ins.then_inc(proj_ready, 1)
            for t in range(TILES):
                if t == 0:
                    pe.wait_ge(proj_out, OUT["up"][0])
                for b in range(2):
                    cols = slice(1536 + b * 512, 1536 + b * 512 + 512)
                    ins = three(ps[:, 2 * t + b, :], xt_hi[:, 2, t * P:(t + 1) * P], xt_lo[:, 2, t * P:(t + 1) * P],
                                w_hi[:, n % 2, cols], w_lo[:, n % 2, cols], True, True)
                ins.then_inc(proj_ready, 1)
            pe.wait_ge(proj_out, OUT["up"][1])
            pe.wait_ge(rope_done, 2)
            for i, src in enumerate((mla_q, mla_k)):
                for hh in range(HEADS):
                    job = job_base["mla"] + HEADS * i + hh
                    if i == 0 and hh == 0:
                        pe.wait_ge(head_out, OUT_BEFORE["mla"])
                    turn(job, [(t_bank(job)[0:MLA_K, t * P:(t + 1) * P], src[:, t, hh, :]) for t in range(TILES)])
            pe.wait_ge(t_done, job_base["mla"] + 16)
            attention("mla", lambda hh: mla_qt[0:MLA_K, hh, :], lambda hh: mla_kt[0:MLA_K, hh, :],
                      lambda kt, hh: val[:, kt, hh * HEAD:(hh + 1) * HEAD])
            pe.wait_ge(head_out, OUT_BEFORE["slc0"])
            turn_pairs("out0", lambda t, k: attn[:, t, k * P:(k + 1) * P], KD)
            pe.wait_ge(t_done, job_base["out0"] + KD)
            w_out(1, n0 + 4)

            norm(2)
            ffn(1, 2)
            norm(3)
            ffn(2, 3)

            n0 = first_block["l1_mix"]
            j0 = proj_base["w_in1"]
            flips(4, 2)
            norm(4)
            pe.wait_ge(t_done, job_base["norm4"] + KD)
            project(n0, j0 + 0, 512, 0)
            flips(6, 4)
            project(n0 + 1, j0 + 2, 512, 2)
            flips(10, 2)
            pe.wait_ge(proj_out, OUT["w_in1"][0])
            turn_pairs("qc", lambda t, k: stage[:, t, k * P:(k + 1) * P], 4)
            project(n0 + 2, j0 + 4, 280, 0)
            pe.wait_ge(proj_out, OUT["w_in1"][1])
            turn_pairs("kvc", lambda t, k: stage[:, t, 512 + k * P:512 + (k + 1) * P], 2)
            turn_pairs("ks", lambda t, k: stage[:, t, 768:768 + P], 1)
            project(n0 + 3, j0 + 6, 512, 2)
            pe.wait_ge(proj_out, OUT["w_in1"][2])
            turn_pairs("kw", lambda t, k: stage[:, t, 0:P], 1)
            project(n0 + 4, j0 + 8, 512, 0)
            pe.wait_ge(proj_out, OUT["w_in1"][3])
            project(n0 + 5, j0 + 10, 512, 2)
            pe.wait_ge(proj_out, OUT["w_in1"][4])
            for i in range(2):
                n = n0 + 6 + i
                pe.wait_ge(z_lo, i + 1)
                pe.wait_ge(main_lo, 2 * n + 2)
                for c in range(2):
                    for m in range(16):
                        cols = slice(m * CMP_HID + c * P, m * CMP_HID + (c + 1) * P)
                        zh = z_part(xt_hi, i)[:, m, :, :].rearrange("p g c -> p (g c)")
                        zl = z_part(xt_lo, i)[:, m, :, :].rearrange("p g c -> p (g c)")
                        ins = three(ps[:, i, c * 2 * NCMP:(c + 1) * 2 * NCMP], w_hi[:, n % 2, cols], w_lo[:, n % 2, cols],
                                    zh, zl, m == 0, m == 15)
                ins.then_inc(hid_ready, 1)
            pe.wait_ge(proj_out, OUT["w_in1"][5])
            pe.wait_ge(hid_done, 1)
            for c in range(2):
                ins = mm(ps[:, 2, 0:2 * NCMP], w2k[:, c, :, :].rearrange("p a d -> p (a d)"), hid[:, 0, c, :], c == 0, c == 1)
            ins.then_inc(cmp_kv_ready, 1)
            pe.wait_ge(hid_spread, 4)
            for g in range(2):
                for c in range(2):
                    ins = mm(ps[:, 3, g * HEAD:(g + 1) * HEAD], hid_rows[:, c, g, :, :].rearrange("p a c -> p (a c)"),
                             w2v[:, c, :], c == 0, c == 1)
            ins.then_inc(cmp_kv_ready, 1)
            pe.wait_ge(cmp_kv_done, 5)
            pe.wait_ge(flip_done, 12)
            for t in range(TILES):
                for hh in range(HEADS):
                    rows = slice(64 * (hh % 2), 64 * (hh % 2) + 64)
                    at = hh // 2 * CPAD
                    ins = mm(ps[:, t + 2 * (hh % 2), at:at + CPAD], qk[rows, hh // 2, t * P:(t + 1) * P],
                             kcmp[rows, hh // 4, :], True, True)
                ins.then_inc(cmp_s_ready, 1)
            for t in range(TILES):
                pe.wait_ge(cmp_p_ready, t + 1)
                for g in range(2):
                    ins = pe.transpose(ps[:, 2 + t, g * P:(g + 1) * P],
                                       hid_rows[:, t, g, :, :].rearrange("p a c -> p (a c)"), ident[:, :])
                ins.then_inc(cmp_t_ready, 1)
            for t in range(TILES):
                pe.wait_ge(cmp_t_done, t + 1)
                if t == 0:
                    pe.wait_ge(t_done, job_base["kw"] + 1)
                for g in range(2):
                    ins = mm(ps[:, 6 + t, g * 256:(g + 1) * 256], probt[:, t, g * P:(g + 1) * P],
                             vcmp[:, g, :, :].rearrange("p a d -> p (a d)"), True, True)
                ins.then_inc(cmp_o_ready, 1)

            def q_pair(hh):
                return qk[64 * (hh % 2):64 * (hh % 2) + 64, hh // 2, :]

            attention("slc", q_pair, lambda hh: qk[64 * (hh % 2):64 * (hh % 2) + 64, 4 + hh // 4, :],
                      lambda kt, hh: val2[:, kt, 0, HEAD * (hh // 4):HEAD * (hh // 4) + HEAD])
            attention("win", q_pair, lambda hh: qk[64 * (hh % 2):64 * (hh % 2) + 64, 6 + hh // 4, :],
                      lambda kt, hh: val2[:, kt, 1, HEAD * (hh // 4):HEAD * (hh // 4) + HEAD])
            pe.wait_ge(head_out, OUT_BEFORE["moba"])
            turn_pairs("qd", lambda t, k: stage[:, t, k * P:(k + 1) * P], 4)
            turn_pairs("kd", lambda t, k: stage[:, t, 512 + k * P:512 + (k + 1) * P], 4)
            pe.wait_ge(t_done, job_base["kd"] + 4)
            attention("moba", q_pair, lambda hh: qk[64 * (hh % 2):64 * (hh % 2) + 64, 4 + hh // 2, :],
                      lambda kt, hh: val[:, kt, hh * HEAD:(hh + 1) * HEAD])
            pe.wait_ge(head_out, OUT_BEFORE["end"])
            turn_pairs("out1", lambda t, k: attn[:, t, k * P:(k + 1) * P], KD)
            pe.wait_ge(t_done, job_base["out1"] + KD)
            w_out(4, n0 + 8)

            norm(5)
            ffn(3, 5)

        @block.vector
        def _(dve):
            outs = [0]
            shares = [0]

            def split_main(n, hi=None):
                for i, part in enumerate(pieces(n)):
                    dve.wait_ge(main_hi, (2 * n + 1 if hi is None else hi) + i)
                    dve.tensor_tensor(part(w_lo), part(raw), part(w_hi).bitcast(F32), ALU.subtract).then_inc(main_lo, 1)

            def turned(name, count, dst, gain=None):
                for k in range(count):
                    job = job_base[name] + k
                    dve.wait_ge(t_hi, hi_base[name] + k + 1)
                    bank = t_bank(job)
                    if gain is None:
                        ins = dve.tensor_tensor(dst[0][:, k, :], bank, dst[1][:, k, :].bitcast(F32), ALU.subtract)
                    else:
                        ins = dve.scalar_tensor_tensor(dst[0][:, k, :], bank, gcol[:, gain + k:gain + k + 1],
                                                       dst[1][:, k, :].bitcast(F32), ALU.mult, ALU.subtract)
                    ins.then_inc(t_done, 1)

            def turned_plain(name, count, dst):
                for k in range(count):
                    job = job_base[name] + k
                    dve.wait_ge(t_ready, job + 1)
                    dve.tensor_copy(dst(k), t_bank(job)).then_inc(t_done, 1)

            def turned_kv_heads(name, slot):
                job = job_base[name]
                dve.wait_ge(t_ready, job + 1)
                for g in range(2):
                    for par in range(2):
                        ins = dve.tensor_copy(qk[64 * par:64 * par + 64, slot + g, :], t_bank(job)[64 * g:64 * g + 64, :])
                ins.then_inc(t_done, 1)

            def pre_norm(s_no):
                r = rstd_base[f"pre{s_no}"]
                for t in range(TILES):
                    dve.wait_ge(rstd_ready, r + t + 1)
                    dve.tensor_scalar(xn[:, t, :], x[:, t, :], rstd[:, r + t:r + t + 1], None, ALU.mult).then_inc(xn_ready, 1)
                turned(f"norm{s_no}", KD, (xt_lo, xt_hi), gain=8 * s_no)

            def post_norm(s_no):
                weight = 0.5 if STAGES[s_no] in FFNS else 1.0
                r = rstd_base[f"post{s_no}"]
                wait_y(dve, s_no)
                dve.wait_ge(gpost_landed, 16 * (s_no + 1))
                for t in range(TILES):
                    dve.wait_ge(rstd_ready, r + t + 1)
                    dve.scalar_tensor_tensor(xn[:, t, :], y_bank(t), rstd[:, r + t:r + t + 1], gpost[:, :],
                                             ALU.mult, ALU.mult).then_inc(y_scaled, 1)
                    dve.wait_ge(y_scaled, 2 * s_no + t + 1)
                    dve.scalar_tensor_tensor(x[:, t, :], xn[:, t, :], weight, x[:, t, :], ALU.mult, ALU.add)\
                       .then_inc(x_new, 1)

            def ffn(u, s_no):
                n0, d0 = first_block[STAGES[s_no]], u * FBLOCKS

                def mul(jc, t, g):
                    dve.wait_ge(silu_done, g(2 * (d0 + jc) + t + 1, 2))
                    dve.tensor_tensor(h[:, t, :], h[:, t, :], ps[:, 4 + t, FB:2 * FB], ALU.mult).then_inc(h_ready, 1)

                def behind(jc, g):
                    dve.wait_ge(ht_h, g(d0 + jc + 1, 1))
                    dve.tensor_tensor(ht_lo[:, :, :], ps[:, 6, :].rearrange("p (c t) -> p c t", c=FC),
                                      ht_hi[:, :, :].bitcast(F32), ALU.subtract).then_inc(ht_l, 1)
                    dve.wait_ge(d_hi, g(d0 + jc + 1, 1))
                    dve.tensor_tensor(down_lo[:, :], raw_down[:, :], down_hi[:, :].bitcast(F32), ALU.subtract)\
                       .then_inc(d_lo, 1)

                def step(jc, g, ahead):
                    if jc >= 1:
                        behind(jc - 1, g)
                    mul(jc, 0, g)
                    if ahead:
                        split_main(n0 + jc + 1, hi=g(2 * (n0 + jc + 1) + 1, 2))
                    mul(jc, 1, g)

                def fixed(c, k):
                    return c
                step(0, fixed, True)
                step(1, fixed, True)
                with dve.Fori(0, (FBLOCKS - PEEL) // 2) as i:
                    for q in range(2):
                        step(2 + q, lambda c, k, i=i: c + 2 * k * i, True)
                step(FBLOCKS - 1, fixed, n0 + FBLOCKS < total_blocks)
                behind(FBLOCKS - 1, fixed)

            def link(ins):
                shares[0] += 1
                ins.then_inc(share_step, 1)
                dve.wait_ge(share_step, shares[0])

            def attention(name, bias_of, finish):
                base = UNITS * ATT[name]

                def logits(n):
                    t, hh = n // HEADS, n % HEADS
                    keys = P * (t + 1)
                    dve.wait_ge(scores_ready, base + n + 1)
                    if base + n >= 3:
                        dve.wait_ge(pt_ready, base + n - 2)
                    first = neg_sinks[:, hh:hh + 1] if name == "swa" else 3.0e38
                    dve.tensor_tensor_reduce(logit[:, n % 3, 0:keys], ps[:, n % 3, 0:keys], bias_of(hh)[:, SEQ - keys:SEQ],
                                             1.0, first, ALU.add, ALU.min, low[:, base + n:base + n + 1])\
                       .then_inc(logits_ready, 1)

                def copy(n):
                    keys = P * (n // HEADS + 1)
                    dve.wait_ge(pt_ready, base + n + 1)
                    if base + n >= 3:
                        dve.wait_ge(pv_ready, base + n - 2)
                    dve.tensor_copy(probt[:, n % 3, 0:keys], ps[:, 3 + n % 3, 0:keys]).then_inc(pt_copied, 1)

                for n in range(UNITS + 4):
                    if n < UNITS:
                        logits(n)
                        if name == "swa" and n % HEADS == HEADS - 1:
                            dve.wait_ge(logits_ready, base + n + 1)
                            cols = slice(n + 1 - HEADS, n + 1)
                            dve.tensor_tensor(sink_exp[:, cols], low[:, cols], sinks[:, :], ALU.add).then_inc(sink_added, 1)
                    if 2 <= n < UNITS + 2:
                        copy(n - 2)
                    if n in (HEADS + 3, UNITS + 3):
                        t = 0 if n == HEADS + 3 else 1
                        dve.wait_ge(pv_ready, base + HEADS * (t + 1))
                        finish(t)

            def head_bank(t):
                return ps[:, 6 + t, :].rearrange("p (h d) -> p h d", h=HEADS)

            def finish_plain(name, col, extra=None, gate_no=None, add=False):
                def finish(t):
                    cols = slice(UNITS * ATT[name] + HEADS * t, UNITS * ATT[name] + HEADS * (t + 1))
                    dve.wait_ge(probs_ready, UNITS * ATT[name] + HEADS * (t + 1))
                    source = total[:, cols]
                    if extra is not None:
                        dve.wait_ge(sink_done, t + 1)
                        link(dve.tensor_tensor(share[:, cols], source, sink_exp[:, HEADS * t:HEADS * (t + 1)], ALU.add))
                        source = share[:, cols]
                    link(dve.reciprocal(share[:, cols], source))
                    if gate_no is not None:
                        link(dve.tensor_tensor(share[:, cols], share[:, cols],
                                               gate[:, t, HEADS * gate_no:HEADS * (gate_no + 1)], ALU.mult))
                    weights = spread(share[:, cols], [P, HEADS, HEAD])
                    dst = attn[:, t, col:col + 512].rearrange("p (h d) -> p h d", h=HEADS)
                    outs[0] += 1
                    if add:
                        ins = dve.tensor_tensor(branch, head_bank(t), weights, ALU.mult)
                        ins.then_inc(head_out, 1)
                        dve.wait_ge(head_out, outs[0])
                        link(dve.tensor_tensor(dst, dst, branch, ALU.add))
                    else:
                        dve.tensor_tensor(dst, head_bank(t), weights, ALU.mult).then_inc(head_out, 1)
                return finish

            dve.wait_ge(t_ready, 1)
            dve.tensor_copy(gcol[:, :], ps[:, 6, 0:G_ROWS]).then_inc(t_done, 1)
            dve.wait_ge(t_ready, 2)
            dve.tensor_scalar(neg_table[:, :], ps[0:SLOTS, 7, 0:BUCKETS], -1.0, None, ALU.mult).then_inc(t_done, 1)
            dve.wait_ge(t_done, 2)
            dve.memset(bias_rows, BIG).then_inc(rows_step, 1)
            dve.wait_ge(rows_step, 1)
            for b, first, last in BUCKET_RANGES:
                width = last - first + 1
                dve.tensor_copy(bias_rows[:, SEQ - 1 - last:SEQ - first], neg_table[:, b:b + 1].to_broadcast([SLOTS, width]))\
                   .then_inc(rows_step, 1)
            dve.wait_ge(rows_step, N_ROWS - 1)
            dve.memset(bias_rows[0:HEADS, 0:P], BIG).then_inc(rows_step, 1)
            dve.wait_ge(small_landed, 16 * N_SMALL)
            dve.tensor_scalar(neg_sinks[:, :], sinks[:, :], -1.0, None, ALU.mult).then_inc(neg_sinks_ready, 1)
            split_main(0)
            pre_norm(0)
            ffn(0, 0)
            post_norm(0)

            n0 = first_block["l0_mix"]
            pre_norm(1)
            split_main(n0 + 1)
            split_main(n0 + 2)
            turned_plain("qa", 4, lambda k: qk[:, k, :])
            turned_kv_heads("ka", 4)
            split_main(n0 + 3)
            lat = rstd_base["lat"]
            for r, buf in enumerate([stage[:, 0, 768:1024], stage[:, 1, 768:1024], latent[:, 0, 0:MLA_KV],
                                     latent[:, 1, 0:MLA_KV]]):
                dve.wait_ge(rstd_ready, lat + r + 1)
                dve.tensor_scalar(buf, buf, rstd[:, lat + r:lat + r + 1], None, ALU.mult).then_inc(lat_ready, 1)
            split_main(n0 + 4)
            turned("lat", 3, (xt_lo, xt_hi), gain=G_Q)
            dve.wait_ge(neg_sinks_ready, 1)
            dve.wait_ge(flip_done, 4)
            dve.wait_ge(d_lo, FBLOCKS)
            attention("swa", lambda hh: bias[:, hh, :], finish_plain("swa", 0, extra=True))

            def rotate(x1, x2, shape, cos, sin, tmp, done):
                for i, (u, v) in enumerate(((x1, cos), (x2, sin), (x2, cos), (x1, sin))):
                    ins = dve.tensor_tensor(tmp[i], u, v, ALU.mult)
                link(ins)
                dve.tensor_tensor(x1, tmp[0], tmp[1], ALU.subtract).then_inc(rope_step, 1)
                dve.tensor_tensor(x2, tmp[2], tmp[3], ALU.add).then_inc(done, 1)

            half_rope = ROPE // 2
            tmp_flat = logit[:, :, :].rearrange("p a b -> p (a b)")
            dve.wait_ge(proj_out, OUT["w_in0"][2])
            kr = [latent[:, :, MLA_KV + i * half_rope:MLA_KV + (i + 1) * half_rope] for i in range(2)]
            tables = [rope[:, :, i * half_rope:(i + 1) * half_rope] for i in range(2)]
            tmp = [tmp_flat[:, 32 * i:32 * i + 32].rearrange("p (t c) -> p t c", t=TILES) for i in range(4)]
            dve.wait_ge(pt_ready, UNITS)
            rotate(kr[0], kr[1], None, tables[0], tables[1], tmp, kr_done)
            dve.wait_ge(kr_done, 1)
            dve.wait_ge(rope_step, 1)
            dve.wait_ge(proj_out, OUT["up"][0])
            for t in range(TILES):
                qr = [mla_q[:, t, :, NOPE + i * half_rope:NOPE + (i + 1) * half_rope] for i in range(2)]
                wide = [tables[i][:, t, :].unsqueeze(1).to_broadcast([P, HEADS, half_rope]) for i in range(2)]
                tmp = [(tmp_flat if i < 2 else probt[:, :, :].rearrange("p a b -> p (a b)"))
                       [:, P * (2 * t + i % 2) + 128:P * (2 * t + i % 2) + 256].rearrange("p (h c) -> p h c", h=HEADS)
                       for i in range(4)]
                rotate(qr[0], qr[1], None, wide[0], wide[1], tmp, q_rotated)
            dve.wait_ge(q_rotated, 2)
            dve.wait_ge(rope_step, 3)
            for t in range(TILES):
                dve.tensor_copy(mla_k[:, t, :, NOPE:MLA_K],
                                latent[:, t, MLA_KV:MLA_KV + ROPE].unsqueeze(1).to_broadcast([P, HEADS, ROPE]))\
                   .then_inc(rope_done, 1)
            for i, dst in enumerate((mla_qt, mla_kt)):
                for hh in range(HEADS):
                    job = job_base["mla"] + HEADS * i + hh
                    dve.wait_ge(t_ready, job + 1)
                    dve.tensor_copy(dst[0:MLA_K, hh, :], t_bank(job)[0:MLA_K, :]).then_inc(t_done, 1)
            split_main(n0 + 5)
            attention("mla", lambda hh: causal[:, :], finish_plain("mla", 512))
            turned("out0", KD, (xt_lo, xt_hi))
            split_main(n0 + 6)
            post_norm(1)

            pre_norm(2)
            ffn(1, 2)
            post_norm(2)
            pre_norm(3)
            ffn(2, 3)
            post_norm(3)

            n0 = first_block["l1_mix"]
            pre_norm(4)
            split_main(n0 + 1)
            turned_plain("qc", 4, lambda k: qk[:, k, :])
            split_main(n0 + 2)
            for i, z in enumerate((zk, zv)):
                job = job_base["kvc"] + i
                dve.wait_ge(t_ready, job + 1)
                pe_cols = gcol[:, (G_PEK, G_PEV)[i]:(G_PEK, G_PEV)[i] + 16]
                for par in range(2):
                    for g in range(2):
                        rows = slice(64 * par, 64 * par + 64)
                        src = t_bank(job)[64 * g:64 * g + 64, :]
                        src = bass.AP(tensor=src.tensor, offset=src.offset + par,
                                      ap=[list(src.ap[0]), [2, 16], [CMP_STRIDE, NCMP]])
                        ins = dve.tensor_tensor(z[rows, :, g, :], src, spread(pe_cols[rows, :], [64, 16, NCMP]), ALU.add)
                ins.then_inc(t_done, 1)
            turned_kv_heads("ks", 4)
            split_main(n0 + 3)
            turned_kv_heads("kw", 6)
            split_main(n0 + 4)
            split_main(n0 + 5)
            split_main(n0 + 6)
            split_main(n0 + 7)
            dve.wait_ge(gate_exp, 2)
            dve.tensor_scalar(gate[:, :, :], gate[:, :, :], 1.0, None, ALU.add).then_inc(gate_done, 1)
            dve.wait_ge(gate_done, 1)
            dve.reciprocal(gate[:, :, :], gate[:, :, :]).then_inc(gate_done, 1)
            for i, z in enumerate((zk, zv)):
                dve.wait_ge(z_hi, i + 1)
                dve.tensor_tensor(z_part(xt_lo, i), z, z_part(xt_hi, i).bitcast(F32), ALU.subtract).then_inc(z_lo, 1)
            dve.wait_ge(hid_zero, 2)
            dve.memset(vcmp, 0.0).then_inc(hid_zero, 1)
            dve.wait_ge(hid_done, 2)
            for c in range(2):
                for g in range(2):
                    src = hid[:, 1, c, g * NCMP:(g + 1) * NCMP].unsqueeze(1).to_broadcast([P, 4, NCMP])
                    dve.tensor_copy(hid_rows[:, c, g, :, 0:NCMP], src).then_inc(hid_spread, 1)
            dve.wait_ge(cmp_kv_ready, 1)
            dve.tensor_copy(kcmp[:, :, 0:NCMP], ps[:, 2, 0:2 * NCMP].rearrange("p (g c) -> p g c", g=2))\
               .then_inc(cmp_kv_done, 1)
            dve.wait_ge(cmp_kv_ready, 2)
            dve.wait_ge(hid_zero, 3)
            for j in range(4):
                rows = slice(32 * j, 32 * j + 32)
                dve.tensor_copy(vcmp[rows, :, j, :], ps[rows, 3, 0:2 * HEAD].rearrange("p (g d) -> p g d", g=2))\
                   .then_inc(cmp_kv_done, 1)
            dve.wait_ge(const_step, N_CONST)
            for t in range(TILES):
                dve.wait_ge(cmp_s_ready, t + 1)
                off = cmp_off[:, t, :].unsqueeze(1).to_broadcast([P, HEADS // 2, CPAD])
                for par in range(2):
                    dve.tensor_tensor(cmp_view(t).rearrange("p (q two) c -> p q two c", two=2)[:, :, par, :],
                                      ps[:, t + 2 * par, 0:HEADS // 2 * CPAD].rearrange("p (q c) -> p q c", c=CPAD), off,
                                      ALU.add).then_inc(cmp_step, 1)
                dve.wait_ge(cmp_step, 4 * t + 2)
                dve.tensor_reduce(cmp_low[:, t, :], cmp_view(t), AX, ALU.min).then_inc(cmp_step, 1)
                dve.wait_ge(cmp_step, 4 * t + 3)
                dve.tensor_tensor(cmp_view(t), cmp_view(t), spread(cmp_low[:, t, :], [P, HEADS, CPAD]), ALU.subtract)\
                   .then_inc(cmp_step, 1)
            dve.wait_ge(gate_done, 2)
            for t in range(TILES):
                dve.wait_ge(cmp_e, t + 1)
                link(dve.tensor_reduce(cmp_sum[:, t, :], cmp_view(t), AX, ALU.add))
                ok = cmp_ok[:, t, :].unsqueeze(1).to_broadcast([P, HEADS, CPAD])
                dve.tensor_tensor(cmp_view(t), cmp_view(t), ok, ALU.mult).then_inc(cmp_p_ready, 1)
                link(dve.reciprocal(cmp_sum[:, t, :], cmp_sum[:, t, :]))
                link(dve.tensor_tensor(cmp_sum[:, t, :], cmp_sum[:, t, :], gate[:, t, 0:HEADS], ALU.mult))
            for t in range(TILES):
                dve.wait_ge(cmp_t_ready, t + 1)
                dve.tensor_copy(probt[:, t, :], ps[:, 2 + t, 0:SEQ]).then_inc(cmp_t_done, 1)
            split_main(n0 + 8)
            dve.wait_ge(d_lo, 3 * FBLOCKS)
            for t in range(TILES):
                dve.wait_ge(cmp_o_ready, t + 1)
                outs[0] += 1
                dve.tensor_tensor(attn[:, t, 0:512].rearrange("p (h d) -> p h d", h=HEADS), head_bank(t),
                                  spread(cmp_sum[:, t, :], [P, HEADS, HEAD]), ALU.mult).then_inc(head_out, 1)
            dve.wait_ge(head_out, outs[0])
            split_main(n0 + 9)
            attention("slc", lambda hh: bias[:, hh, :], finish_plain("slc", 0, gate_no=1, add=True))
            attention("win", lambda hh: bias[:, hh, :], finish_plain("win", 0, gate_no=2, add=True))
            turned_plain("qd", 4, lambda k: qk[:, k, :])
            turned_plain("kd", 4, lambda k: qk[:, 4 + k, :])
            attention("moba", lambda hh: bias[:, HEADS + hh, :], finish_plain("moba", 512))
            turned("out1", KD, (xt_lo, xt_hi))
            split_main(n0 + 10)
            post_norm(4)

            pre_norm(5)
            ffn(3, 5)
            post_norm(5)


def rope_tables():
    inv = (np.float32(10000.0) ** (-np.arange(0, ROPE, 2, dtype=np.float32) / np.float32(ROPE))).astype(np.float32)
    angle = np.arange(SEQ, dtype=np.float32)[:, None] * inv[None, :]
    return np.concatenate([np.cos(angle), np.sin(angle)], axis=1).astype(np.float32)


_INS = ["x", "rel_bias_table"]
for _s in STAGES:
    _INS += [f"{_s}_pre", f"{_s}_post"]
    if _s in FFNS:
        _INS += [f"{_s}_wg", f"{_s}_wu", f"{_s}_wd"]
_INS += ["l0_w_in", "l0_sinks", "l0_mla_q_norm", "l0_mla_w_uq", "l0_mla_kv_norm", "l0_mla_w_ukv", "l0_w_out",
         "l1_w_in", "l1_nsa_pe_k", "l1_nsa_pe_v", "l1_nsa_wk1", "l1_nsa_wk2", "l1_nsa_wv1", "l1_nsa_wv2", "l1_w_out"]


def kernel(**inputs):
    import concourse.bacc as bacc
    from concourse.bass_utils import run_bass_kernel_spmd

    nc = bacc.Bacc("TRN2", target_bir_lowering=False, num_devices=1)
    arrays, args = {}, {}
    given = {name: np.ascontiguousarray(inputs[name]) for name in _INS}
    given["rope_tables"] = rope_tables()
    for name, value in given.items():
        arrays[f"in_{name}"] = value
        args[name] = nc.dram_tensor(f"in_{name}", value.shape, mybir.dt.from_np(value.dtype), kind="ExternalInput").ap()
    out = nc.dram_tensor("out_0", (1, SEQ, D), F32, kind="ExternalOutput").ap()
    trunk(nc, args, out)
    result = run_bass_kernel_spmd(nc, [arrays], core_ids=[0])
    return result.results[0]["out_0"]
```

```python
import math
from contextlib import ExitStack

import numpy as np

import concourse.bass as bass
from concourse import mybir

F32 = mybir.dt.float32
F32R = mybir.dt.float32r
ALU = mybir.AluOpType
ACT = mybir.ActivationFunctionType
AX = mybir.AxisListType.X

P = 128
SEQ = 256
TILES = SEQ // P
D = 1024
KD = D // P
DFF = 2816
EPS = 1e-6
BIG = 1e30

HEAD = 64
HEADS = 8
BUCKETS, SLOTS, MAX_DIST = 32, 24, 1024
MLA_Q, MLA_KV, NOPE, ROPE = 256, 128, 64, 32
MLA_K = NOPE + ROPE
CMP_BLOCK, CMP_STRIDE, CMP_HID = 32, 16, 256
NCMP = (SEQ - CMP_BLOCK) // CMP_STRIDE + 1
CPAD = 16
CROW = 32

FB = 256
FBLOCKS = DFF // FB
FC = FB // P
PEEL = 3
MAIN = KD * 512
DOWN = FC * D

FFNS = ("l0_ffn1", "l0_ffn2", "l1_ffn1", "l1_ffn2")
STAGES = ("l0_ffn1", "l0_mix", "l0_ffn2", "l1_ffn1", "l1_mix", "l1_ffn2")
MIX0_BLOCKS = ((0, 512), (512, 512), (1024, 160))
MIX1_BLOCKS = ((0, 512), (512, 512), (1024, 280), "l1_nsa_wk1", "l1_nsa_wv1", (1304, 512), (1816, 512), (2328, 512))


def bucket_ranges():
    n = np.arange(SEQ)
    nf = np.maximum(n, 1).astype(np.float32)
    exact = BUCKETS // 2
    large = exact + (np.log(nf / np.float32(exact)) / np.float32(math.log(MAX_DIST / exact))
                     * np.float32(BUCKETS - exact)).astype(np.int32)
    bucket = np.where(n < exact, n, np.minimum(large, BUCKETS - 1))
    return [(int(b), int(np.flatnonzero(bucket == b)[0]), int(np.flatnonzero(bucket == b)[-1]))
            for b in np.unique(bucket)]


BUCKET_RANGES = bucket_ranges()


def trunk(nc, a, out):
    n_mix0 = len(MIX0_BLOCKS) + 3
    n_mix1 = len(MIX1_BLOCKS) + 2
    counts = {"l0_mix": n_mix0, "l1_mix": n_mix1}
    first_block, n = {}, 0
    for s in STAGES:
        first_block[s] = n
        n += counts.get(s, FBLOCKS)
    total_blocks = n

    def main_dmas(n):
        for s in STAGES:
            if s in FFNS and first_block[s] <= n < first_block[s] + FBLOCKS:
                return 0 if n == 0 else 2
        return 2 if n == first_block["l0_mix"] + len(MIX0_BLOCKS) else 1

    def landed_value(n):
        return 16 * sum(main_dmas(m) for m in range(n % 2, n + 1, 2))

    job_counts = [("qa", 4), ("ka", 1), ("lat", 3), ("mla", 16), ("qc", 4), ("kvc", 2), ("ks", 1),
                  ("kw", 1), ("qd", 4), ("kd", 4)]
    job_base, n = {}, 0
    for name, k in job_counts:
        job_base[name] = n
        n += k

    TURNS = {name: i for i, name in enumerate(("norm0", "norm1", "out0", "norm2", "norm3", "norm4", "out1", "norm5"))}

    proj_base = {"w_in0": 0, "up": 2 * len(MIX0_BLOCKS), "w_in1": 2 * len(MIX0_BLOCKS) + 4}
    rstd_base, n = {}, 0
    for name, k in [("pre0", 2), ("post0", 2), ("pre1", 2), ("lat", 4), ("post1", 2), ("pre2", 2), ("post2", 2),
                    ("pre3", 2), ("post3", 2), ("pre4", 2), ("post4", 2), ("pre5", 2), ("post5", 2)]:
        rstd_base[name] = n
        n += k
    n_rstd = n
    ss_of, n = {}, 0
    for name, r in rstd_base.items():
        for i in range(4 if name == "lat" else 2):
            ss_of[r + i] = n
            n += 2 if name.startswith("post") else 1
    n_ss = n
    OUT = {"w_in0": [2, 4, 6], "up": [10, 18], "w_in1": [20, 24, 30, 32, 34, 36]}
    ATT = {"swa": 0, "mla": 1, "slc": 2, "win": 3, "moba": 4}
    UNITS = TILES * HEADS
    OUT_BEFORE = {"swa": 0, "mla": 2, "slc0": 4, "slc": 6, "win": 8, "moba": 10, "end": 12}

    LAG_T, LAG_V = 3, 5

    G_PRE, G_Q, G_KV, G_PEK, G_PEV, G_ROWS = 0, 48, 50, 51, 67, 83

    with ExitStack() as ctx:
        def sb(name, shape, dt=F32):
            return ctx.enter_context(nc.sbuf_tensor(name, shape, dt))

        def sem(name):
            return ctx.enter_context(nc.semaphore(name))

        ps = ctx.enter_context(nc.psum_tensor("ps", [P, 8, 512], F32))

        raw = sb("raw", [P, 2, MAIN])
        w_hi = sb("w_hi", [P, 2, MAIN], F32R)
        w_lo = sb("w_lo", [P, 2, MAIN], F32R)
        raw_down = sb("raw_down", [P, DOWN])
        down_hi = sb("down_hi", [P, DOWN], F32R)
        down_lo = sb("down_lo", [P, DOWN], F32R)
        x = sb("x", [P, TILES, D])
        xn = sb("xn", [P, TILES, D])
        xt_hi = sb("xt_hi", [P, KD, SEQ], F32R)
        xt_lo = sb("xt_lo", [P, KD, SEQ], F32R)
        gpost = sb("gpost", [P, D])
        h = sb("h", [P, TILES, FB])
        ht_hi = sb("ht_hi", [P, FC, SEQ], F32R)
        ht_lo = sb("ht_lo", [P, FC, SEQ], F32R)
        bias = sb("bias", [P, 2 * HEADS, SEQ])
        qk = sb("qk", [P, 10, SEQ])
        val = sb("val", [P, TILES, 512])
        val2 = sb("val2", [P, TILES, 2, P])
        logit = sb("logit", [P, 3, SEQ])
        probt = sb("probt", [P, 3, SEQ])
        ident = sb("ident", [P, P])
        flip = sb("flip", [P, P])
        causal = sb("causal", [P, SEQ])
        cmp_off = sb("cmp_off", [P, TILES, CPAD])
        cmp_ok = sb("cmp_ok", [P, TILES, CPAD])
        grows = sb("grows", [G_ROWS, P])
        gcol = sb("gcol", [P, G_ROWS])
        table = sb("table", [BUCKETS, SLOTS])
        neg_table = sb("neg_table", [SLOTS, BUCKETS])
        half = sb("half", [P, 1])
        sumsq = sb("sumsq", [P, n_ss])
        meansq = sb("meansq", [P, n_rstd])
        rstd = sb("rstd", [P, n_rstd])
        low = sb("low", [P, len(ATT) * UNITS])
        total = sb("total", [P, len(ATT) * UNITS])
        share = sb("share", [P, len(ATT) * UNITS])
        cmp_low = sb("cmp_low", [P, TILES, HEADS])
        cmp_sum = sb("cmp_sum", [P, TILES, HEADS])
        neg_sinks = sb("neg_sinks", [P, HEADS])
        sinks = sb("sinks", [P, HEADS])
        sink_exp = sb("sink_exp", [P, UNITS])
        gate = sb("gate", [P, TILES, 3 * HEADS])
        rope = sb("rope", [P, TILES, ROPE])
        w2k = sb("w2k", [P, 2, 2, HEAD])
        w2v = sb("w2v", [P, 2, HEAD])
        hid = sb("hid", [P, 2, 2 * NCMP])
        rows_dram = nc.dram_tensor("bias_rows", [SLOTS, SEQ + P], F32, kind="Internal").ap()

        grows0 = probt[0:8, 0, 0:P]
        stage = xn
        bias_rows = logit[0:SLOTS, :, :].rearrange("p t c -> p (t c)")[:, 0:SEQ + P]
        hankel = [val[:, :, :].rearrange("p t (h c) -> p (t h) c", h=2), qk[:, 0:4, :], qk[:, 4:8, :]]
        attn = raw_down[:, :].rearrange("p (t c) -> p t c", t=TILES)
        latent = val2[:, :, :, :].rearrange("p t a c -> p t (a c)")[:, :, 0:MLA_KV + ROPE]
        mla_qt = bias[:, HEADS:2 * HEADS, :]
        mla_kt = qk
        hid_rows = gpost[:, 0:512].rearrange("p (a b j c) -> p a b j c", a=2, b=2, j=4)
        kcmp = gpost[:, 512:512 + CPAD]
        moba_at = (first_block["l1_mix"] + len(MIX1_BLOCKS)) % 2
        moba_q = raw[:, moba_at, 0:8 * SEQ].rearrange("p (h c) -> p h c", h=8)
        moba_k = raw[:, moba_at, 8 * SEQ:12 * SEQ].rearrange("p (h c) -> p h c", h=4)
        mla_q = xn[:, :, 0:HEADS * MLA_K].rearrange("p t (h c) -> p t h c", h=HEADS)
        mla_k = bias[:, 0:6, :].rearrange("p a b -> p (a b)").rearrange("p (t h c) -> p t h c", t=TILES, h=HEADS)
        zk = logit[:, :, :].rearrange("p a b -> p (a b)")[:, 0:480].rearrange("p (m g c) -> p m g c", m=16, g=2)
        zv = probt[:, :, :].rearrange("p a b -> p (a b)")[:, 0:480].rearrange("p (m g c) -> p m g c", m=16, g=2)
        vcmp = h[:, :, :].rearrange("p g (a d) -> p g a d", a=4)
        branch = h[:, :, :].rearrange("p t c -> p (t c)").rearrange("p (h d) -> p h d", h=HEADS)

        def score_bank(u):
            return ps[:, u % 3, :]

        def turned_bank(u):
            return ps[:, 3 + u % 3, :]

        def prob_slot(u):
            return logit[:, u % 6, :] if u % 6 < 3 else gpost[:, (u % 6 - 3) * SEQ:(u % 6 - 2) * SEQ]

        def probt_slot(u):
            return probt[:, u % 4, :] if u % 4 < 3 else gpost[:, 3 * SEQ:4 * SEQ]

        x_landed = [sem("x_landed0"), sem("x_landed1")]
        first_landed = [sem("first_landed0"), sem("first_landed1")]
        small_landed, gains_landed = sem("small_landed"), sem("gains_landed")
        main_landed = [sem("main_landed0"), sem("main_landed1")]
        down_landed = sem("down_landed")
        gpost_landed = sem("gpost_landed")
        rows_stored = sem("rows_stored")
        hankel_landed = sem("hankel_landed")
        main_hi, main_lo = sem("main_hi"), sem("main_lo")
        d_hi, d_lo, down_used = sem("d_hi"), sem("d_lo"), sem("down_used")
        const_step = sem("const_step")
        ss_ready, ms_ready, rstd_ready = sem("ss_ready"), sem("ms_ready"), sem("rstd_ready")
        y_ready = sem("y_ready")
        y_scaled, x_new = sem("y_scaled"), sem("x_new")
        xt_ready, xt_h, xt_done = sem("xt_ready"), sem("xt_h"), sem("xt_done")
        prep_ready, prep_done = sem("prep_ready"), sem("prep_done")
        t_ready, t_hi, t_done = sem("t_ready"), sem("t_hi"), sem("t_done")
        gu_ready, silu_done, h_ready = sem("gu_ready"), sem("silu_done"), sem("h_ready")
        ht_ready, ht_h, ht_l = sem("ht_ready"), sem("ht_h"), sem("ht_l")
        rows_step = sem("rows_step")
        flip_ready, flip_done = sem("flip_ready"), sem("flip_done")
        proj_ready, proj_out = sem("proj_ready"), sem("proj_out")
        rope_step, rope_done = sem("rope_step"), sem("rope_done")
        kr_done, q_rotated, lat_ready = sem("kr_done"), sem("q_rotated"), sem("lat_ready")
        scores_ready, logits_ready, probs_ready = sem("scores_ready"), sem("logits_ready"), sem("probs_ready")
        pt_ready, pt_copied = sem("pt_ready"), sem("pt_copied")
        pv_ready, head_out, share_step = sem("pv_ready"), sem("head_out"), sem("share_step")
        sink_added, sink_done = sem("sink_added"), sem("sink_done")
        z_hi, z_lo = sem("z_hi"), sem("z_lo")
        hid_ready, hid_done, hid_turned = sem("hid_ready"), sem("hid_done"), sem("hid_turned")
        hid_spread, hid_zero = sem("hid_spread"), sem("hid_zero")
        cmp_kv_ready, cmp_kv_done, vcmp_zero = sem("cmp_kv_ready"), sem("cmp_kv_done"), sem("vcmp_zero")
        cmp_s_ready, cmp_step, cmp_e, cmp_p_ready = sem("cmp_s_ready"), sem("cmp_step"), sem("cmp_e"), sem("cmp_p_ready")
        neg_sinks_ready, q_zeroed = sem("neg_sinks_ready"), sem("q_zeroed")
        cmp_t_ready, cmp_t_done, cmp_o_ready, cmp_out = sem("cmp_t_ready"), sem("cmp_t_done"), sem("cmp_o_ready"), sem("cmp_out")
        gate_exp, gate_done = sem("gate_exp"), sem("gate_done")
        stored = sem("stored")
        block = ctx.enter_context(nc.Block())

        scale_a = -HEAD ** -0.5
        N_CONST = 11
        N_SMALL = len(STAGES) + 10
        N_ROWS = len(BUCKET_RANGES) + 2

        def main_view(buf, n, k, width):
            return buf[:, n % 2, k * 512:k * 512 + width]

        def wait_block_used(eng, n, g=lambda c, k: c):
            if n < 0:
                return
            s = next(s for s in reversed(STAGES) if first_block[s] <= n)
            m = n - first_block[s]
            if s in FFNS:
                eng.wait_ge(gu_ready, g(2 * (FFNS.index(s) * FBLOCKS + m + 1), 2))
            elif s == "l0_mix":
                if m <= len(MIX0_BLOCKS):
                    eng.wait_ge(proj_ready, 2 * (m + 1) + (2 if m == len(MIX0_BLOCKS) else 0))
                else:
                    eng.wait_ge(y_ready, 4 + 2 * (m - len(MIX0_BLOCKS)))
            elif m >= len(MIX1_BLOCKS):
                eng.wait_ge(y_ready, 16 + 2 * (m - len(MIX1_BLOCKS) + 1))
            elif isinstance(MIX1_BLOCKS[m], str):
                eng.wait_ge(hid_ready, m - 2)
            else:
                eng.wait_ge(proj_ready, proj_base["w_in1"] + 2 * (m + 1 if m < 3 else m - 1))

        def y_value(s_no, t, part):
            return 4 * s_no + (2 * t + part if STAGES[s_no] in FFNS else 2 * part + t) + 1

        def pieces(n):
            m = n - first_block["l0_mix"]
            if m == len(MIX0_BLOCKS):
                return [lambda b: b[:, n % 2, 0:1536], lambda b: b[:, n % 2, 1536:2560]]
            width = 512
            if 0 <= m < len(MIX0_BLOCKS):
                width = MIX0_BLOCKS[m][1]
            m = n - first_block["l1_mix"]
            if 0 <= m < len(MIX1_BLOCKS) and not isinstance(MIX1_BLOCKS[m], str):
                width = MIX1_BLOCKS[m][1]

            def part(half_no):
                lo, hi = half_no * MAIN // 2, (half_no + 1) * MAIN // 2
                return lambda b: b[:, n % 2, lo:hi].rearrange("p (k c) -> p k c", c=512)[:, :, 0:width]
            return [part(0), part(1)]

        def z_part(buf, i):
            return buf[:, 1024 * i:1024 * i + 480].rearrange("p (m g c) -> p m g c", m=16, g=2)

        def cmp_view(t, width=CPAD):
            return hid_rows[:, t, :, :, 0:width].rearrange("p g a c -> p (g a) c")

        def spread(ap, shape):
            return ap.unsqueeze(len(ap.shape)).to_broadcast(shape)

        def xt_bank(t, k):
            return ps[:, (4 if t == 0 else 0) + k // 2, k % 2 * P:(k % 2 + 1) * P]

        def down_part(buf, part):
            return buf[:, :].rearrange("p (c n) -> p c n", c=FC)[:, :, part * 512:part * 512 + 512]

        def t_bank(job):
            return ps[:, 6 + job % 2, 0:SEQ]

        @block.sync
        def _(sp):
            def ffn_main(w, j, n):
                cols = bass.ds(j * FB, FB) if not isinstance(j, int) else slice(j * FB, (j + 1) * FB)
                dst = raw[:, n % 2, :].rearrange("p (k two c) -> p k two c", two=2, c=FB)
                size = KD // 2 if isinstance(n, int) and n == 0 else KD
                for k in range(0, KD, size):
                    for i, part in enumerate(("wg", "wu")):
                        src = a[f"{w}_{part}"].rearrange("(k p) n -> p k n", p=P)[:, k:k + size, cols]
                        landed = main_landed[n % 2] if size == KD else first_landed[k // size]
                        sp.dma_start(dst[:, k:k + size, i, :], src).then_inc(landed, 16)

            def ffn_down(w, j):
                rows = a[f"{w}_wd"].rearrange("(j c p) n -> j p c n", p=P, c=FC)
                src = rows[j] if isinstance(j, int) else rows[bass.ds(j, 1)].rearrange("o p c n -> (o p) c n")
                sp.dma_start(raw_down[:, :].rearrange("p (c n) -> p c n", c=FC), src).then_inc(down_landed, 16)

            def ring_wait(n):
                if n >= 2:
                    sp.wait_ge(main_lo, 2 * (n - 1))

            def down_wait(d):
                if d >= 1:
                    sp.wait_ge(d_lo, 2 * d)

            for t in range(TILES):
                sp.dma_start(x[:, t, :], a["x"][0, t * P:(t + 1) * P, :]).then_inc(x_landed[t], 16)
            late_down = None
            for s_no, s in enumerate(STAGES):
                n0 = first_block[s]
                if s in FFNS:
                    d0 = FFNS.index(s) * FBLOCKS
                    for j in range(PEEL):
                        ring_wait(n0 + j)
                        if j == 0 and s_no == 5:
                            sp.wait_ge(scores_ready, UNITS * len(ATT))
                        ffn_main(s, j, n0 + j)
                        if j == 0 and late_down:
                            late_down()
                        if j == 1 and s_no > 0 and STAGES[s_no - 1] not in FFNS:
                            sp.wait_ge(xt_ready, 8 * (TURNS["out0" if s_no == 2 else "out1"] + 1))
                        if j >= 1:
                            down_wait(d0 + j - 1)
                            ffn_down(s, j - 1)
                    with sp.Fori(0, (FBLOCKS - PEEL) // 2) as i:
                        for q in range(2):
                            j = PEEL + q
                            sp.wait_ge(main_lo, 4 * i + 2 * (n0 + j - 1))
                            ffn_main(s, 2 * i + j, n0 + j)
                            sp.wait_ge(d_lo, 4 * i + 2 * (d0 + j - 1))
                            ffn_down(s, 2 * i + (j - 1))

                    def late_down(s=s, d=d0 + FBLOCKS - 1):
                        down_wait(d)
                        ffn_down(s, FBLOCKS - 1)
                    if s == STAGES[-1]:
                        late_down()
                    continue
                if s == "l0_mix":
                    for b, (c0, width) in enumerate(MIX0_BLOCKS):
                        ring_wait(n0 + b)
                        dst = raw[:, (n0 + b) % 2, :].rearrange("p (k c) -> p k c", c=512)[:, :, 0:width]
                        sp.dma_start(dst, a["l0_w_in"].rearrange("(k p) n -> p k n", p=P)[:, :, c0:c0 + width])\
                          .then_inc(main_landed[(n0 + b) % 2], 16)
                        if b == 0:
                            late_down()
                            late_down = None
                    n = n0 + len(MIX0_BLOCKS)
                    ring_wait(n)
                    sp.dma_start(raw[:, n % 2, 0:1536].rearrange("p (k c) -> p k c", k=2),
                                 a["l0_mla_w_uq"].rearrange("(k p) n -> p k n", p=P)).then_inc(main_landed[n % 2], 16)
                    sp.dma_start(raw[:, n % 2, 1536:2560], a["l0_mla_w_ukv"]).then_inc(main_landed[n % 2], 16)
                    n += 1
                else:
                    for b, what in enumerate(MIX1_BLOCKS):
                        ring_wait(n0 + b)
                        if isinstance(what, str):
                            sp.dma_start(raw[:, (n0 + b) % 2, :].rearrange("p (m c) -> p m c", c=CMP_HID),
                                         a[what].rearrange("(m p) n -> p m n", p=P)).then_inc(main_landed[(n0 + b) % 2], 16)
                            continue
                        c0, width = what
                        dst = raw[:, (n0 + b) % 2, :].rearrange("p (k c) -> p k c", c=512)[:, :, 0:width]
                        sp.dma_start(dst, a["l1_w_in"].rearrange("(k p) n -> p k n", p=P)[:, :, c0:c0 + width])\
                          .then_inc(main_landed[(n0 + b) % 2], 16)
                        if b == 0:
                            late_down()
                            late_down = None
                    n = n0 + len(MIX1_BLOCKS)
                w_out = a["l0_w_out" if s == "l0_mix" else "l1_w_out"].rearrange("(k p) n -> p k n", p=P)
                for half_no in range(2):
                    ring_wait(n)
                    sp.dma_start(raw[:, n % 2, :].rearrange("p (k c) -> p k c", c=512),
                                 w_out[:, :, half_no * 512:(half_no + 1) * 512]).then_inc(main_landed[n % 2], 16)
                    n += 1
            for t in range(TILES):
                for part in range(2):
                    sp.wait_ge(x_new, 4 * (len(STAGES) - 1) + 2 * t + part + 1)
                    cols = slice(part * 512, part * 512 + 512)
                    sp.dma_start(out[0, t * P:(t + 1) * P, cols], x[:, t, cols]).then_inc(stored, 16)
            sp.wait_ge(stored, 2 * 16 * TILES)

        @block.gpsimd
        def _(pool):
            steps = [0]

            def step(ins):
                steps[0] += 1
                ins.then_inc(const_step, 1)
                pool.wait_ge(const_step, steps[0])

            step(pool.memset(ident[:, :], 0.0))
            step(pool.affine_select(out=ident[:, :], in_=ident[:, :], compare_op=ALU.not_equal, fill=1.0,
                                    base=0, pattern=[[-1, P]], channel_multiplier=1))
            loads = [(table[:, :], a["rel_bias_table"])]
            for s_no, s in enumerate(STAGES):
                loads.append((grows[8 * s_no:8 * s_no + 8, :], a[f"{s}_pre"].rearrange("(c p) -> c p", p=P)))
            loads += [(grows[G_Q:G_Q + 2, :], a["l0_mla_q_norm"].rearrange("(c p) -> c p", p=P)),
                      (grows[G_KV:G_KV + 1, :], a["l0_mla_kv_norm"].rearrange("(c p) -> c p", p=P)),
                      (grows[G_PEK:G_PEK + 16, :], a["l1_nsa_pe_k"].rearrange("(m a) d -> m (a d)", a=2)),
                      (grows[G_PEV:G_PEV + 16, :], a["l1_nsa_pe_v"].rearrange("(m a) d -> m (a d)", a=2)),
                      (w2v[:, :, :], a["l1_nsa_wv2"].rearrange("(k p) d -> p k d", p=P)),
                      (w2k[:, :, 0, :], a["l1_nsa_wk2"].rearrange("(k p) d -> p k d", p=P)),
                      (w2k[:, :, 1, :], a["l1_nsa_wk2"].rearrange("(k p) d -> p k d", p=P)),
                      (rope[:, :, :], a["rope_tables"].rearrange("(t p) c -> p t c", p=P)),
                      (sinks[:, :], bass.AP(tensor=a["l0_sinks"].tensor, offset=0, ap=[[0, P], [1, HEADS]]))]
            assert len(loads) == N_SMALL
            for dst, src in loads:
                pool.dma_start(dst, src).then_inc(small_landed, 16)
            for m in (flip, causal):
                step(pool.memset(m[:, :], 0.0))
            step(pool.memset(cmp_off[:, :, :], 0.0))
            step(pool.memset(cmp_ok[:, :, :], 1.0))
            step(pool.memset(half[:, :], -0.5))
            step(pool.affine_select(out=flip[:, :], in_=flip[:, :], compare_op=ALU.not_equal, fill=1.0,
                                    base=1 - P, pattern=[[1, P]], channel_multiplier=1))
            step(pool.affine_select(out=causal[:, P:SEQ], in_=causal[:, P:SEQ], compare_op=ALU.is_ge, fill=BIG,
                                    base=0, pattern=[[-1, P]], channel_multiplier=1))
            for m, fill in ((cmp_off, BIG), (cmp_ok, 0.0)):
                step(pool.affine_select(out=m[:, :, :], in_=m[:, :, :], compare_op=ALU.is_ge, fill=fill,
                                        base=1 - CMP_BLOCK, pattern=[[P, TILES], [-CMP_STRIDE, CPAD]],
                                        channel_multiplier=1))

            zeroed = [0]

            def zero_q(buf):
                for i in range(2):
                    pool.memset(buf[64 * (1 - i):64 * (2 - i), 4 * i:4 * i + 4, :], 0.0).then_inc(q_zeroed, 1)
                    zeroed[0] += 1
                    pool.wait_ge(q_zeroed, zeroed[0])
            lat = rstd_base["lat"]
            for r in range(n_rstd):
                if r == lat:
                    pool.wait_ge(flip_ready, 4)
                    zero_q(qk)
                if r == rstd_base["post4"]:
                    pool.wait_ge(x_new, 4 * 4)
                    pool.memset(gpost[:, 0:512 + CPAD], 0.0).then_inc(hid_zero, 1)
                    pool.wait_ge(hid_zero, 1)
                    pool.wait_ge(flip_ready, 10)
                    zero_q(qk)
                    pool.wait_ge(main_lo, 2 * (first_block["l1_mix"] + len(MIX1_BLOCKS) + 1))
                    zero_q(moba_q)
                size = D if not lat <= r < lat + 4 else (MLA_Q if r < lat + 2 else MLA_KV)
                c = ss_of[r]
                if ss_of.get(r + 1, n_ss) == c + 2:
                    pool.wait_ge(ss_ready, c + 2)
                    pool.tensor_scalar(meansq[:, r:r + 1], sumsq[:, c:c + 1], sumsq[:, c + 1:c + 2], D * EPS, ALU.add,
                                       ALU.add).then_inc(ms_ready, 1)
                else:
                    pool.wait_ge(ss_ready, c + 1)
                    pool.tensor_scalar(meansq[:, r:r + 1], sumsq[:, c:c + 1], 1.0 / size, EPS, ALU.mult, ALU.add)\
                        .then_inc(ms_ready, 1)
                pool.wait_ge(ms_ready, r + 1)
                pool.tensor_tensor(rstd[:, r:r + 1], meansq[:, r:r + 1], half[:, :], ALU.pow).then_inc(rstd_ready, 1)

        @block.scalar
        def _(act):
            act.dma_start(grows0, a[f"{STAGES[0]}_pre"].rearrange("(c p) -> c p", p=P)).then_inc(gains_landed, 16)

            def load_hankel(quartet, slot):
                src = bass.AP(tensor=rows_dram.tensor, offset=quartet * 4 * (SEQ + P),
                              ap=[[1, P], [SEQ + P, 4], [1, SEQ]])
                act.dma_start(hankel[slot], src).then_inc(hankel_landed, 16)

            def copy_bias(f0, count):
                for f in range(f0, f0 + count):
                    pair = f if f < 4 else f - 4
                    act.wait_ge(flip_ready, f + 1)
                    act.activation(bias[:, 2 * pair:2 * pair + 2, :],
                                   ps[:, 4 + f % 2, :].rearrange("p (h c) -> p h c", h=2), ACT.Copy).then_inc(flip_done, 1)

            def load_gpost(s):
                act.dma_start(gpost[:, :], bass.AP(tensor=a[f"{s}_post"].tensor, offset=0, ap=[[0, P], [1, D]]))\
                   .then_inc(gpost_landed, 16)

            def split_main(n, g=lambda c, k: c):
                if n > 0:
                    act.wait_ge(main_landed[n % 2], g(landed_value(n), 32))
                wait_block_used(act, n - 2, g)
                for i, part in enumerate(pieces(n)):
                    if n == 0:
                        act.wait_ge(first_landed[i], 32)
                    act.activation(part(w_hi), part(raw), ACT.Copy).then_inc(main_hi, 1)

            def turned_hi(name, t, gain=None):
                base = TURNS[name]
                for k in range(KD):
                    if k % 2 == 0:
                        act.wait_ge(xt_ready, 8 * base + 4 * t + k // 2 + 1)
                    kw = {} if gain is None else {"scale": gcol[:, gain + k:gain + k + 1]}
                    act.activation(xt_hi[:, k, t * P:(t + 1) * P], xt_bank(t, k), ACT.Copy, **kw).then_inc(xt_h, 1)

            def pre_norm(s_no):
                if s_no == 0:
                    act.wait_ge(prep_done, 1)
                for t in range(TILES):
                    turned_hi(f"norm{s_no}", t, gain=8 * s_no)
                    r = ss_of[rstd_base[f"pre{s_no}"] + t]
                    act.activation(xn[:, t, :], x[:, t, :], ACT.Square, accum_out=sumsq[:, r:r + 1]).then_inc(ss_ready, 1)
                    if s_no == 0 and t == 0:
                        split_main(0)
                if STAGES[s_no] in FFNS:
                    load_gpost(STAGES[s_no])

            def post_squares(s_no):
                for t in range(TILES):
                    for part in range(2):
                        act.wait_ge(y_ready, y_value(s_no, t, part))
                        if t == 1:
                            act.wait_ge(y_scaled, 4 * s_no + part + 1)
                        r = ss_of[rstd_base[f"post{s_no}"] + t] + part
                        act.activation(ps[:, (6, 0)[t] + part, :], ps[:, 2 * t + part, :], ACT.Square,
                                       accum_out=sumsq[:, r:r + 1]).then_inc(ss_ready, 1)

            def ffn(u, s_no, aside=None):
                n0, d0 = first_block[STAGES[s_no]], u * FBLOCKS

                def silu(jc, t, g):
                    act.wait_ge(gu_ready, g(2 * (d0 + jc) + t + 1, 2))
                    if d0 + jc >= 1:
                        act.wait_ge(ht_ready, g(d0 + jc, 1))
                    r = rstd_base[f"pre{s_no}"] + t
                    if isinstance(jc, int) and jc == 0:
                        act.wait_ge(rstd_ready, r + 1)
                    act.activation(h[:, t, :], ps[:, 4 + t, 0:FB], ACT.Silu, scale=rstd[:, r:r + 1]).then_inc(silu_done, 1)

                def turned_h(jc, g):
                    act.wait_ge(ht_ready, g(d0 + jc + 1, 1))
                    act.activation(ht_hi[:, :, :], ps[:, 6, :].rearrange("p (c t) -> p c t", c=FC), ACT.Copy)\
                       .then_inc(ht_h, 1)

                def down_rows(jc, part, g):
                    if part == 0:
                        act.wait_ge(down_landed, g(16 * (d0 + jc + 1), 16))
                    act.activation(down_part(down_hi, part), down_part(raw_down, part), ACT.Copy).then_inc(d_hi, 1)

                def behind(jc, g):
                    turned_h(jc, g)
                    for part in range(2):
                        down_rows(jc, part, g)

                def step(jc, g, ahead):
                    if jc >= 1:
                        behind(jc - 1, g)
                    silu(jc, 0, g)
                    if ahead:
                        split_main(n0 + jc + 1, g)
                    silu(jc, 1, g)

                def fixed(c, k):
                    return c
                step(0, fixed, True)
                if aside:
                    aside()
                step(1, fixed, True)
                with act.Fori(0, (FBLOCKS - PEEL) // 2) as i:
                    for q in range(2):
                        step(2 + q, lambda c, k, i=i: c + (2 * k if k != 32 else 32) * i, True)
                step(FBLOCKS - 1, fixed, n0 + FBLOCKS < total_blocks)
                act.wait_ge(down_used, 2 * (d0 - u + FBLOCKS - 2) + 1)
                down_rows(FBLOCKS - 1, 0, fixed)
                turned_h(FBLOCKS - 1, fixed)
                down_rows(FBLOCKS - 1, 1, fixed)

            def project_out(j0, s_no, copies):
                for t in range(TILES):
                    r = rstd_base[f"pre{s_no}"] + t
                    act.wait_ge(rstd_ready, r + 1)
                    act.wait_ge(proj_ready, j0 + t + 1)
                    for dst, src in copies(t):
                        act.activation(dst, src, ACT.Copy, scale=rstd[:, r:r + 1]).then_inc(proj_out, 1)

            def exps(*names):
                base = UNITS * ATT[names[0]]
                for u in range(base, base + UNITS * len(names)):
                    n = u % UNITS
                    t = n // HEADS
                    keys = P * (t + 1)
                    act.wait_ge(logits_ready, u + 1)
                    act.activation(prob_slot(u)[:, 0:keys], prob_slot(u)[:, 0:keys], ACT.Exp,
                                   bias=low[:, u:u + 1], scale=-1.0, accum_out=total[:, u:u + 1]).then_inc(probs_ready, 1)
                    if u < UNITS and n % HEADS == HEADS - 1:
                        act.wait_ge(sink_added, t + 1)
                        cols = slice(HEADS * t, HEADS * (t + 1))
                        act.activation(sink_exp[:, cols], sink_exp[:, cols], ACT.Exp).then_inc(sink_done, 1)

            pre_norm(0)

            def rows_and_hankel():
                act.wait_ge(rows_step, N_ROWS)
                act.dma_start(rows_dram, bias_rows).then_inc(rows_stored, 16)
                act.wait_ge(rows_stored, 16)
                for k in range(2):
                    load_hankel(k, k)
            ffn(0, 0, rows_and_hankel)
            post_squares(0)

            n0 = first_block["l0_mix"]
            pre_norm(1)
            j0 = proj_base["w_in0"]
            split_main(n0 + 1)
            project_out(j0, 1, lambda t: [(stage[:, t, 0:512], ps[:, 4 + t, :])])
            split_main(n0 + 2)
            project_out(j0 + 2, 1, lambda t: [(stage[:, t, 512:1024], ps[:, 2 + t, :])])
            copy_bias(0, 4)
            split_main(n0 + 3)
            project_out(j0 + 4, 1, lambda t: [(latent[:, t, :], ps[:, t, 0:160])])
            split_main(n0 + 4)
            lat = ss_of[rstd_base["lat"]]
            for r, (src, width, need) in enumerate(
                    [(stage[:, 0, 768:1024], MLA_Q, 4), (stage[:, 1, 768:1024], MLA_Q, 4),
                     (latent[:, 0, 0:MLA_KV], MLA_KV, 6), (latent[:, 1, 0:MLA_KV], MLA_KV, 6)]):
                act.wait_ge(proj_out, need)
                act.activation(h[:, r % 2, 0:width], src, ACT.Square, accum_out=sumsq[:, lat + r:lat + r + 1])\
                   .then_inc(ss_ready, 1)
                act.wait_ge(ss_ready, lat + r + 1)
            for k in range(3):
                job = job_base["lat"] + k
                act.wait_ge(t_ready, job + 1)
                act.activation(xt_hi[:, k, :], t_bank(job), ACT.Copy, scale=gcol[:, G_Q + k:G_Q + k + 1])\
                   .then_inc(t_hi, 1)
            exps("swa")
            j0 = proj_base["up"]
            scale_b = -MLA_K ** -0.5
            act.wait_ge(pv_ready, UNITS * (ATT["swa"] + 1))
            for t in range(TILES):
                act.wait_ge(proj_ready, j0 + t + 1)
                for b in range(2):
                    act.activation(mla_q[:, t, 4 * b:4 * b + 4, :],
                                   ps[:, 2 * t + b, 0:384].rearrange("p (h c) -> p h c", h=4), ACT.Copy,
                                   scale=scale_b).then_inc(proj_out, 1)
            for t in range(TILES):
                act.wait_ge(proj_ready, j0 + 2 + t + 1)
                act.wait_ge(logits_ready, UNITS * (ATT["swa"] + 1))
                for b in range(2):
                    kv = ps[:, 2 * t + b, :].rearrange("p (h c) -> p h c", h=4)
                    act.activation(mla_k[:, t, 4 * b:4 * b + 4, 0:NOPE], kv[:, :, 0:NOPE], ACT.Copy).then_inc(proj_out, 1)
                    act.activation(val[:, t, 256 * b:256 * b + 256].rearrange("p (h c) -> p h c", h=4),
                                   kv[:, :, NOPE:2 * NOPE], ACT.Copy).then_inc(proj_out, 1)
            split_main(n0 + 5)
            exps("mla")
            act.wait_ge(pv_ready, 2 * UNITS)
            load_gpost("l0_mix")
            for t in range(TILES):
                turned_hi("out0", t)
            split_main(n0 + 6)
            post_squares(1)
            for k in range(3):
                load_hankel(2 + k, k)

            pre_norm(2)
            ffn(1, 2)
            post_squares(2)
            pre_norm(3)
            ffn(2, 3)
            post_squares(3)

            n0 = first_block["l1_mix"]
            pre_norm(4)
            j0 = proj_base["w_in1"]
            split_main(n0 + 1)
            project_out(j0, 4, lambda t: [(stage[:, t, 0:512], ps[:, 4 + t, :])])
            split_main(n0 + 2)
            project_out(j0 + 2, 4, lambda t: [(stage[:, t, 512:896], ps[:, 2 + t, 0:384]),
                                              (val2[:, t, 0, :], ps[:, 2 + t, 384:512])])
            copy_bias(4, 2)
            load_hankel(5, 0)
            copy_bias(6, 4)
            split_main(n0 + 3)
            act.wait_ge(t_ready, job_base["qc"] + 4)
            project_out(j0 + 4, 4, lambda t: [(stage[:, t, 0:P], ps[:, t, 0:P]),
                                              (val2[:, t, 1, :], ps[:, t, P:2 * P]),
                                              (gate[:, t, :], ps[:, t, 2 * P:2 * P + 24])])
            for i, z in enumerate((zk, zv)):
                act.wait_ge(t_done, job_base["kvc"] + i + 1)
                act.activation(z_part(down_hi, i), z, ACT.Copy).then_inc(z_hi, 1)
            for t in range(TILES):
                act.wait_ge(proj_out, OUT["w_in1"][2])
                act.activation(gate[:, t, :], gate[:, t, :], ACT.Exp, scale=-1.0).then_inc(gate_exp, 1)
            copy_bias(10, 2)
            split_main(n0 + 4)
            split_main(n0 + 5)
            for i in range(2):
                act.wait_ge(hid_ready, i + 1)
                act.activation(logit[0:2 * NCMP, i, :], ps[0:2 * NCMP, 2 + i, 0:CMP_HID], ACT.Silu).then_inc(hid_done, 1)
            split_main(n0 + 6)
            act.wait_ge(t_ready, job_base["kw"] + 1)
            project_out(j0 + 6, 4, lambda t: [(stage[:, t, 0:512], ps[:, t, :])])
            split_main(n0 + 7)
            project_out(j0 + 8, 4, lambda t: [(stage[:, t, 512:1024], ps[:, 2 + t, :])])
            for t in range(TILES):
                act.wait_ge(cmp_step, 3 * t + 3)
                act.activation(cmp_view(t), cmp_view(t), ACT.Exp, scale=-1.0).then_inc(cmp_e, 1)
            split_main(n0 + 8)
            project_out(j0 + 10, 4, lambda t: [(val[:, t, :], ps[:, t, :])])
            split_main(n0 + 9)
            exps("slc", "win", "moba")
            act.wait_ge(pv_ready, UNITS * len(ATT))
            load_gpost("l1_mix")
            for t in range(TILES):
                turned_hi("out1", t)
            split_main(n0 + 10)
            post_squares(4)
            pre_norm(5)
            ffn(3, 5)
            post_squares(5)

        @block.tensor
        def _(pe):
            def mm(dst, lhs, rhs, start, stop):
                return pe.matmul(dst, lhs, rhs, start=start, stop=stop, skip_group_check=True)

            def three(dst, lhs_hi, lhs_lo, rhs_hi, rhs_lo, start, stop):
                mm(dst, lhs_hi, rhs_hi, start, False)
                mm(dst, lhs_hi, rhs_lo, False, False)
                return mm(dst, lhs_lo, rhs_hi, False, stop)

            def turn(job, parts):
                if job >= 2:
                    pe.wait_ge(t_done, job - 1)
                for dst, src in parts:
                    ins = pe.transpose(dst, src, ident[0:src.shape[0], 0:src.shape[0]])
                ins.then_inc(t_ready, 1)

            def turn_pairs(name, source, count):
                for k in range(count):
                    bank = t_bank(job_base[name] + k)
                    turn(job_base[name] + k, [(bank[:, t * P:(t + 1) * P], source(t, k)) for t in range(TILES)])

            def turn_whole(src, t, halves=(0, 1)):
                for pair in range(2 * halves[0], 2 * halves[-1] + 2):
                    for k in (2 * pair, 2 * pair + 1):
                        ins = pe.transpose(xt_bank(t, k), src[:, t, k * P:(k + 1) * P], ident[:, :])
                    ins.then_inc(xt_ready, 1)

            def turn_x(s_no, t):
                for half_no in range(2):
                    if s_no == 0:
                        pe.wait_ge(x_landed[t], 16)
                    else:
                        pe.wait_ge(x_new, 4 * (s_no - 1) + 2 * t + half_no + 1)
                    turn_whole(x, t, (half_no,))

            def product(n, t, width, bank, lo=None, chunks=None, midway=None):
                for k in range(KD):
                    if k == KD // 2 and midway:
                        midway()
                    if chunks is not None and k % 2 == 0:
                        need = max(8 * t + k + 2, (10, 16)[t] if chunks.startswith("out") else 0)
                        pe.wait_ge(xt_done, 16 * TURNS[chunks] + need)
                    if k % (KD // 2) == 0:
                        half_no = k // (KD // 2)
                        pe.wait_ge(main_lo, (2 * n + 1 if lo is None else lo) + half_no)
                    ins = three(ps[:, bank, 0:width], xt_hi[:, k, t * P:(t + 1) * P], xt_lo[:, k, t * P:(t + 1) * P],
                                main_view(w_hi, n, k, width), main_view(w_lo, n, k, width), k == 0, k == KD - 1)
                return ins

            def ffn(u, s_no, aside=None):
                n0, d0 = first_block[STAGES[s_no]], u * FBLOCKS
                turn_x(s_no, 0)

                def gate_up(jc, g, between=None):
                    n = n0 + jc
                    first = isinstance(jc, int) and jc == 0
                    for t in range(TILES):
                        if t == 1 and between:
                            between()
                        if d0 + jc >= 1:
                            pe.wait_ge(h_ready, g(2 * (d0 + jc - 1) + t + 1, 2))
                        product(n, t, 512, 4 + t, lo=g(2 * n + 1, 2), chunks=f"norm{s_no}" if first else None,
                                midway=(lambda: turn_x(s_no, 1)) if first and t == 0 else None).then_inc(gu_ready, 1)

                def turn_h(jc, g):
                    pe.wait_ge(h_ready, g(2 * (d0 + jc) + 2, 2))
                    if d0 + jc >= 1:
                        pe.wait_ge(ht_l, g(d0 + jc, 1))
                    for c in range(FC):
                        for t in range(TILES):
                            at = c * SEQ + t * P
                            ins = pe.transpose(ps[:, 6, at:at + P], h[:, t, c * P:(c + 1) * P], ident[:, :])
                    ins.then_inc(ht_ready, 1)

                def down(jc, g):
                    pe.wait_ge(ht_l, g(d0 + jc + 1, 1))
                    last = jc == FBLOCKS - 1
                    order = [(t, part) for t in range(TILES) for part in range(2)]
                    if not last:
                        order = [(t, part) for part in range(2) for t in range(TILES)]
                    for i, (t, part) in enumerate(order):
                        if t == 0:
                            pe.wait_ge(d_lo, g(2 * (d0 + jc) + part + 1, 2))
                        for c in range(FC):
                            cols = slice(c * D + part * 512, c * D + part * 512 + 512)
                            ins = three(ps[:, 2 * t + part, :], ht_hi[:, c, t * P:(t + 1) * P],
                                        ht_lo[:, c, t * P:(t + 1) * P], down_hi[:, cols], down_lo[:, cols],
                                        jc == 0 and c == 0, last and c == FC - 1)
                        if last:
                            ins.then_inc(y_ready, 1)
                        elif i % 2 == 1:
                            ins.then_inc(down_used, 1)

                def fixed(c, k):
                    return c
                gate_up(0, fixed)
                if aside:
                    aside()
                gate_up(1, fixed, between=lambda: turn_h(0, fixed))
                down(0, fixed)
                turn_h(1, fixed)
                gate_up(2, fixed)
                down(1, fixed)
                turn_h(2, fixed)
                with pe.Fori(0, (FBLOCKS - PEEL) // 2) as i:
                    for q in range(2):
                        def looped(c, k, i=i):
                            return c + 2 * k * i
                        gate_up(PEEL + q, looped)
                        down(PEEL + q - 1, looped)
                        turn_h(PEEL + q, looped)
                down(FBLOCKS - 1, fixed)

            def flips(f0, count):
                for f in range(f0, f0 + count):
                    quartet = f // 2 if f < 4 else (f - 4) // 2
                    slot = quartet if quartet < 3 else 0
                    pe.wait_ge(hankel_landed, 16 * (2 if f < 4 else (5 if quartet < 3 else 6)))
                    if f >= 2:
                        pe.wait_ge(flip_done, f - 1)
                    mm(ps[:, 4 + f % 2, :], flip[:, :], hankel[slot][:, 2 * (f % 2):2 * (f % 2) + 2, :].rearrange("p h c -> p (h c)"), True, True)\
                        .then_inc(flip_ready, 1)

            def project(n, job, width, bank, s_no=None, between=None):
                if s_no is not None:
                    turn_x(s_no, 0)
                for t in range(TILES):
                    if t == 1 and between:
                        between()
                    ins = product(n, t, width, bank + t, chunks=None if s_no is None else f"norm{s_no}",
                                  midway=(lambda: turn_x(s_no, 1)) if s_no is not None and t == 0 else None)
                    ins.then_inc(proj_ready, 1)

            def attention(*parts):
                base = UNITS * ATT[parts[0][0]]
                count = UNITS * len(parts)

                def scores(u):
                    _, q_of, k_of, _ = parts[(u - base) // UNITS]
                    t, hh = u % UNITS // HEADS, u % HEADS
                    if u >= 3:
                        pe.wait_ge(logits_ready, u - 2)
                    mm(score_bank(u)[:, 0:P * (t + 1)], q_of(hh)[:, t * P:(t + 1) * P], k_of(hh)[:, 0:P * (t + 1)],
                       True, True).then_inc(scores_ready, 1)

                def turn_probs(u):
                    t = u % UNITS // HEADS
                    pe.wait_ge(probs_ready, u + 1)
                    if u >= 3:
                        pe.wait_ge(pt_copied, u - 2)
                    for kt in range(t + 1):
                        ins = pe.transpose(turned_bank(u)[:, kt * P:(kt + 1) * P], prob_slot(u)[:, kt * P:(kt + 1) * P],
                                           ident[:, :])
                    ins.then_inc(pt_ready, 1)

                def values(u):
                    name, _, _, v_of = parts[(u - base) // UNITS]
                    t, hh = u % UNITS // HEADS, u % HEADS
                    pe.wait_ge(pt_copied, u + 1)
                    if hh == 0 and OUT_BEFORE[name] > 0:
                        pe.wait_ge(head_out, OUT_BEFORE[name] - 1 + t)
                    for kt in range(t + 1):
                        ins = mm(ps[:, 6 + t, hh * HEAD:(hh + 1) * HEAD], probt_slot(u)[:, kt * P:(kt + 1) * P],
                                 v_of(kt, hh), kt == 0, kt == t)
                    ins.then_inc(pv_ready, 1)

                for n in range(count + LAG_V):
                    if n < count:
                        scores(base + n)
                    if LAG_T <= n < count + LAG_T:
                        turn_probs(base + n - LAG_T)
                    if n >= LAG_V:
                        values(base + n - LAG_V)

            def w_out(turned, n):
                for part in range(2):
                    for t in range(TILES):
                        ins = product(n + part, t, 512, 2 * t + part, chunks=turned if part == 0 else None)
                        ins.then_inc(y_ready, 1)

            pe.wait_ge(const_step, 2)
            pe.wait_ge(gains_landed, 16)
            pe.transpose(ps[:, 3, 0:8], grows0, ident[0:8, 0:8]).then_inc(prep_ready, 1)

            def turn_small():
                pe.wait_ge(const_step, N_CONST)
                pe.wait_ge(small_landed, 16 * N_SMALL)
                pe.transpose(ps[:, 7, 0:G_ROWS], grows[:, :], ident[0:G_ROWS, 0:G_ROWS])
                pe.transpose(ps[0:SLOTS, 7, P:P + BUCKETS], table[:, :], ident[0:BUCKETS, 0:BUCKETS])\
                    .then_inc(prep_ready, 1)
            ffn(0, 0, turn_small)

            n0 = first_block["l0_mix"]
            project(n0, 0, 512, 4, s_no=1)
            project(n0 + 1, 2, 512, 2)
            project(n0 + 2, 4, 160, 0)
            pe.wait_ge(proj_out, OUT["w_in0"][0])
            flips(0, 4)
            turn_pairs("qa", lambda t, k: stage[:, t, k * P:(k + 1) * P], 4)
            pe.wait_ge(proj_out, OUT["w_in0"][1])
            turn_pairs("ka", lambda t, k: stage[:, t, 512:512 + P], 1)
            pe.wait_ge(lat_ready, 4)
            turn_pairs("lat", lambda t, k: stage[:, t, 768 + k * P:768 + (k + 1) * P] if k < 2 else latent[:, t, 0:P], 3)
            pe.wait_ge(t_done, job_base["lat"] + 3)
            pe.wait_ge(flip_done, 4)
            attention(("swa", lambda hh: qk[:, hh, :], lambda hh: qk[:, 8, :],
                       lambda kt, hh: stage[:, kt, 640 + HEAD * (hh // 4):640 + HEAD * (hh // 4) + HEAD]))
            n = n0 + len(MIX0_BLOCKS)
            pe.wait_ge(main_lo, 2 * n + 2)
            pe.wait_ge(pt_copied, UNITS)
            pe.wait_ge(logits_ready, UNITS)
            for t in range(TILES):
                for b in range(2):
                    for k in range(2):
                        cols = slice(k * 768 + b * 384, k * 768 + b * 384 + 384)
                        ins = three(ps[:, 2 * t + b, 0:384], xt_hi[:, k, t * P:(t + 1) * P], xt_lo[:, k, t * P:(t + 1) * P],
                                    w_hi[:, n % 2, cols], w_lo[:, n % 2, cols], k == 0, k == 1)
                ins.then_inc(proj_ready, 1)
            for t in range(TILES):
                if t == 0:
                    pe.wait_ge(proj_out, OUT["up"][0])
                for b in range(2):
                    cols = slice(1536 + b * 512, 1536 + b * 512 + 512)
                    ins = three(ps[:, 2 * t + b, :], xt_hi[:, 2, t * P:(t + 1) * P], xt_lo[:, 2, t * P:(t + 1) * P],
                                w_hi[:, n % 2, cols], w_lo[:, n % 2, cols], True, True)
                ins.then_inc(proj_ready, 1)
            pe.wait_ge(proj_out, OUT["up"][1])
            pe.wait_ge(rope_done, 2)
            for i, src in enumerate((mla_q, mla_k)):
                for hh in range(HEADS):
                    job = job_base["mla"] + HEADS * i + hh
                    if i == 0 and hh == 0:
                        pe.wait_ge(head_out, OUT_BEFORE["mla"])
                    turn(job, [(t_bank(job)[0:MLA_K, t * P:(t + 1) * P], src[:, t, hh, :]) for t in range(TILES)])
            pe.wait_ge(t_done, job_base["mla"] + 16)
            attention(("mla", lambda hh: mla_qt[0:MLA_K, hh, :], lambda hh: mla_kt[0:MLA_K, hh, :],
                       lambda kt, hh: val[:, kt, hh * HEAD:(hh + 1) * HEAD]))
            pe.wait_ge(head_out, OUT_BEFORE["slc0"])
            for t in range(TILES):
                turn_whole(attn, t)
            w_out("out0", n0 + 4)

            ffn(1, 2)
            ffn(2, 3)

            n0 = first_block["l1_mix"]
            j0 = proj_base["w_in1"]
            project(n0, j0 + 0, 512, 4, s_no=4)
            project(n0 + 1, j0 + 2, 512, 2)
            pe.wait_ge(proj_out, OUT["w_in1"][0])
            flips(4, 6)
            turn_pairs("qc", lambda t, k: stage[:, t, k * P:(k + 1) * P], 4)
            project(n0 + 2, j0 + 4, 280, 0)
            pe.wait_ge(proj_out, OUT["w_in1"][1])
            turn_pairs("kvc", lambda t, k: stage[:, t, 512 + k * P:512 + (k + 1) * P], 2)
            turn_pairs("ks", lambda t, k: stage[:, t, 768:768 + P], 1)
            pe.wait_ge(proj_out, OUT["w_in1"][2])
            turn_pairs("kw", lambda t, k: stage[:, t, 0:P], 1)
            flips(10, 2)
            for i in range(2):
                n = n0 + 3 + i
                pe.wait_ge(z_lo, i + 1)
                for m in range(16):
                    if m % 8 == 0:
                        pe.wait_ge(main_lo, 2 * n + 1 + m // 8)
                    at = 1024 * i + 2 * NCMP * m
                    cols = slice(m * CMP_HID, (m + 1) * CMP_HID)
                    ins = three(ps[0:120, 2 + i, 0:CMP_HID], down_hi[:, at:at + 120], down_lo[:, at:at + 120],
                                w_hi[:, n % 2, cols], w_lo[:, n % 2, cols], m == 0, m == 15)
                ins.then_inc(hid_ready, 1)

            def turn_hidden():
                pe.wait_ge(flip_done, 12)
                for i in range(2):
                    pe.wait_ge(hid_done, i + 1)
                    for c in range(2):
                        ins = pe.transpose(ps[:, 4 + i, c * 2 * NCMP:(c + 1) * 2 * NCMP],
                                           logit[0:2 * NCMP, i, c * P:(c + 1) * P], ident[0:2 * NCMP, 0:2 * NCMP])
                    ins.then_inc(hid_turned, 1)

            def compressed_kv():
                pe.wait_ge(t_done, job_base["kw"] + 1)
                pe.wait_ge(hid_spread, 5)
                for c in range(2):
                    ins = mm(ps[:, 6, 0:2 * NCMP], w2k[:, c, :, :].rearrange("p a d -> p (a d)"), hid[:, c, :],
                             c == 0, c == 1)
                ins.then_inc(cmp_kv_ready, 1)
                for g in range(2):
                    for c in range(2):
                        ins = mm(ps[:, 7, g * HEAD:(g + 1) * HEAD], hid_rows[:, c, g, :, :].rearrange("p a c -> p (a c)"),
                                 w2v[:, c, :], c == 0, c == 1)
                ins.then_inc(cmp_kv_ready, 1)

            def compressed_scores():
                pe.wait_ge(cmp_kv_done, 2)
                for t in range(TILES):
                    for hh in range(HEADS):
                        ins = mm(ps[:, 4 + t, hh * CPAD:(hh + 1) * CPAD], qk[:, hh, t * P:(t + 1) * P], kcmp, True, True)
                    ins.then_inc(cmp_s_ready, 1)

            def compressed_turns():
                pe.wait_ge(proj_out, OUT["w_in1"][4])
                for t in range(TILES):
                    pe.wait_ge(cmp_p_ready, t + 1)
                    for g in range(2):
                        ins = pe.transpose(ps[:, 2 + t, g * P:(g + 1) * P],
                                           hid_rows[:, t, g, :, :].rearrange("p a c -> p (a c)"), ident[:, :])
                    ins.then_inc(cmp_t_ready, 1)

            project(n0 + 5, j0 + 6, 512, 0, between=turn_hidden)
            compressed_kv()
            project(n0 + 6, j0 + 8, 512, 2, between=compressed_scores)
            pe.wait_ge(proj_out, OUT["w_in1"][3])
            project(n0 + 7, j0 + 10, 512, 0, between=compressed_turns)
            pe.wait_ge(cmp_kv_done, 6)
            for t in range(TILES):
                pe.wait_ge(cmp_t_done, t + 1)
                for g in range(2):
                    ins = mm(ps[:, 6 + t, g * 256:(g + 1) * 256], probt[:, t, g * P:(g + 1) * P],
                             vcmp[:, g, :, :].rearrange("p a d -> p (a d)"), True, True)
                ins.then_inc(cmp_o_ready, 1)
            pe.wait_ge(head_out, OUT_BEFORE["slc"])
            turn_pairs("qd", lambda t, k: stage[:, t, k * P:(k + 1) * P], 4)
            turn_pairs("kd", lambda t, k: stage[:, t, 512 + k * P:512 + (k + 1) * P], 4)
            pe.wait_ge(t_done, job_base["kd"] + 4)
            pe.wait_ge(proj_out, OUT["w_in1"][5])
            attention(("slc", lambda hh: qk[:, hh, :], lambda hh: qk[:, 8, :],
                       lambda kt, hh: val2[:, kt, 0, HEAD * (hh // 4):HEAD * (hh // 4) + HEAD]),
                      ("win", lambda hh: qk[:, hh, :], lambda hh: qk[:, 9, :],
                       lambda kt, hh: val2[:, kt, 1, HEAD * (hh // 4):HEAD * (hh // 4) + HEAD]),
                      ("moba", lambda hh: moba_q[:, 4 * (hh % 2) + hh // 2, :], lambda hh: moba_k[:, hh // 2, :],
                       lambda kt, hh: val[:, kt, hh * HEAD:(hh + 1) * HEAD]))
            pe.wait_ge(head_out, OUT_BEFORE["end"])
            for t in range(TILES):
                turn_whole(attn, t)
            w_out("out1", n0 + 8)

            ffn(3, 5)

        @block.vector
        def _(dve):
            outs = [0]
            shares = [0]

            def split_main(n, hi=None):
                for i, part in enumerate(pieces(n)):
                    dve.wait_ge(main_hi, (2 * n + 1 if hi is None else hi) + i)
                    dve.tensor_tensor(part(w_lo), part(raw), part(w_hi).bitcast(F32), ALU.subtract).then_inc(main_lo, 1)

            def turned_lo(name, t, gain=None):
                for k in range(KD):
                    if k % 2 == 0:
                        dve.wait_ge(xt_h, 16 * TURNS[name] + 8 * t + k + 2)
                    hi = xt_hi[:, k, t * P:(t + 1) * P].bitcast(F32)
                    lo = xt_lo[:, k, t * P:(t + 1) * P]
                    if gain is None:
                        ins = dve.tensor_tensor(lo, xt_bank(t, k), hi, ALU.subtract)
                    else:
                        ins = dve.scalar_tensor_tensor(lo, xt_bank(t, k), gcol[:, gain + k:gain + k + 1], hi,
                                                       ALU.mult, ALU.subtract)
                    ins.then_inc(xt_done, 1)

            def turned_plain(name, count, dst, scale=1.0):
                for k in range(count):
                    job = job_base[name] + k
                    dve.wait_ge(t_ready, job + 1)
                    dve.tensor_scalar(dst(k), t_bank(job), scale, None, ALU.mult).then_inc(t_done, 1)

            def turned_q(name, place):
                for k in range(4):
                    job = job_base[name] + k
                    dve.wait_ge(t_ready, job + 1)
                    for par in range(2):
                        half_no, dst = place(2 * k + par)
                        ins = dve.tensor_scalar(dst[64 * half_no:64 * half_no + 64, :], t_bank(job)[64 * par:64 * par + 64, :],
                                                scale_a, None, ALU.mult)
                    ins.then_inc(t_done, 1)

            def by_group(hh):
                return hh // 4, qk[:, hh, :]

            def pre_norm(s_no, t):
                turned_lo(f"norm{s_no}", t, gain=8 * s_no)

            def post_norm(s_no):
                weight = (0.5 if STAGES[s_no] in FFNS else 1.0) * D ** 0.5
                r = rstd_base[f"post{s_no}"]
                more = s_no + 1 < len(STAGES)
                dve.wait_ge(gpost_landed, 16 * (s_no + 1))
                for t in range(TILES):
                    for part in range(2):
                        cols = slice(part * 512, part * 512 + 512)
                        dve.wait_ge(ss_ready, ss_of[r + t] + part + 1)
                        dve.scalar_tensor_tensor(xn[:, t, cols], ps[:, 2 * t + part, :], weight, gpost[:, cols],
                                                 ALU.mult, ALU.mult).then_inc(y_scaled, 1)
                    if t == 1 and more:
                        pre_norm(s_no + 1, 0)
                    dve.wait_ge(rstd_ready, r + t + 1)
                    for part in range(2):
                        cols = slice(part * 512, part * 512 + 512)
                        dve.wait_ge(y_scaled, 4 * s_no + 2 * t + part + 1)
                        dve.scalar_tensor_tensor(x[:, t, cols], xn[:, t, cols], rstd[:, r + t:r + t + 1], x[:, t, cols],
                                                 ALU.mult, ALU.add).then_inc(x_new, 1)
                if more:
                    pre_norm(s_no + 1, 1)

            def ffn(u, s_no, aside=None):
                n0, d0 = first_block[STAGES[s_no]], u * FBLOCKS

                def mul(jc, t, g):
                    dve.wait_ge(silu_done, g(2 * (d0 + jc) + t + 1, 2))
                    r = rstd_base[f"pre{s_no}"] + t
                    dve.scalar_tensor_tensor(h[:, t, :], ps[:, 4 + t, FB:2 * FB], rstd[:, r:r + 1], h[:, t, :],
                                             ALU.mult, ALU.mult).then_inc(h_ready, 1)

                def turned_h(jc, g):
                    dve.wait_ge(ht_h, g(d0 + jc + 1, 1))
                    dve.tensor_tensor(ht_lo[:, :, :], ps[:, 6, :].rearrange("p (c t) -> p c t", c=FC),
                                      ht_hi[:, :, :].bitcast(F32), ALU.subtract).then_inc(ht_l, 1)

                def down_rows(jc, part, g):
                    dve.wait_ge(d_hi, g(2 * (d0 + jc) + part + 1, 2))
                    dve.tensor_tensor(down_part(down_lo, part), down_part(raw_down, part),
                                      down_part(down_hi, part).bitcast(F32), ALU.subtract).then_inc(d_lo, 1)

                def behind(jc, g):
                    turned_h(jc, g)
                    for part in range(2):
                        down_rows(jc, part, g)

                def step(jc, g, ahead):
                    if jc >= 1:
                        behind(jc - 1, g)
                    mul(jc, 0, g)
                    if ahead:
                        split_main(n0 + jc + 1, hi=g(2 * (n0 + jc + 1) + 1, 2))
                    mul(jc, 1, g)

                def fixed(c, k):
                    return c
                step(0, fixed, True)
                if aside:
                    aside()
                step(1, fixed, True)
                with dve.Fori(0, (FBLOCKS - PEEL) // 2) as i:
                    for q in range(2):
                        step(2 + q, lambda c, k, i=i: c + 2 * k * i, True)
                step(FBLOCKS - 1, fixed, n0 + FBLOCKS < total_blocks)
                down_rows(FBLOCKS - 1, 0, fixed)
                turned_h(FBLOCKS - 1, fixed)
                down_rows(FBLOCKS - 1, 1, fixed)

            def link(ins):
                shares[0] += 1
                ins.then_inc(share_step, 1)
                dve.wait_ge(share_step, shares[0])

            def attention(*parts):
                base = UNITS * ATT[parts[0][0]]
                count = UNITS * len(parts)

                def logits(u):
                    name, bias_of, _ = parts[(u - base) // UNITS]
                    t, hh = u % UNITS // HEADS, u % HEADS
                    keys = P * (t + 1)
                    dve.wait_ge(scores_ready, u + 1)
                    if u >= 6:
                        dve.wait_ge(pt_ready, u - 5)
                    first = neg_sinks[:, hh:hh + 1] if name == "swa" else 3.0e38
                    dve.tensor_tensor_reduce(prob_slot(u)[:, 0:keys], score_bank(u)[:, 0:keys],
                                             bias_of(hh)[:, SEQ - keys:SEQ], 1.0, first, ALU.add, ALU.min,
                                             low[:, u:u + 1]).then_inc(logits_ready, 1)
                    if name == "swa" and hh == HEADS - 1:
                        dve.wait_ge(logits_ready, u + 1)
                        cols = slice(u + 1 - HEADS, u + 1)
                        dve.tensor_tensor(sink_exp[:, cols], low[:, cols], sinks[:, :], ALU.add).then_inc(sink_added, 1)

                def copy(u):
                    keys = P * (u % UNITS // HEADS + 1)
                    dve.wait_ge(pt_ready, u + 1)
                    if u >= 4:
                        dve.wait_ge(pv_ready, u - 3)
                    dve.tensor_copy(probt_slot(u)[:, 0:keys], turned_bank(u)[:, 0:keys]).then_inc(pt_copied, 1)

                for n in range(count + LAG_V + 1):
                    if n < count:
                        logits(base + n)
                    if LAG_T <= n < count + LAG_T:
                        copy(base + n - LAG_T)
                    done = n - LAG_V
                    if done > 0 and done % HEADS == 0:
                        t = (done // HEADS - 1) % TILES
                        dve.wait_ge(pv_ready, base + done)
                        parts[(done - 1) // UNITS][2](t)

            def head_bank(t):
                return ps[:, 6 + t, :].rearrange("p (h d) -> p h d", h=HEADS)

            def finish_plain(name, col, extra=None, gate_no=None, add=False):
                def finish(t):
                    cols = slice(UNITS * ATT[name] + HEADS * t, UNITS * ATT[name] + HEADS * (t + 1))
                    dve.wait_ge(probs_ready, UNITS * ATT[name] + HEADS * (t + 1))
                    source = total[:, cols]
                    if extra is not None:
                        dve.wait_ge(sink_done, t + 1)
                        link(dve.tensor_tensor(share[:, cols], source, sink_exp[:, HEADS * t:HEADS * (t + 1)], ALU.add))
                        source = share[:, cols]
                    link(dve.reciprocal(share[:, cols], source))
                    if gate_no is not None:
                        link(dve.tensor_tensor(share[:, cols], share[:, cols],
                                               gate[:, t, HEADS * gate_no:HEADS * (gate_no + 1)], ALU.mult))
                    weights = spread(share[:, cols], [P, HEADS, HEAD])
                    dst = attn[:, t, col:col + 512].rearrange("p (h d) -> p h d", h=HEADS)
                    outs[0] += 1
                    if add:
                        ins = dve.tensor_tensor(branch, head_bank(t), weights, ALU.mult)
                        ins.then_inc(head_out, 1)
                        dve.wait_ge(head_out, outs[0])
                        link(dve.tensor_tensor(dst, dst, branch, ALU.add))
                    else:
                        dve.tensor_tensor(dst, head_bank(t), weights, ALU.mult).then_inc(head_out, 1)
                return finish

            dve.wait_ge(prep_ready, 1)
            dve.tensor_copy(gcol[:, 0:8], ps[:, 3, 0:8]).then_inc(prep_done, 1)

            def make_rows():
                dve.wait_ge(prep_ready, 2)
                dve.tensor_copy(gcol[:, 8:G_ROWS], ps[:, 7, 8:G_ROWS]).then_inc(prep_done, 1)
                dve.tensor_scalar(neg_table[:, :], ps[0:SLOTS, 7, P:P + BUCKETS], -1.0, None, ALU.mult)\
                   .then_inc(prep_done, 1)
                dve.wait_ge(prep_done, 3)
                dve.memset(bias_rows, BIG).then_inc(rows_step, 1)
                dve.wait_ge(rows_step, 1)
                for b, first, last in BUCKET_RANGES:
                    width = last - first + 1
                    dve.tensor_copy(bias_rows[:, SEQ - 1 - last:SEQ - first],
                                    neg_table[:, b:b + 1].to_broadcast([SLOTS, width])).then_inc(rows_step, 1)
                dve.wait_ge(rows_step, N_ROWS - 1)
                dve.memset(bias_rows[0:HEADS, 0:P], BIG).then_inc(rows_step, 1)
                dve.tensor_scalar(neg_sinks[:, :], sinks[:, :], -1.0, None, ALU.mult).then_inc(neg_sinks_ready, 1)
            pre_norm(0, 0)
            split_main(0)
            pre_norm(0, 1)
            ffn(0, 0, make_rows)
            post_norm(0)

            n0 = first_block["l0_mix"]
            split_main(n0 + 1)
            split_main(n0 + 2)
            dve.wait_ge(q_zeroed, 2)
            turned_q("qa", by_group)
            turned_plain("ka", 1, lambda k: qk[:, 8, :])
            split_main(n0 + 3)
            lat = rstd_base["lat"]
            for r, buf in enumerate([stage[:, 0, 768:1024], stage[:, 1, 768:1024], latent[:, 0, 0:MLA_KV],
                                     latent[:, 1, 0:MLA_KV]]):
                dve.wait_ge(rstd_ready, lat + r + 1)
                dve.tensor_scalar(buf, buf, rstd[:, lat + r:lat + r + 1], None, ALU.mult).then_inc(lat_ready, 1)
            split_main(n0 + 4)
            for k in range(3):
                job = job_base["lat"] + k
                dve.wait_ge(t_hi, k + 1)
                dve.scalar_tensor_tensor(xt_lo[:, k, :], t_bank(job), gcol[:, G_Q + k:G_Q + k + 1],
                                         xt_hi[:, k, :].bitcast(F32), ALU.mult, ALU.subtract).then_inc(t_done, 1)
            dve.wait_ge(neg_sinks_ready, 1)
            dve.wait_ge(flip_done, 4)
            dve.wait_ge(d_lo, 2 * FBLOCKS)
            attention(("swa", lambda hh: bias[:, hh, :], finish_plain("swa", 0, extra=True)))

            def rotate(x1, x2, shape, cos, sin, tmp, done):
                for i, (u, v) in enumerate(((x1, cos), (x2, sin), (x2, cos), (x1, sin))):
                    ins = dve.tensor_tensor(tmp[i], u, v, ALU.mult)
                link(ins)
                dve.tensor_tensor(x1, tmp[0], tmp[1], ALU.subtract).then_inc(rope_step, 1)
                dve.tensor_tensor(x2, tmp[2], tmp[3], ALU.add).then_inc(done, 1)

            half_rope = ROPE // 2
            tmp_flat = logit[:, :, :].rearrange("p a b -> p (a b)")
            dve.wait_ge(proj_out, OUT["w_in0"][2])
            kr = [latent[:, :, MLA_KV + i * half_rope:MLA_KV + (i + 1) * half_rope] for i in range(2)]
            tables = [rope[:, :, i * half_rope:(i + 1) * half_rope] for i in range(2)]
            tmp = [tmp_flat[:, 32 * i:32 * i + 32].rearrange("p (t c) -> p t c", t=TILES) for i in range(4)]
            dve.wait_ge(pt_ready, UNITS)
            rotate(kr[0], kr[1], None, tables[0], tables[1], tmp, kr_done)
            dve.wait_ge(kr_done, 1)
            dve.wait_ge(rope_step, 1)
            dve.wait_ge(proj_out, OUT["up"][0])
            for t in range(TILES):
                qr = [mla_q[:, t, :, NOPE + i * half_rope:NOPE + (i + 1) * half_rope] for i in range(2)]
                wide = [tables[i][:, t, :].unsqueeze(1).to_broadcast([P, HEADS, half_rope]) for i in range(2)]
                tmp = [(tmp_flat if i < 2 else probt[:, :, :].rearrange("p a b -> p (a b)"))
                       [:, P * (2 * t + i % 2) + 128:P * (2 * t + i % 2) + 256].rearrange("p (h c) -> p h c", h=HEADS)
                       for i in range(4)]
                rotate(qr[0], qr[1], None, wide[0], wide[1], tmp, q_rotated)
            dve.wait_ge(q_rotated, 2)
            dve.wait_ge(rope_step, 3)
            for t in range(TILES):
                dve.tensor_copy(mla_k[:, t, :, NOPE:MLA_K],
                                latent[:, t, MLA_KV:MLA_KV + ROPE].unsqueeze(1).to_broadcast([P, HEADS, ROPE]))\
                   .then_inc(rope_done, 1)
            for i, dst in enumerate((mla_qt, mla_kt)):
                for hh in range(HEADS):
                    job = job_base["mla"] + HEADS * i + hh
                    dve.wait_ge(t_ready, job + 1)
                    dve.tensor_copy(dst[0:MLA_K, hh, :], t_bank(job)[0:MLA_K, :]).then_inc(t_done, 1)
            split_main(n0 + 5)
            attention(("mla", lambda hh: causal[:, :], finish_plain("mla", 512)))
            for t in range(TILES):
                turned_lo("out0", t)
            split_main(n0 + 6)
            post_norm(1)

            ffn(1, 2)
            post_norm(2)
            ffn(2, 3)
            post_norm(3)

            n0 = first_block["l1_mix"]
            split_main(n0 + 1)
            dve.wait_ge(q_zeroed, 4)
            turned_q("qc", by_group)
            split_main(n0 + 2)
            for i, z in enumerate((zk, zv)):
                job = job_base["kvc"] + i
                dve.wait_ge(t_ready, job + 1)
                pe_cols = gcol[:, (G_PEK, G_PEV)[i]:(G_PEK, G_PEV)[i] + 16]
                for par in range(2):
                    for g in range(2):
                        rows = slice(64 * par, 64 * par + 64)
                        src = t_bank(job)[64 * g:64 * g + 64, :]
                        src = bass.AP(tensor=src.tensor, offset=src.offset + par,
                                      ap=[list(src.ap[0]), [2, 16], [CMP_STRIDE, NCMP]])
                        ins = dve.tensor_tensor(z[rows, :, g, :], src, spread(pe_cols[rows, :], [64, 16, NCMP]), ALU.add)
                ins.then_inc(t_done, 1)
            turned_plain("ks", 1, lambda k: qk[:, 8, :])
            split_main(n0 + 3)
            for i, z in enumerate((zk, zv)):
                dve.wait_ge(z_hi, i + 1)
                dve.tensor_tensor(z_part(down_lo, i), z, z_part(down_hi, i).bitcast(F32), ALU.subtract).then_inc(z_lo, 1)
            turned_plain("kw", 1, lambda k: qk[:, 9, :])
            split_main(n0 + 4)
            dve.wait_ge(gate_exp, 2)
            dve.tensor_scalar(gate[:, :, :], gate[:, :, :], 1.0, None, ALU.add).then_inc(gate_done, 1)
            dve.wait_ge(gate_done, 1)
            dve.reciprocal(gate[:, :, :], gate[:, :, :]).then_inc(gate_done, 1)
            dve.memset(vcmp, 0.0).then_inc(vcmp_zero, 1)
            split_main(n0 + 5)
            split_main(n0 + 6)
            dve.wait_ge(hid_turned, 1)
            dve.tensor_copy(hid[:, :, :], ps[:, 4, 0:4 * NCMP].rearrange("p (c r) -> p c r", c=2)).then_inc(hid_spread, 1)
            dve.wait_ge(hid_zero, 1)
            dve.wait_ge(hid_turned, 2)
            for c in range(2):
                for g in range(2):
                    at = (2 * c + g) * NCMP
                    dve.tensor_copy(hid_rows[:, c, g, :, 0:NCMP],
                                    ps[:, 5, at:at + NCMP].unsqueeze(1).to_broadcast([P, 4, NCMP])).then_inc(hid_spread, 1)
            dve.wait_ge(cmp_kv_ready, 1)
            for g in range(2):
                rows = slice(64 * g, 64 * g + 64)
                dve.tensor_copy(kcmp[rows, 0:NCMP], ps[rows, 6, g * NCMP:(g + 1) * NCMP]).then_inc(cmp_kv_done, 1)
            dve.wait_ge(cmp_kv_ready, 2)
            dve.wait_ge(vcmp_zero, 1)
            for j in range(4):
                rows = slice(32 * j, 32 * j + 32)
                dve.tensor_copy(vcmp[rows, :, j, :], ps[rows, 7, 0:2 * HEAD].rearrange("p (g d) -> p g d", g=2))\
                   .then_inc(cmp_kv_done, 1)
            split_main(n0 + 7)
            dve.wait_ge(const_step, N_CONST)
            for t in range(TILES):
                dve.wait_ge(cmp_s_ready, t + 1)
                off = cmp_off[:, t, :].unsqueeze(1).to_broadcast([P, HEADS, CPAD])
                dve.tensor_tensor(cmp_view(t), ps[:, 4 + t, 0:HEADS * CPAD].rearrange("p (q c) -> p q c", c=CPAD), off,
                                  ALU.add).then_inc(cmp_step, 1)
                dve.wait_ge(cmp_step, 3 * t + 1)
                dve.tensor_reduce(cmp_low[:, t, :], cmp_view(t), AX, ALU.min).then_inc(cmp_step, 1)
                dve.wait_ge(cmp_step, 3 * t + 2)
                dve.tensor_tensor(cmp_view(t), cmp_view(t), spread(cmp_low[:, t, :], [P, HEADS, CPAD]), ALU.subtract)\
                   .then_inc(cmp_step, 1)
            dve.wait_ge(gate_done, 2)
            for t in range(TILES):
                dve.wait_ge(cmp_e, t + 1)
                link(dve.tensor_reduce(cmp_sum[:, t, :], cmp_view(t), AX, ALU.add))
                ok = cmp_ok[:, t, :].unsqueeze(1).to_broadcast([P, HEADS, CPAD])
                dve.tensor_tensor(cmp_view(t), cmp_view(t), ok, ALU.mult).then_inc(cmp_p_ready, 1)
                link(dve.reciprocal(cmp_sum[:, t, :], cmp_sum[:, t, :]))
                link(dve.tensor_tensor(cmp_sum[:, t, :], cmp_sum[:, t, :], gate[:, t, 0:HEADS], ALU.mult))
            split_main(n0 + 8)
            for t in range(TILES):
                dve.wait_ge(cmp_t_ready, t + 1)
                dve.tensor_copy(probt[:, t, :], ps[:, 2 + t, 0:SEQ]).then_inc(cmp_t_done, 1)
            dve.wait_ge(d_lo, 6 * FBLOCKS)
            for t in range(TILES):
                dve.wait_ge(cmp_o_ready, t + 1)
                outs[0] += 1
                dve.tensor_tensor(attn[:, t, 0:512].rearrange("p (h d) -> p h d", h=HEADS), head_bank(t),
                                  spread(cmp_sum[:, t, :], [P, HEADS, HEAD]), ALU.mult).then_inc(head_out, 1)
            dve.wait_ge(q_zeroed, 6)
            turned_q("qd", lambda hh: (hh % 2, moba_q[:, 4 * (hh % 2) + hh // 2, :]))
            turned_plain("kd", 4, lambda k: moba_k[:, k, :])
            dve.wait_ge(head_out, outs[0])
            split_main(n0 + 9)
            attention(("slc", lambda hh: bias[:, hh, :], finish_plain("slc", 0, gate_no=1, add=True)),
                      ("win", lambda hh: bias[:, hh, :], finish_plain("win", 0, gate_no=2, add=True)),
                      ("moba", lambda hh: bias[:, HEADS + hh, :], finish_plain("moba", 512)))
            for t in range(TILES):
                turned_lo("out1", t)
            split_main(n0 + 10)
            post_norm(4)

            ffn(3, 5)
            post_norm(5)


def rope_tables():
    inv = (np.float32(10000.0) ** (-np.arange(0, ROPE, 2, dtype=np.float32) / np.float32(ROPE))).astype(np.float32)
    angle = np.arange(SEQ, dtype=np.float32)[:, None] * inv[None, :]
    return np.concatenate([np.cos(angle), np.sin(angle)], axis=1).astype(np.float32)


_INS = ["x", "rel_bias_table"]
for _s in STAGES:
    _INS += [f"{_s}_pre", f"{_s}_post"]
    if _s in FFNS:
        _INS += [f"{_s}_wg", f"{_s}_wu", f"{_s}_wd"]
_INS += ["l0_w_in", "l0_sinks", "l0_mla_q_norm", "l0_mla_w_uq", "l0_mla_kv_norm", "l0_mla_w_ukv", "l0_w_out",
         "l1_w_in", "l1_nsa_pe_k", "l1_nsa_pe_v", "l1_nsa_wk1", "l1_nsa_wk2", "l1_nsa_wv1", "l1_nsa_wv2", "l1_w_out"]


def kernel(**inputs):
    import concourse.bacc as bacc
    from concourse.bass_utils import run_bass_kernel_spmd

    nc = bacc.Bacc("TRN2", target_bir_lowering=False, num_devices=1)
    arrays, args = {}, {}
    given = {name: np.ascontiguousarray(inputs[name]) for name in _INS}
    given["rope_tables"] = rope_tables()
    for name, value in given.items():
        arrays[f"in_{name}"] = value
        args[name] = nc.dram_tensor(f"in_{name}", value.shape, mybir.dt.from_np(value.dtype), kind="ExternalInput").ap()
    out = nc.dram_tensor("out_0", (1, SEQ, D), F32, kind="ExternalOutput").ap()
    trunk(nc, args, out)
    result = run_bass_kernel_spmd(nc, [arrays], core_ids=[0])
    return result.results[0]["out_0"]
```

```python
import math
from contextlib import ExitStack

import numpy as np

import concourse.bass as bass
from concourse import mybir

F32 = mybir.dt.float32
F32R = mybir.dt.float32r
ALU = mybir.AluOpType
ACT = mybir.ActivationFunctionType
AX = mybir.AxisListType.X

P = 128
SEQ = 256
TILES = SEQ // P
D = 1024
KD = D // P
DFF = 2816
EPS = 1e-6
BIG = 1e30

HEAD = 64
HEADS = 8
BUCKETS, SLOTS, MAX_DIST = 32, 24, 1024
MLA_Q, MLA_KV, NOPE, ROPE = 256, 128, 64, 32
MLA_K = NOPE + ROPE
CMP_BLOCK, CMP_STRIDE, CMP_HID = 32, 16, 256
NCMP = (SEQ - CMP_BLOCK) // CMP_STRIDE + 1
CPAD = 16
CROW = 32

FB = 256
FBLOCKS = DFF // FB
FC = FB // P
PEEL = 3
MAIN = KD * 512
DOWN = FC * D

FFNS = ("l0_ffn1", "l0_ffn2", "l1_ffn1", "l1_ffn2")
STAGES = ("l0_ffn1", "l0_mix", "l0_ffn2", "l1_ffn1", "l1_mix", "l1_ffn2")
MIX0_BLOCKS = ((512, 512), (1024, 160), (0, 512))
MIX1_BLOCKS = ((512, 512), (0, 512), (1024, 280), "l1_nsa_wk1", "l1_nsa_wv1", (1304, 512), (1816, 512), (2328, 512))


def bucket_ranges():
    n = np.arange(SEQ)
    nf = np.maximum(n, 1).astype(np.float32)
    exact = BUCKETS // 2
    large = exact + (np.log(nf / np.float32(exact)) / np.float32(math.log(MAX_DIST / exact))
                     * np.float32(BUCKETS - exact)).astype(np.int32)
    bucket = np.where(n < exact, n, np.minimum(large, BUCKETS - 1))
    return [(int(b), int(np.flatnonzero(bucket == b)[0]), int(np.flatnonzero(bucket == b)[-1]))
            for b in np.unique(bucket)]


BUCKET_RANGES = bucket_ranges()


def trunk(nc, a, out):
    n_mix0 = len(MIX0_BLOCKS) + 3
    n_mix1 = len(MIX1_BLOCKS) + 2
    counts = {"l0_mix": n_mix0, "l1_mix": n_mix1}
    first_block, n = {}, 0
    for s in STAGES:
        first_block[s] = n
        n += counts.get(s, FBLOCKS)
    total_blocks = n

    def main_dmas(n):
        for s in STAGES:
            if s in FFNS and first_block[s] <= n < first_block[s] + FBLOCKS:
                return 0 if n == 0 else 2
        return 2 if n == first_block["l0_mix"] + len(MIX0_BLOCKS) else 1

    def landed_value(n):
        return 16 * sum(main_dmas(m) for m in range(n % 2, n + 1, 2))

    job_counts = [("ka", 1), ("lat", 3), ("qa", 2), ("mla", 8), ("kvc", 2), ("ks", 1), ("kw", 1),
                  ("qc", 2), ("qd", 2), ("kd", 2)]
    job_base, n = {}, 0
    for name, k in job_counts:
        job_base[name] = n
        n += k

    XT_GROUPS = ((0,), (1, 2), (3, 4), (5, 6, 7))

    TURNS = {name: i for i, name in enumerate(("norm0", "norm1", "out0", "norm2", "norm3", "norm4", "out1", "norm5"))}

    proj_base = {"w_in0": 0, "up": 2 * len(MIX0_BLOCKS), "w_in1": 2 * len(MIX0_BLOCKS) + 4}
    rstd_base, n = {}, 0
    for name, k in [("pre0", 2), ("post0", 2), ("pre1", 2), ("lat", 4), ("post1", 2), ("pre2", 2), ("post2", 2),
                    ("pre3", 2), ("post3", 2), ("pre4", 2), ("post4", 2), ("pre5", 2), ("post5", 2)]:
        rstd_base[name] = n
        n += k
    n_rstd = n
    ss_of, n = {}, 0
    for name, r in rstd_base.items():
        for i in range(4 if name == "lat" else 2):
            ss_of[r + i] = n
            n += 2 if name.startswith("post") else 1
    n_ss = n
    OUT = {"w_in0": [4, 6, 8], "up": [12, 20], "w_in1": [24, 26, 32, 34, 36, 38]}
    ATT = {"swa": 0, "mla": 1, "slc": 2, "win": 3, "moba": 4}
    UNITS = TILES * HEADS
    OUT_BEFORE = {"swa": 0, "mla": 2, "slc0": 4, "slc": 6, "win": 8, "moba": 10, "end": 12}

    LAG_T, LAG_V = 3, 5

    G_PRE, G_Q, G_KV, G_PEK, G_PEV, G_ROWS = 0, 48, 50, 51, 67, 83

    with ExitStack() as ctx:
        def sb(name, shape, dt=F32):
            return ctx.enter_context(nc.sbuf_tensor(name, shape, dt))

        def sem(name):
            return ctx.enter_context(nc.semaphore(name))

        ps = ctx.enter_context(nc.psum_tensor("ps", [P, 8, 512], F32))

        raw = sb("raw", [P, 2, MAIN])
        w_hi = sb("w_hi", [P, 2, MAIN], F32R)
        w_lo = sb("w_lo", [P, 2, MAIN], F32R)
        raw_down = sb("raw_down", [P, DOWN])
        down_hi = sb("down_hi", [P, DOWN], F32R)
        down_lo = sb("down_lo", [P, DOWN], F32R)
        x = sb("x", [P, TILES, D])
        xn = sb("xn", [P, TILES, D])
        xt_hi = sb("xt_hi", [P, KD, SEQ], F32R)
        xt_lo = sb("xt_lo", [P, KD, SEQ], F32R)
        gpost = sb("gpost", [P, D])
        h = sb("h", [P, TILES, FB])
        ht_hi = sb("ht_hi", [P, FC, SEQ], F32R)
        ht_lo = sb("ht_lo", [P, FC, SEQ], F32R)
        bias = sb("bias", [P, 2 * HEADS, SEQ])
        qk = sb("qk", [P, 10, SEQ])
        val = sb("val", [P, TILES, 512])
        val2 = sb("val2", [P, TILES, 2, P])
        logit = sb("logit", [P, 3, SEQ])
        probt = sb("probt", [P, 3, SEQ])
        ident = sb("ident", [P, P])
        causal = sb("causal", [P, SEQ])
        cmp_off = sb("cmp_off", [P, TILES, CPAD])
        cmp_ok = sb("cmp_ok", [P, TILES, CPAD])
        grows = sb("grows", [G_ROWS, P])
        gcol = sb("gcol", [P, G_ROWS])
        table = sb("table", [BUCKETS, SLOTS])
        neg_table = sb("neg_table", [SLOTS, BUCKETS])
        half = sb("half", [P, 1])
        sumsq = sb("sumsq", [P, n_ss])
        meansq = sb("meansq", [P, n_rstd])
        rstd = sb("rstd", [P, n_rstd])
        low = sb("low", [P, len(ATT) * UNITS])
        total = sb("total", [P, len(ATT) * UNITS])
        share = sb("share", [P, len(ATT) * UNITS])
        cmp_low = sb("cmp_low", [P, TILES, HEADS])
        cmp_sum = sb("cmp_sum", [P, TILES, HEADS])
        neg_sinks = sb("neg_sinks", [P, HEADS])
        sinks = sb("sinks", [P, HEADS])
        sink_exp = sb("sink_exp", [P, UNITS])
        gate = sb("gate", [P, TILES, 3 * HEADS])
        rope_cs = sb("rope_cs", [P, TILES, ROPE])
        w2k = sb("w2k", [P, 2, 2, HEAD])
        w2v = sb("w2v", [P, 2, HEAD])
        hid = sb("hid", [P, 2, 2 * NCMP])
        ROW = SEQ + P
        rows_dram = nc.dram_tensor("bias_rows", [SLOTS, P, ROW + 1], F32, kind="Internal").ap()

        grows0 = probt[0:8, 0, 0:P]
        stage = xn
        bias_rows = logit[0:SLOTS, :, :].rearrange("p t c -> p (t c)")[:, 0:SEQ + P]
        attn = raw_down[:, :].rearrange("p (t c) -> p t c", t=TILES)
        latent = val2[:, :, :, :].rearrange("p t a c -> p t (a c)")[:, :, 0:MLA_KV + ROPE]
        mla_qt = bias[:, HEADS:2 * HEADS, :]
        mla_kt = qk
        lat_hi = down_hi[:, 0:3 * SEQ].rearrange("p (k t) -> p k t", k=3)
        lat_lo = down_lo[:, 0:3 * SEQ].rearrange("p (k t) -> p k t", k=3)
        hid_rows = gpost[:, 0:512].rearrange("p (a b j c) -> p a b j c", a=2, b=2, j=4)
        kcmp = gpost[:, 512:512 + CPAD]
        moba_at = (first_block["l1_mix"] + len(MIX1_BLOCKS)) % 2
        moba_q = raw[:, moba_at, 0:8 * SEQ].rearrange("p (h c) -> p h c", h=8)
        moba_k = raw[:, moba_at, 8 * SEQ:12 * SEQ].rearrange("p (h c) -> p h c", h=4)
        mla_q = xn[:, :, 0:HEADS * MLA_K].rearrange("p t (h c) -> p t h c", h=HEADS)
        mla_k = bias[:, 0:6, :].rearrange("p a b -> p (a b)").rearrange("p (t h c) -> p t h c", t=TILES, h=HEADS)
        zk = logit[:, :, :].rearrange("p a b -> p (a b)")[:, 0:480].rearrange("p (m g c) -> p m g c", m=16, g=2)
        zv = probt[:, :, :].rearrange("p a b -> p (a b)")[:, 0:480].rearrange("p (m g c) -> p m g c", m=16, g=2)
        vcmp = h[:, :, :].rearrange("p g (a d) -> p g a d", a=4)
        branch = h[:, :, :].rearrange("p t c -> p (t c)").rearrange("p (h d) -> p h d", h=HEADS)

        def score_bank(u):
            return ps[:, u % 3, :]

        def turned_bank(u):
            return ps[:, 3 + u % 3, :]

        def prob_slot(u):
            return logit[:, u % 6, :] if u % 6 < 3 else gpost[:, (u % 6 - 3) * SEQ:(u % 6 - 2) * SEQ]

        def probt_slot(u):
            return probt[:, u % 4, :] if u % 4 < 3 else gpost[:, 3 * SEQ:4 * SEQ]

        x_landed = [sem("x_landed0"), sem("x_landed1")]
        first_landed = [sem("first_landed0"), sem("first_landed1")]
        small_landed, gains_landed = sem("small_landed"), sem("gains_landed")
        main_landed = [sem("main_landed0"), sem("main_landed1")]
        down_landed = sem("down_landed")
        gpost_landed = sem("gpost_landed")
        rows_stored, bias_landed = sem("rows_stored"), sem("bias_landed")
        main_hi, main_lo = sem("main_hi"), sem("main_lo")
        d_hi, d_lo, down_used = sem("d_hi"), sem("d_lo"), sem("down_used")
        const_step = sem("const_step")
        ss_ready, ms_ready, rstd_ready = sem("ss_ready"), sem("ms_ready"), sem("rstd_ready")
        y_ready = sem("y_ready")
        y_scaled, x_new = sem("y_scaled"), sem("x_new")
        xt_ready, xt_h, xt_done = sem("xt_ready"), sem("xt_h"), sem("xt_done")
        prep_ready, prep_done = sem("prep_ready"), sem("prep_done")
        t_ready, t_hi, t_done = sem("t_ready"), sem("t_hi"), sem("t_done")
        gu_ready, silu_done, h_ready = sem("gu_ready"), sem("silu_done"), sem("h_ready")
        ht_ready, ht_h, ht_l = sem("ht_ready"), sem("ht_h"), sem("ht_l")
        rows_step = sem("rows_step")
        proj_ready, proj_out = sem("proj_ready"), sem("proj_out")
        rope_step = sem("rope_step")
        scores_ready, logits_ready, probs_ready = sem("scores_ready"), sem("logits_ready"), sem("probs_ready")
        pt_ready, pt_copied = sem("pt_ready"), sem("pt_copied")
        pv_ready, head_out, share_step = sem("pv_ready"), sem("head_out"), sem("share_step")
        sink_added, sink_done = sem("sink_added"), sem("sink_done")
        z_hi, z_lo = sem("z_hi"), sem("z_lo")
        hid_ready, hid_done, hid_turned = sem("hid_ready"), sem("hid_done"), sem("hid_turned")
        hid_spread, hid_zero = sem("hid_spread"), sem("hid_zero")
        cmp_kv_ready, cmp_kv_done, vcmp_zero = sem("cmp_kv_ready"), sem("cmp_kv_done"), sem("vcmp_zero")
        cmp_s_ready, cmp_step, cmp_e, cmp_p_ready = sem("cmp_s_ready"), sem("cmp_step"), sem("cmp_e"), sem("cmp_p_ready")
        neg_sinks_ready, q_zeroed = sem("neg_sinks_ready"), sem("q_zeroed")
        cmp_t_ready, cmp_t_done, cmp_o_ready = sem("cmp_t_ready"), sem("cmp_t_done"), sem("cmp_o_ready")
        gate_exp, gate_done = sem("gate_exp"), sem("gate_done")
        stored = sem("stored")
        block = ctx.enter_context(nc.Block())

        scale_a = -HEAD ** -0.5
        N_CONST = 9
        N_SMALL = len(STAGES) + 10
        ROPE_Q, ROPE_ALL = 18, 20
        N_ROWS = len(BUCKET_RANGES) + 2

        def main_view(buf, n, k, width):
            return buf[:, n % 2, k * 512:k * 512 + width]

        def wait_block_used(eng, n, g=lambda c, k: c):
            if n < 0:
                return
            s = next(s for s in reversed(STAGES) if first_block[s] <= n)
            m = n - first_block[s]
            if s in FFNS:
                eng.wait_ge(gu_ready, g(2 * (FFNS.index(s) * FBLOCKS + m + 1), 2))
            elif s == "l0_mix":
                if m <= len(MIX0_BLOCKS):
                    eng.wait_ge(proj_ready, 2 * (m + 1) + (2 if m == len(MIX0_BLOCKS) else 0))
                else:
                    eng.wait_ge(y_ready, 4 + 2 * (m - len(MIX0_BLOCKS)))
            elif m >= len(MIX1_BLOCKS):
                eng.wait_ge(y_ready, 16 + 2 * (m - len(MIX1_BLOCKS) + 1))
            elif isinstance(MIX1_BLOCKS[m], str):
                eng.wait_ge(hid_ready, m - 2)
            else:
                eng.wait_ge(proj_ready, proj_base["w_in1"] + 2 * (m + 1 if m < 3 else m - 1))

        def y_value(s_no, t, part):
            return 4 * s_no + (2 * t + part if STAGES[s_no] in FFNS else 2 * part + t) + 1

        def pieces(n):
            m = n - first_block["l0_mix"]
            if m == len(MIX0_BLOCKS):
                return [lambda b: b[:, n % 2, 0:1536], lambda b: b[:, n % 2, 1536:2560]]
            width = 512
            if 0 <= m < len(MIX0_BLOCKS):
                width = MIX0_BLOCKS[m][1]
            m = n - first_block["l1_mix"]
            if 0 <= m < len(MIX1_BLOCKS) and not isinstance(MIX1_BLOCKS[m], str):
                width = MIX1_BLOCKS[m][1]

            def part(half_no):
                lo, hi = half_no * MAIN // 2, (half_no + 1) * MAIN // 2
                return lambda b: b[:, n % 2, lo:hi].rearrange("p (k c) -> p k c", c=512)[:, :, 0:width]
            return [part(0), part(1)]

        def z_part(buf, i):
            return buf[:, 1024 * i:1024 * i + 480].rearrange("p (m g c) -> p m g c", m=16, g=2)

        def cmp_view(t):
            return hid_rows[:, t, :, :, 0:CPAD].rearrange("p g a c -> p (g a) c")

        def spread(ap, shape):
            return ap.unsqueeze(len(ap.shape)).to_broadcast(shape)

        def xt_bank(t, k):
            i = next(i for i, group in enumerate(XT_GROUPS) if k in group)
            at = k - XT_GROUPS[i][0]
            return ps[:, (4 if t == 0 else 0) + i, at * P:(at + 1) * P]

        def down_part(buf, part):
            return buf[:, :].rearrange("p (c n) -> p c n", c=FC)[:, :, part * 512:part * 512 + 512]

        def t_bank(job):
            return ps[:, 6 + job % 2, 0:SEQ]

        def t_bank_two(job):
            return ps[:, 6 + job % 2, :].rearrange("p (k t) -> p k t", k=2)

        @block.sync
        def _(sp):
            def ffn_main(w, j, n):
                cols = bass.ds(j * FB, FB) if not isinstance(j, int) else slice(j * FB, (j + 1) * FB)
                dst = raw[:, n % 2, :].rearrange("p (k two c) -> p k two c", two=2, c=FB)
                size = KD // 2 if isinstance(n, int) and n == 0 else KD
                for k in range(0, KD, size):
                    if size < KD:
                        t = k // size
                        sp.dma_start(x[:, t, :], a["x"][0, t * P:(t + 1) * P, :]).then_inc(x_landed[t], 16)
                    for i, part in enumerate(("wg", "wu")):
                        src = a[f"{w}_{part}"].rearrange("(k p) n -> p k n", p=P)[:, k:k + size, cols]
                        landed = main_landed[n % 2] if size == KD else first_landed[k // size]
                        sp.dma_start(dst[:, k:k + size, i, :], src).then_inc(landed, 16)

            def ffn_down(w, j):
                rows = a[f"{w}_wd"].rearrange("(j c p) n -> j p c n", p=P, c=FC)
                src = rows[j] if isinstance(j, int) else rows[bass.ds(j, 1)].rearrange("o p c n -> (o p) c n")
                sp.dma_start(raw_down[:, :].rearrange("p (c n) -> p c n", c=FC), src).then_inc(down_landed, 16)

            def ring_wait(n):
                if n >= 2:
                    sp.wait_ge(main_lo, 2 * (n - 1))

            def down_wait(d):
                if d >= 1:
                    sp.wait_ge(d_lo, 2 * d)

            late_down = None
            for s_no, s in enumerate(STAGES):
                n0 = first_block[s]
                if s in FFNS:
                    d0 = FFNS.index(s) * FBLOCKS
                    for j in range(PEEL):
                        ring_wait(n0 + j)
                        if j == 0 and s_no == 5:
                            sp.wait_ge(scores_ready, UNITS * len(ATT))
                        ffn_main(s, j, n0 + j)
                        if j == 0 and late_down:
                            late_down()
                        if j == 1 and s_no > 0 and STAGES[s_no - 1] not in FFNS:
                            sp.wait_ge(xt_ready, 8 * (TURNS["out0" if s_no == 2 else "out1"] + 1))
                        if j >= 1:
                            down_wait(d0 + j - 1)
                            ffn_down(s, j - 1)
                    with sp.Fori(0, (FBLOCKS - PEEL) // 2) as i:
                        for q in range(2):
                            j = PEEL + q
                            sp.wait_ge(main_lo, 4 * i + 2 * (n0 + j - 1))
                            ffn_main(s, 2 * i + j, n0 + j)
                            sp.wait_ge(d_lo, 4 * i + 2 * (d0 + j - 1))
                            ffn_down(s, 2 * i + (j - 1))

                    def late_down(s=s, d=d0 + FBLOCKS - 1):
                        down_wait(d)
                        ffn_down(s, FBLOCKS - 1)
                    if s == STAGES[-1]:
                        late_down()
                    continue
                if s == "l0_mix":
                    for b, (c0, width) in enumerate(MIX0_BLOCKS):
                        ring_wait(n0 + b)
                        dst = raw[:, (n0 + b) % 2, :].rearrange("p (k c) -> p k c", c=512)[:, :, 0:width]
                        sp.dma_start(dst, a["l0_w_in"].rearrange("(k p) n -> p k n", p=P)[:, :, c0:c0 + width])\
                          .then_inc(main_landed[(n0 + b) % 2], 16)
                        if b == 0:
                            late_down()
                            late_down = None
                    n = n0 + len(MIX0_BLOCKS)
                    ring_wait(n)
                    sp.dma_start(raw[:, n % 2, 0:1536].rearrange("p (k c) -> p k c", k=2),
                                 a["l0_mla_w_uq"].rearrange("(k p) n -> p k n", p=P)).then_inc(main_landed[n % 2], 16)
                    sp.dma_start(raw[:, n % 2, 1536:2560], a["l0_mla_w_ukv"]).then_inc(main_landed[n % 2], 16)
                    n += 1
                else:
                    for b, what in enumerate(MIX1_BLOCKS):
                        ring_wait(n0 + b)
                        if isinstance(what, str):
                            sp.dma_start(raw[:, (n0 + b) % 2, :].rearrange("p (m c) -> p m c", c=CMP_HID),
                                         a[what].rearrange("(m p) n -> p m n", p=P)).then_inc(main_landed[(n0 + b) % 2], 16)
                            continue
                        c0, width = what
                        dst = raw[:, (n0 + b) % 2, :].rearrange("p (k c) -> p k c", c=512)[:, :, 0:width]
                        sp.dma_start(dst, a["l1_w_in"].rearrange("(k p) n -> p k n", p=P)[:, :, c0:c0 + width])\
                          .then_inc(main_landed[(n0 + b) % 2], 16)
                        if b == 0:
                            late_down()
                            late_down = None
                    n = n0 + len(MIX1_BLOCKS)
                w_out = a["l0_w_out" if s == "l0_mix" else "l1_w_out"].rearrange("(k p) n -> p k n", p=P)
                for half_no in range(2):
                    ring_wait(n)
                    sp.dma_start(raw[:, n % 2, :].rearrange("p (k c) -> p k c", c=512),
                                 w_out[:, :, half_no * 512:(half_no + 1) * 512]).then_inc(main_landed[n % 2], 16)
                    n += 1
            for t in range(TILES):
                for part in range(2):
                    sp.wait_ge(x_new, 4 * (len(STAGES) - 1) + 2 * t + part + 1)
                    cols = slice(part * 512, part * 512 + 512)
                    sp.dma_start(out[0, t * P:(t + 1) * P, cols], x[:, t, cols]).then_inc(stored, 16)
            sp.wait_ge(stored, 2 * 16 * TILES)

        @block.gpsimd
        def _(pool):
            steps = [0]

            def step(ins):
                steps[0] += 1
                ins.then_inc(const_step, 1)
                pool.wait_ge(const_step, steps[0])

            step(pool.memset(ident[:, :], 0.0))
            step(pool.affine_select(out=ident[:, :], in_=ident[:, :], compare_op=ALU.not_equal, fill=1.0,
                                    base=0, pattern=[[-1, P]], channel_multiplier=1))
            loads = [(table[:, :], a["rel_bias_table"])]
            for s_no, s in enumerate(STAGES):
                loads.append((grows[8 * s_no:8 * s_no + 8, :], a[f"{s}_pre"].rearrange("(c p) -> c p", p=P)))
            loads += [(grows[G_Q:G_Q + 2, :], a["l0_mla_q_norm"].rearrange("(c p) -> c p", p=P)),
                      (grows[G_KV:G_KV + 1, :], a["l0_mla_kv_norm"].rearrange("(c p) -> c p", p=P)),
                      (grows[G_PEK:G_PEK + 16, :], a["l1_nsa_pe_k"].rearrange("(m a) d -> m (a d)", a=2)),
                      (grows[G_PEV:G_PEV + 16, :], a["l1_nsa_pe_v"].rearrange("(m a) d -> m (a d)", a=2)),
                      (w2v[:, :, :], a["l1_nsa_wv2"].rearrange("(k p) d -> p k d", p=P)),
                      (w2k[:, :, 0, :], a["l1_nsa_wk2"].rearrange("(k p) d -> p k d", p=P)),
                      (w2k[:, :, 1, :], a["l1_nsa_wk2"].rearrange("(k p) d -> p k d", p=P)),
                      (rope_cs[:, :, :], a["rope_tables"].rearrange("(t p) c -> p t c", p=P)),
                      (sinks[:, :], bass.AP(tensor=a["l0_sinks"].tensor, offset=0, ap=[[0, P], [1, HEADS]]))]
            assert len(loads) == N_SMALL
            for dst, src in loads:
                pool.dma_start(dst, src).then_inc(small_landed, 16)
            step(pool.memset(causal[:, :], 0.0))
            step(pool.memset(cmp_off[:, :, :], 0.0))
            step(pool.memset(cmp_ok[:, :, :], 1.0))
            step(pool.memset(half[:, :], -0.5))
            step(pool.affine_select(out=causal[:, P:SEQ], in_=causal[:, P:SEQ], compare_op=ALU.is_ge, fill=BIG,
                                    base=0, pattern=[[-1, P]], channel_multiplier=1))
            for m, fill in ((cmp_off, BIG), (cmp_ok, 0.0)):
                step(pool.affine_select(out=m[:, :, :], in_=m[:, :, :], compare_op=ALU.is_ge, fill=fill,
                                        base=1 - CMP_BLOCK, pattern=[[P, TILES], [-CMP_STRIDE, CPAD]],
                                        channel_multiplier=1))

            steps_rope = [0]

            def rope_op(ins):
                steps_rope[0] += 1
                ins.then_inc(rope_step, 1)
                pool.wait_ge(rope_step, steps_rope[0])

            def rotate(x1, x2, cos, sin, tmp):
                for i, (u, v) in enumerate(((x1, cos), (x2, sin), (x2, cos), (x1, sin))):
                    rope_op(pool.tensor_tensor(tmp[i], u, v, ALU.mult))
                rope_op(pool.tensor_tensor(x1, tmp[0], tmp[1], ALU.subtract))
                rope_op(pool.tensor_tensor(x2, tmp[2], tmp[3], ALU.add))

            def rope():
                parts = [slice(i * (ROPE // 2), (i + 1) * (ROPE // 2)) for i in range(2)]
                tmp_flat = h[:, :, :].rearrange("p t c -> p (t c)")
                tables = [rope_cs[:, :, part] for part in parts]
                pool.wait_ge(small_landed, 16 * N_SMALL)
                pool.wait_ge(ss_ready, ss_of[lat] + 4)
                pool.wait_ge(proj_out, OUT["w_in0"][1])
                tmp = [tmp_flat[:, 32 * i:32 * i + 32].rearrange("p (t c) -> p t c", t=TILES) for i in range(4)]
                k_rope = latent[:, :, MLA_KV:MLA_KV + ROPE]
                rotate(k_rope[:, :, parts[0]], k_rope[:, :, parts[1]], tables[0], tables[1], tmp)
                pool.wait_ge(proj_out, OUT["up"][0])
                tmp = [tmp_flat[:, P * i:P * (i + 1)].rearrange("p (h c) -> p h c", h=HEADS) for i in range(4)]
                for t in range(TILES):
                    q_rope = mla_q[:, t, :, NOPE:MLA_K]
                    wide = [table[:, t, :].unsqueeze(1).to_broadcast([P, HEADS, ROPE // 2]) for table in tables]
                    rotate(q_rope[:, :, parts[0]], q_rope[:, :, parts[1]], wide[0], wide[1], tmp)
                pool.wait_ge(logits_ready, UNITS)
                for t in range(TILES):
                    rope_op(pool.tensor_copy(mla_k[:, t, :, NOPE:MLA_K],
                                             k_rope[:, t, :].unsqueeze(1).to_broadcast([P, HEADS, ROPE])))

            zeroed = [0]

            def zero_q(buf):
                for i in range(2):
                    pool.memset(buf[64 * (1 - i):64 * (2 - i), 4 * i:4 * i + 4, :], 0.0).then_inc(q_zeroed, 1)
                    zeroed[0] += 1
                    pool.wait_ge(q_zeroed, zeroed[0])
            lat = rstd_base["lat"]
            for r in range(n_rstd):
                if r == lat:
                    pool.wait_ge(rstd_ready, r)
                    zero_q(qk)
                if r == rstd_base["post1"]:
                    pool.wait_ge(rstd_ready, r)
                    rope()
                if r == rstd_base["post4"]:
                    pool.wait_ge(rstd_ready, r)
                    pool.wait_ge(x_new, 4 * 4)
                    pool.memset(gpost[:, 0:512 + CPAD], 0.0).then_inc(hid_zero, 1)
                    pool.wait_ge(hid_zero, 1)
                    zero_q(qk)
                    pool.wait_ge(main_lo, 2 * (first_block["l1_mix"] + len(MIX1_BLOCKS) + 1))
                    zero_q(moba_q)
                size = D if not lat <= r < lat + 4 else (MLA_Q if r < lat + 2 else MLA_KV)
                c = ss_of[r]
                if ss_of.get(r + 1, n_ss) == c + 2:
                    pool.wait_ge(ss_ready, c + 2)
                    pool.tensor_scalar(meansq[:, r:r + 1], sumsq[:, c:c + 1], sumsq[:, c + 1:c + 2], D * EPS, ALU.add,
                                       ALU.add).then_inc(ms_ready, 1)
                else:
                    pool.wait_ge(ss_ready, c + 1)
                    pool.tensor_scalar(meansq[:, r:r + 1], sumsq[:, c:c + 1], 1.0 / size, EPS, ALU.mult, ALU.add)\
                        .then_inc(ms_ready, 1)
                pool.wait_ge(ms_ready, r + 1)
                pool.tensor_tensor(rstd[:, r:r + 1], meansq[:, r:r + 1], half[:, :], ALU.pow).then_inc(rstd_ready, 1)

        @block.scalar
        def _(act):
            act.dma_start(grows0, a[f"{STAGES[0]}_pre"].rearrange("(c p) -> c p", p=P)).then_inc(gains_landed, 16)

            def load_bias(first, count):
                src = bass.AP(tensor=rows_dram.tensor, offset=first * P * (ROW + 1) + P - 1,
                              ap=[[ROW, P], [P * (ROW + 1), count], [1, SEQ]])
                act.dma_start(bias[:, 0:count, :], src).then_inc(bias_landed, 16)

            def load_gpost(s):
                act.dma_start(gpost[:, :], bass.AP(tensor=a[f"{s}_post"].tensor, offset=0, ap=[[0, P], [1, D]]))\
                   .then_inc(gpost_landed, 16)

            def split_main(n, g=lambda c, k: c):
                if n > 0:
                    act.wait_ge(main_landed[n % 2], g(landed_value(n), 32))
                wait_block_used(act, n - 2, g)
                for i, part in enumerate(pieces(n)):
                    if n == 0:
                        act.wait_ge(first_landed[i], 32)
                    act.activation(part(w_hi), part(raw), ACT.Copy).then_inc(main_hi, 1)

            def turned_hi(name, t, gain=None):
                base = TURNS[name]
                for i, group in enumerate(XT_GROUPS):
                    act.wait_ge(xt_ready, 8 * base + 4 * t + i + 1)
                    for k in group:
                        kw = {} if gain is None else {"scale": gcol[:, gain + k:gain + k + 1]}
                        act.activation(xt_hi[:, k, t * P:(t + 1) * P], xt_bank(t, k), ACT.Copy, **kw).then_inc(xt_h, 1)

            def pre_norm(s_no):
                if s_no == 0:
                    act.wait_ge(prep_done, 1)
                for t in range(TILES):
                    turned_hi(f"norm{s_no}", t, gain=8 * s_no)
                    if s_no == 0 and t == 0:
                        split_main(0)
                    r = ss_of[rstd_base[f"pre{s_no}"] + t]
                    act.activation(xn[:, t, :], x[:, t, :], ACT.Square, accum_out=sumsq[:, r:r + 1]).then_inc(ss_ready, 1)
                if STAGES[s_no] in FFNS:
                    load_gpost(STAGES[s_no])

            def post_squares(s_no):
                for t in range(TILES):
                    for part in range(2):
                        act.wait_ge(y_ready, y_value(s_no, t, part))
                        if t == 1:
                            act.wait_ge(y_scaled, 4 * s_no + part + 1)
                        r = ss_of[rstd_base[f"post{s_no}"] + t] + part
                        act.activation(ps[:, (6, 0)[t] + part, :], ps[:, 2 * t + part, :], ACT.Square,
                                       accum_out=sumsq[:, r:r + 1]).then_inc(ss_ready, 1)

            def ffn(u, s_no, aside=None, later=()):
                n0, d0 = first_block[STAGES[s_no]], u * FBLOCKS

                def silu(jc, t, g):
                    act.wait_ge(gu_ready, g(2 * (d0 + jc) + t + 1, 2))
                    if d0 + jc >= 1:
                        act.wait_ge(ht_ready, g(d0 + jc, 1))
                    r = rstd_base[f"pre{s_no}"] + t
                    if isinstance(jc, int) and jc == 0:
                        act.wait_ge(rstd_ready, r + 1)
                    act.activation(h[:, t, :], ps[:, 4 + t, 0:FB], ACT.Silu, scale=rstd[:, r:r + 1]).then_inc(silu_done, 1)

                def turned_h(jc, g):
                    act.wait_ge(ht_ready, g(d0 + jc + 1, 1))
                    dst = xt_hi[:, 0:FC, :] if jc == FBLOCKS - 1 else ht_hi[:, :, :]
                    act.activation(dst, ps[:, 6, :].rearrange("p (c t) -> p c t", c=FC), ACT.Copy).then_inc(ht_h, 1)

                def down_rows(jc, part, g):
                    if part == 0:
                        act.wait_ge(down_landed, g(16 * (d0 + jc + 1), 16))
                    act.activation(down_part(down_hi, part), down_part(raw_down, part), ACT.Copy).then_inc(d_hi, 1)

                def behind(jc, g):
                    turned_h(jc, g)
                    for part in range(2):
                        down_rows(jc, part, g)

                def step(jc, g, ahead):
                    if jc >= 1:
                        behind(jc - 1, g)
                    silu(jc, 0, g)
                    if ahead:
                        split_main(n0 + jc + 1, g)
                    silu(jc, 1, g)

                def fixed(c, k):
                    return c
                step(0, fixed, True)
                if aside:
                    aside()
                step(1, fixed, True)
                if later:
                    later[0]()
                with act.Fori(0, (FBLOCKS - PEEL) // 2) as i:
                    for q in range(2):
                        step(2 + q, lambda c, k, i=i: c + (2 * k if k != 32 else 32) * i, True)
                if later:
                    later[1]()
                step(FBLOCKS - 1, fixed, n0 + FBLOCKS < total_blocks)
                act.wait_ge(down_used, 2 * (d0 - u + FBLOCKS - 2) + 1)
                down_rows(FBLOCKS - 1, 0, fixed)
                turned_h(FBLOCKS - 1, fixed)
                act.wait_ge(down_used, 2 * (d0 - u + FBLOCKS - 1))
                down_rows(FBLOCKS - 1, 1, fixed)

            def project_out(j0, s_no, copies):
                for t in range(TILES):
                    r = rstd_base[f"pre{s_no}"] + t
                    act.wait_ge(rstd_ready, r + 1)
                    act.wait_ge(proj_ready, j0 + t + 1)
                    for dst, src in copies(t):
                        act.activation(dst, src, ACT.Copy, scale=rstd[:, r:r + 1]).then_inc(proj_out, 1)

            def exps(*names):
                base = UNITS * ATT[names[0]]
                for u in range(base, base + UNITS * len(names)):
                    n = u % UNITS
                    t = n // HEADS
                    keys = P * (t + 1)
                    act.wait_ge(logits_ready, u + 1)
                    act.activation(prob_slot(u)[:, 0:keys], prob_slot(u)[:, 0:keys], ACT.Exp,
                                   bias=low[:, u:u + 1], scale=-1.0, accum_out=total[:, u:u + 1]).then_inc(probs_ready, 1)
                    if u < UNITS and n % HEADS == HEADS - 1:
                        act.wait_ge(sink_added, t + 1)
                        cols = slice(HEADS * t, HEADS * (t + 1))
                        act.activation(sink_exp[:, cols], sink_exp[:, cols], ACT.Exp).then_inc(sink_done, 1)

            pre_norm(0)

            def store_rows():
                act.wait_ge(rows_step, N_ROWS)
                store_heads(0)

            def store_heads(first):
                dst = bass.AP(tensor=rows_dram.tensor, offset=first * P * (ROW + 1),
                              ap=[[P * (ROW + 1), HEADS], [ROW + 1, P], [1, ROW]])
                act.dma_start(dst, bias_rows[first:first + HEADS, :].unsqueeze(1).to_broadcast([HEADS, P, ROW]))\
                   .then_inc(rows_stored, 16)
            ffn(0, 0, store_rows, (lambda: store_heads(HEADS), lambda: store_heads(2 * HEADS)))
            act.wait_ge(rows_stored, 3 * 16)
            load_bias(0, HEADS)
            post_squares(0)

            n0 = first_block["l0_mix"]
            pre_norm(1)
            j0 = proj_base["w_in0"]
            split_main(n0 + 1)
            project_out(j0, 1, lambda t: [(stage[:, t, 768:1024], ps[:, 4 + t, 0:256]),
                                          (stage[:, t, 0:256], ps[:, 4 + t, 256:512])])
            split_main(n0 + 2)
            project_out(j0 + 2, 1, lambda t: [(latent[:, t, :], ps[:, 2 + t, 0:160])])
            act.wait_ge(proj_out, OUT["w_in0"][1])
            lat = ss_of[rstd_base["lat"]]
            for r, (src, width) in enumerate([(stage[:, 0, 0:256], MLA_Q), (stage[:, 1, 0:256], MLA_Q),
                                              (latent[:, 0, 0:MLA_KV], MLA_KV), (latent[:, 1, 0:MLA_KV], MLA_KV)]):
                act.activation(h[:, r % 2, 0:width], src, ACT.Square, accum_out=sumsq[:, lat + r:lat + r + 1])\
                   .then_inc(ss_ready, 1)
                if r == 1:
                    act.wait_ge(ss_ready, lat + 2)
            split_main(n0 + 3)
            for k in range(3):
                job = job_base["lat"] + k
                act.wait_ge(t_ready, job + 1)
                act.activation(lat_hi[:, k, :], t_bank(job), ACT.Copy, scale=gcol[:, G_Q + k:G_Q + k + 1])\
                   .then_inc(t_hi, 1)
            project_out(j0 + 4, 1, lambda t: [(stage[:, t, 256:768], ps[:, t, :])])
            lat, j0 = rstd_base["lat"], proj_base["up"]
            act.wait_ge(rstd_ready, lat + 4)
            act.wait_ge(t_ready, job_base["qa"] + 2)
            for t in range(TILES):
                act.wait_ge(proj_ready, j0 + t + 1)
                for b in range(2):
                    act.activation(mla_q[:, t, 4 * b:4 * b + 4, :],
                                   ps[:, 2 + 2 * t + b, 0:384].rearrange("p (h c) -> p h c", h=4), ACT.Copy,
                                   scale=rstd[:, lat + t:lat + t + 1]).then_inc(proj_out, 1)
            exps("swa")
            split_main(n0 + 4)
            for t in range(TILES):
                act.wait_ge(proj_ready, j0 + 2 + t + 1)
                scale = rstd[:, lat + 2 + t:lat + 3 + t]
                for b in range(2):
                    kv = ps[:, 2 * t + b, :].rearrange("p (h c) -> p h c", h=4)
                    act.activation(mla_k[:, t, 4 * b:4 * b + 4, 0:NOPE], kv[:, :, 0:NOPE], ACT.Copy, scale=scale)\
                       .then_inc(proj_out, 1)
                    act.activation(val[:, t, 256 * b:256 * b + 256].rearrange("p (h c) -> p h c", h=4),
                                   kv[:, :, NOPE:2 * NOPE], ACT.Copy, scale=scale).then_inc(proj_out, 1)
            exps("mla")
            split_main(n0 + 5)
            act.wait_ge(pv_ready, 2 * UNITS)
            load_gpost("l0_mix")
            load_bias(HEADS, 2 * HEADS)
            for t in range(TILES):
                turned_hi("out0", t)
            split_main(n0 + 6)
            post_squares(1)
            pre_norm(2)
            ffn(1, 2)
            post_squares(2)
            pre_norm(3)
            ffn(2, 3)
            post_squares(3)

            n0 = first_block["l1_mix"]
            pre_norm(4)
            j0 = proj_base["w_in1"]
            split_main(n0 + 1)
            project_out(j0, 4, lambda t: [(stage[:, t, 512:896], ps[:, 4 + t, 0:384]),
                                          (val2[:, t, 0, :], ps[:, 4 + t, 384:512])])
            split_main(n0 + 2)
            for i, z in enumerate((zk, zv)):
                act.wait_ge(t_done, job_base["kvc"] + i + 1)
                act.activation(z_part(down_hi, i), z, ACT.Copy).then_inc(z_hi, 1)
            project_out(j0 + 2, 4, lambda t: [(stage[:, t, 0:512], ps[:, 2 + t, :])])
            split_main(n0 + 3)
            project_out(j0 + 4, 4, lambda t: [(stage[:, t, 896:1024], ps[:, t, 0:P]),
                                              (val2[:, t, 1, :], ps[:, t, P:2 * P]),
                                              (gate[:, t, :], ps[:, t, 2 * P:2 * P + 24])])
            for t in range(TILES):
                act.wait_ge(proj_out, OUT["w_in1"][2])
                act.activation(gate[:, t, :], gate[:, t, :], ACT.Exp, scale=-1.0).then_inc(gate_exp, 1)
            split_main(n0 + 4)
            split_main(n0 + 5)
            for i in range(2):
                act.wait_ge(hid_ready, i + 1)
                act.activation(logit[0:2 * NCMP, i, :], ps[0:2 * NCMP, 2 + i, 0:CMP_HID], ACT.Silu).then_inc(hid_done, 1)
            split_main(n0 + 6)
            act.wait_ge(t_ready, job_base["qc"] + 2)
            project_out(j0 + 6, 4, lambda t: [(stage[:, t, 0:512], ps[:, t, :])])
            split_main(n0 + 7)
            project_out(j0 + 8, 4, lambda t: [(stage[:, t, 512:1024], ps[:, 2 + t, :])])
            for t in range(TILES):
                act.wait_ge(cmp_step, 3 * t + 3)
                act.activation(cmp_view(t), cmp_view(t), ACT.Exp, scale=-1.0).then_inc(cmp_e, 1)
            split_main(n0 + 8)
            project_out(j0 + 10, 4, lambda t: [(val[:, t, :], ps[:, t, :])])
            split_main(n0 + 9)
            exps("slc", "win", "moba")
            act.wait_ge(pv_ready, UNITS * len(ATT))
            load_gpost("l1_mix")
            for t in range(TILES):
                turned_hi("out1", t)
            split_main(n0 + 10)
            post_squares(4)
            pre_norm(5)
            ffn(3, 5)
            post_squares(5)

        @block.tensor
        def _(pe):
            def mm(dst, lhs, rhs, start, stop):
                return pe.matmul(dst, lhs, rhs, start=start, stop=stop, skip_group_check=True)

            def three(dst, lhs_hi, lhs_lo, rhs_hi, rhs_lo, start, stop):
                mm(dst, lhs_hi, rhs_hi, start, False)
                mm(dst, lhs_hi, rhs_lo, False, False)
                return mm(dst, lhs_lo, rhs_hi, False, stop)

            def turn(job, parts):
                if job >= 2:
                    pe.wait_ge(t_done, job - 1)
                for dst, src in parts:
                    ins = pe.transpose(dst, src, ident[0:src.shape[0], 0:src.shape[0]])
                ins.then_inc(t_ready, 1)

            def turn_pairs(name, source, count):
                for k in range(count):
                    bank = t_bank(job_base[name] + k)
                    turn(job_base[name] + k, [(bank[:, t * P:(t + 1) * P], source(t, k)) for t in range(TILES)])

            def turn_two(job, source, rows=P):
                turn(job, [(t_bank_two(job)[0:rows, i, t * P:(t + 1) * P], source(t, i))
                           for i in range(2) for t in range(TILES)])

            def turn_four(name, at):
                for i in range(2):
                    turn_two(job_base[name] + i, lambda t, k: stage[:, t, at + (2 * i + k) * P:at + (2 * i + k + 1) * P])

            def turn_whole(src, t, before=lambda k: None):
                for group in XT_GROUPS:
                    before(group[-1])
                    for k in group:
                        ins = pe.transpose(xt_bank(t, k), src[:, t, k * P:(k + 1) * P], ident[:, :])
                    ins.then_inc(xt_ready, 1)

            def turn_x(s_no, t):
                def x_is_new(k):
                    if s_no == 0:
                        pe.wait_ge(x_landed[t], 16)
                    else:
                        pe.wait_ge(x_new, 4 * (s_no - 1) + 2 * t + k // (KD // 2) + 1)
                turn_whole(x, t, x_is_new)

            def product(n, t, width, bank, lo=None, chunks=None, midway=None):
                for k in range(KD):
                    if k == KD // 2 and midway:
                        midway()
                    if chunks is not None:
                        need = max(8 * t + k + 1, (9, 16)[t] if chunks.startswith("out") else 0)
                        pe.wait_ge(xt_done, 16 * TURNS[chunks] + need)
                    if k % (KD // 2) == 0:
                        half_no = k // (KD // 2)
                        pe.wait_ge(main_lo, (2 * n + 1 if lo is None else lo) + half_no)
                    ins = three(ps[:, bank, 0:width], xt_hi[:, k, t * P:(t + 1) * P], xt_lo[:, k, t * P:(t + 1) * P],
                                main_view(w_hi, n, k, width), main_view(w_lo, n, k, width), k == 0, k == KD - 1)
                return ins

            def ffn(u, s_no, aside=None):
                n0, d0 = first_block[STAGES[s_no]], u * FBLOCKS
                turn_x(s_no, 0)

                def gate_up(jc, g, between=None):
                    n = n0 + jc
                    first = isinstance(jc, int) and jc == 0
                    for t in range(TILES):
                        if t == 1 and between:
                            between()
                        if d0 + jc >= 1:
                            pe.wait_ge(h_ready, g(2 * (d0 + jc - 1) + t + 1, 2))
                        product(n, t, 512, 4 + t, lo=g(2 * n + 1, 2), chunks=f"norm{s_no}" if first else None,
                                midway=(lambda: turn_x(s_no, 1)) if first and t == 0 else None).then_inc(gu_ready, 1)

                def turn_h(jc, g):
                    pe.wait_ge(h_ready, g(2 * (d0 + jc) + 2, 2))
                    if d0 + jc >= 1:
                        pe.wait_ge(ht_l, g(d0 + jc, 1))
                    for c in range(FC):
                        for t in range(TILES):
                            at = c * SEQ + t * P
                            ins = pe.transpose(ps[:, 6, at:at + P], h[:, t, c * P:(c + 1) * P], ident[:, :])
                    ins.then_inc(ht_ready, 1)

                def down(jc, g, parts=(0, 1)):
                    last = jc == FBLOCKS - 1
                    if parts[0] == 0:
                        pe.wait_ge(ht_l, g(d0 + jc + 1, 1))
                    hi, lo = (xt_hi, xt_lo) if last else (ht_hi, ht_lo)
                    order = [(t, part) for t in range(TILES) for part in range(2)]
                    if not last:
                        order = [(t, part) for part in parts for t in range(TILES)]
                    for i, (t, part) in enumerate(order):
                        if t == 0:
                            pe.wait_ge(d_lo, g(2 * (d0 + jc) + part + 1, 2))
                        for c in range(FC):
                            cols = slice(c * D + part * 512, c * D + part * 512 + 512)
                            ins = three(ps[:, 2 * t + part, :], hi[:, c, t * P:(t + 1) * P],
                                        lo[:, c, t * P:(t + 1) * P], down_hi[:, cols], down_lo[:, cols],
                                        jc == 0 and c == 0, last and c == FC - 1)
                        if last:
                            ins.then_inc(y_ready, 1)
                        elif i % 2 == 1:
                            ins.then_inc(down_used, 1)

                def fixed(c, k):
                    return c
                gate_up(0, fixed)
                if aside:
                    aside()
                gate_up(1, fixed, between=lambda: turn_h(0, fixed))
                down(0, fixed)
                turn_h(1, fixed)
                gate_up(2, fixed)
                down(1, fixed)
                turn_h(2, fixed)
                with pe.Fori(0, (FBLOCKS - PEEL) // 2 - 1) as i:
                    for q in range(2):
                        def looped(c, k, i=i):
                            return c + 2 * k * i
                        gate_up(PEEL + q, looped)
                        down(PEEL + q - 1, looped)
                        turn_h(PEEL + q, looped)
                gate_up(FBLOCKS - 2, fixed)
                down(FBLOCKS - 3, fixed)
                turn_h(FBLOCKS - 2, fixed)
                gate_up(FBLOCKS - 1, fixed)
                down(FBLOCKS - 2, fixed, parts=(0,))
                turn_h(FBLOCKS - 1, fixed)
                down(FBLOCKS - 2, fixed, parts=(1,))
                down(FBLOCKS - 1, fixed)

            def project(n, job, width, bank, s_no=None, between=None):
                if s_no is not None:
                    turn_x(s_no, 0)
                for t in range(TILES):
                    if t == 1 and between:
                        between()
                    ins = product(n, t, width, bank + t, chunks=None if s_no is None else f"norm{s_no}",
                                  midway=(lambda: turn_x(s_no, 1)) if s_no is not None and t == 0 else None)
                    ins.then_inc(proj_ready, 1)

            def attention(*parts):
                base = UNITS * ATT[parts[0][0]]
                count = UNITS * len(parts)

                def scores(u):
                    _, q_of, k_of, _ = parts[(u - base) // UNITS]
                    t, hh = u % UNITS // HEADS, u % HEADS
                    if u >= 3:
                        pe.wait_ge(logits_ready, u - 2)
                    mm(score_bank(u)[:, 0:P * (t + 1)], q_of(hh)[:, t * P:(t + 1) * P], k_of(hh)[:, 0:P * (t + 1)],
                       True, True).then_inc(scores_ready, 1)

                def turn_probs(u):
                    t = u % UNITS // HEADS
                    pe.wait_ge(probs_ready, u + 1)
                    if u >= 3:
                        pe.wait_ge(pt_copied, u - 2)
                    for kt in range(t + 1):
                        ins = pe.transpose(turned_bank(u)[:, kt * P:(kt + 1) * P], prob_slot(u)[:, kt * P:(kt + 1) * P],
                                           ident[:, :])
                    ins.then_inc(pt_ready, 1)

                def values(u):
                    name, _, _, v_of = parts[(u - base) // UNITS]
                    t, hh = u % UNITS // HEADS, u % HEADS
                    pe.wait_ge(pt_copied, u + 1)
                    if hh == 0 and OUT_BEFORE[name] > 0:
                        pe.wait_ge(head_out, OUT_BEFORE[name] - 1 + t)
                    for kt in range(t + 1):
                        ins = mm(ps[:, 6 + t, hh * HEAD:(hh + 1) * HEAD], probt_slot(u)[:, kt * P:(kt + 1) * P],
                                 v_of(kt, hh), kt == 0, kt == t)
                    ins.then_inc(pv_ready, 1)

                for n in range(count + LAG_V):
                    if n < count:
                        scores(base + n)
                    if LAG_T <= n < count + LAG_T:
                        turn_probs(base + n - LAG_T)
                    if n >= LAG_V:
                        values(base + n - LAG_V)

            def w_out(turned, n):
                for part in range(2):
                    for t in range(TILES):
                        ins = product(n + part, t, 512, 2 * t + part, chunks=turned if part == 0 else None)
                        ins.then_inc(y_ready, 1)

            pe.wait_ge(const_step, 2)
            pe.wait_ge(gains_landed, 16)
            pe.transpose(ps[:, 3, 0:8], grows0, ident[0:8, 0:8]).then_inc(prep_ready, 1)

            def turn_small():
                pe.wait_ge(const_step, N_CONST)
                pe.wait_ge(small_landed, 16 * N_SMALL)
                pe.transpose(ps[:, 7, 0:G_ROWS], grows[:, :], ident[0:G_ROWS, 0:G_ROWS])
                pe.transpose(ps[0:SLOTS, 7, P:P + BUCKETS], table[:, :], ident[0:BUCKETS, 0:BUCKETS])\
                    .then_inc(prep_ready, 1)
            ffn(0, 0, turn_small)

            n0 = first_block["l0_mix"]
            project(n0, 0, 512, 4, s_no=1)
            project(n0 + 1, 2, 160, 2)

            def turn_k_and_latents():
                pe.wait_ge(proj_out, OUT["w_in0"][0])
                turn_pairs("ka", lambda t, k: stage[:, t, 768:768 + P], 1)
                pe.wait_ge(proj_out, OUT["w_in0"][1])
                turn_pairs("lat", lambda t, k: stage[:, t, k * P:(k + 1) * P] if k < 2 else latent[:, t, 0:P], 3)
            project(n0 + 2, 4, 512, 0, between=turn_k_and_latents)
            pe.wait_ge(proj_out, OUT["w_in0"][2])
            turn_four("qa", 256)
            n = n0 + len(MIX0_BLOCKS)
            pe.wait_ge(t_done, job_base["lat"] + 3)
            pe.wait_ge(main_lo, 2 * n + 2)
            for t in range(TILES):
                for b in range(2):
                    for k in range(2):
                        cols = slice(k * 768 + b * 384, k * 768 + b * 384 + 384)
                        ins = three(ps[:, 2 + 2 * t + b, 0:384], lat_hi[:, k, t * P:(t + 1) * P],
                                    lat_lo[:, k, t * P:(t + 1) * P], w_hi[:, n % 2, cols], w_lo[:, n % 2, cols],
                                    k == 0, k == 1)
                ins.then_inc(proj_ready, 1)
            pe.wait_ge(t_done, job_base["qa"] + 2)
            pe.wait_ge(proj_out, OUT["up"][0])
            attention(("swa", lambda hh: qk[:, hh, :], lambda hh: qk[:, 8, :],
                       lambda kt, hh: stage[:, kt, 896 + HEAD * (hh // 4):896 + HEAD * (hh // 4) + HEAD]))
            pe.wait_ge(pt_copied, UNITS)
            pe.wait_ge(logits_ready, UNITS)
            for t in range(TILES):
                for b in range(2):
                    cols = slice(1536 + b * 512, 1536 + b * 512 + 512)
                    ins = three(ps[:, 2 * t + b, :], lat_hi[:, 2, t * P:(t + 1) * P], lat_lo[:, 2, t * P:(t + 1) * P],
                                w_hi[:, n % 2, cols], w_lo[:, n % 2, cols], True, True)
                ins.then_inc(proj_ready, 1)
            for i, src in enumerate((mla_q, mla_k)):
                pe.wait_ge(rope_step, (ROPE_Q, ROPE_ALL)[i])
                if i == 1:
                    pe.wait_ge(proj_out, OUT["up"][1])
                for hh in range(0, HEADS, 2):
                    if i == 0 and hh == 0:
                        pe.wait_ge(head_out, OUT_BEFORE["mla"])
                    turn_two(job_base["mla"] + (HEADS * i + hh) // 2, lambda t, k: src[:, t, hh + k, :], rows=MLA_K)
            pe.wait_ge(t_done, job_base["mla"] + 8)
            attention(("mla", lambda hh: mla_qt[0:MLA_K, hh, :], lambda hh: mla_kt[0:MLA_K, hh, :],
                       lambda kt, hh: val[:, kt, hh * HEAD:(hh + 1) * HEAD]))
            pe.wait_ge(head_out, OUT_BEFORE["slc0"])
            for t in range(TILES):
                turn_whole(attn, t)
            w_out("out0", n0 + 4)

            ffn(1, 2)
            ffn(2, 3)

            n0 = first_block["l1_mix"]
            j0 = proj_base["w_in1"]
            project(n0, j0 + 0, 512, 4, s_no=4)

            def turn_compressed_inputs():
                pe.wait_ge(proj_out, OUT["w_in1"][0])
                turn_pairs("kvc", lambda t, k: stage[:, t, 512 + k * P:512 + (k + 1) * P], 2)
                turn_pairs("ks", lambda t, k: stage[:, t, 768:768 + P], 1)

            def turn_q():
                pe.wait_ge(proj_out, OUT["w_in1"][1])
                turn_four("qc", 0)
            project(n0 + 1, j0 + 2, 512, 2, between=turn_compressed_inputs)
            project(n0 + 2, j0 + 4, 280, 0)
            pe.wait_ge(proj_out, OUT["w_in1"][2])
            turn_pairs("kw", lambda t, k: stage[:, t, 896:1024], 1)
            for i in range(2):
                n = n0 + 3 + i
                if i == 1:
                    turn_q()
                pe.wait_ge(z_lo, i + 1)
                for m in range(16):
                    if m % 8 == 0:
                        pe.wait_ge(main_lo, 2 * n + 1 + m // 8)
                    at = 1024 * i + 2 * NCMP * m
                    cols = slice(m * CMP_HID, (m + 1) * CMP_HID)
                    ins = three(ps[0:120, 2 + i, 0:CMP_HID], down_hi[:, at:at + 120], down_lo[:, at:at + 120],
                                w_hi[:, n % 2, cols], w_lo[:, n % 2, cols], m == 0, m == 15)
                ins.then_inc(hid_ready, 1)

            def turn_hidden():
                for i in range(2):
                    pe.wait_ge(hid_done, i + 1)
                    for c in range(2):
                        ins = pe.transpose(ps[:, 4 + i, c * 2 * NCMP:(c + 1) * 2 * NCMP],
                                           logit[0:2 * NCMP, i, c * P:(c + 1) * P], ident[0:2 * NCMP, 0:2 * NCMP])
                    ins.then_inc(hid_turned, 1)

            def compressed_kv():
                pe.wait_ge(t_done, job_base["qc"] + 2)
                pe.wait_ge(hid_spread, 5)
                for c in range(2):
                    ins = mm(ps[:, 6, 0:2 * NCMP], w2k[:, c, :, :].rearrange("p a d -> p (a d)"), hid[:, c, :],
                             c == 0, c == 1)
                ins.then_inc(cmp_kv_ready, 1)
                for g in range(2):
                    for c in range(2):
                        ins = mm(ps[:, 7, g * HEAD:(g + 1) * HEAD], hid_rows[:, c, g, :, :].rearrange("p a c -> p (a c)"),
                                 w2v[:, c, :], c == 0, c == 1)
                ins.then_inc(cmp_kv_ready, 1)

            def compressed_scores(t):
                pe.wait_ge(cmp_kv_done, 2)
                for hh in range(HEADS):
                    ins = mm(ps[:, 4 + t, hh * CPAD:(hh + 1) * CPAD], qk[:, hh, t * P:(t + 1) * P], kcmp, True, True)
                ins.then_inc(cmp_s_ready, 1)

            def compressed_turns():
                pe.wait_ge(proj_out, OUT["w_in1"][4])
                for t in range(TILES):
                    pe.wait_ge(cmp_p_ready, t + 1)
                    for g in range(2):
                        ins = pe.transpose(ps[:, 2 + t, g * P:(g + 1) * P],
                                           hid_rows[:, t, g, :, :].rearrange("p a c -> p (a c)"), ident[:, :])
                    ins.then_inc(cmp_t_ready, 1)

            project(n0 + 5, j0 + 6, 512, 0, between=turn_hidden)
            compressed_kv()
            project(n0 + 6, j0 + 8, 512, 2, between=lambda: compressed_scores(0))
            compressed_scores(1)
            pe.wait_ge(proj_out, OUT["w_in1"][3])
            project(n0 + 7, j0 + 10, 512, 0, between=compressed_turns)
            pe.wait_ge(cmp_kv_done, 6)
            for t in range(TILES):
                pe.wait_ge(cmp_t_done, t + 1)
                for g in range(2):
                    ins = mm(ps[:, 6 + t, g * 256:(g + 1) * 256], probt[:, t, g * P:(g + 1) * P],
                             vcmp[:, g, :, :].rearrange("p a d -> p (a d)"), True, True)
                ins.then_inc(cmp_o_ready, 1)
            pe.wait_ge(head_out, OUT_BEFORE["slc"])
            turn_four("qd", 0)
            turn_four("kd", 512)
            pe.wait_ge(t_done, job_base["kd"] + 2)
            pe.wait_ge(proj_out, OUT["w_in1"][5])
            attention(("slc", lambda hh: qk[:, hh, :], lambda hh: qk[:, 8, :],
                       lambda kt, hh: val2[:, kt, 0, HEAD * (hh // 4):HEAD * (hh // 4) + HEAD]),
                      ("win", lambda hh: qk[:, hh, :], lambda hh: qk[:, 9, :],
                       lambda kt, hh: val2[:, kt, 1, HEAD * (hh // 4):HEAD * (hh // 4) + HEAD]),
                      ("moba", lambda hh: moba_q[:, 4 * (hh % 2) + hh // 2, :], lambda hh: moba_k[:, hh // 2, :],
                       lambda kt, hh: val[:, kt, hh * HEAD:(hh + 1) * HEAD]))
            pe.wait_ge(head_out, OUT_BEFORE["end"])
            for t in range(TILES):
                turn_whole(attn, t)
            w_out("out1", n0 + 8)

            ffn(3, 5)

        @block.vector
        def _(dve):
            outs = [0]
            shares = [0]

            def split_main(n, hi=None, which=(0, 1)):
                for i in which:
                    part = pieces(n)[i]
                    dve.wait_ge(main_hi, (2 * n + 1 if hi is None else hi) + i)
                    dve.tensor_tensor(part(w_lo), part(raw), part(w_hi).bitcast(F32), ALU.subtract).then_inc(main_lo, 1)

            def turned_lo(name, t, gain=None, chunks=range(KD)):
                for k in chunks:
                    group = next(group for group in XT_GROUPS if k in group)
                    if k == group[0]:
                        dve.wait_ge(xt_h, 16 * TURNS[name] + 8 * t + group[-1] + 1)
                    hi = xt_hi[:, k, t * P:(t + 1) * P].bitcast(F32)
                    lo = xt_lo[:, k, t * P:(t + 1) * P]
                    if gain is None:
                        ins = dve.tensor_tensor(lo, xt_bank(t, k), hi, ALU.subtract)
                    else:
                        ins = dve.scalar_tensor_tensor(lo, xt_bank(t, k), gcol[:, gain + k:gain + k + 1], hi,
                                                       ALU.mult, ALU.subtract)
                    ins.then_inc(xt_done, 1)

            def turned_plain(name, count, dst, scale=1.0):
                for k in range(count):
                    job = job_base[name] + k
                    dve.wait_ge(t_ready, job + 1)
                    dve.tensor_scalar(dst(k), t_bank(job), scale, None, ALU.mult).then_inc(t_done, 1)

            def turned_q(name, half_of, slots_of):
                for i in range(2):
                    job = job_base[name] + i
                    dve.wait_ge(t_ready, job + 1)
                    for par in range(2):
                        rows = slice(64 * half_of(i, par), 64 * half_of(i, par) + 64)
                        ins = dve.tensor_scalar(slots_of(i, par)[rows, :, :], t_bank_two(job)[64 * par:64 * par + 64, :, :],
                                                scale_a, None, ALU.mult)
                    ins.then_inc(t_done, 1)

            def turned_by_group(name):
                heads = qk[:, 0:HEADS, :].rearrange("p (i k par) c -> p i par k c", i=2, par=2)
                turned_q(name, lambda i, par: i, lambda i, par: heads[:, i, par, :, :])

            def pre_norm(s_no, t):
                turned_lo(f"norm{s_no}", t, gain=8 * s_no)

            def post_norm(s_no):
                weight = (0.5 if STAGES[s_no] in FFNS else 1.0) * D ** 0.5
                r = rstd_base[f"post{s_no}"]
                more = s_no + 1 < len(STAGES)
                dve.wait_ge(gpost_landed, 16 * (s_no + 1))
                for t in range(TILES):
                    for part in range(2):
                        cols = slice(part * 512, part * 512 + 512)
                        dve.wait_ge(ss_ready, ss_of[r + t] + part + 1)
                        dve.scalar_tensor_tensor(xn[:, t, cols], ps[:, 2 * t + part, :], weight, gpost[:, cols],
                                                 ALU.mult, ALU.mult).then_inc(y_scaled, 1)
                    if t == 1 and more:
                        pre_norm(s_no + 1, 0)
                    dve.wait_ge(rstd_ready, r + t + 1)
                    for part in range(2):
                        cols = slice(part * 512, part * 512 + 512)
                        dve.wait_ge(y_scaled, 4 * s_no + 2 * t + part + 1)
                        dve.scalar_tensor_tensor(x[:, t, cols], xn[:, t, cols], rstd[:, r + t:r + t + 1], x[:, t, cols],
                                                 ALU.mult, ALU.add).then_inc(x_new, 1)
                if more:
                    pre_norm(s_no + 1, 1)

            def ffn(u, s_no, aside=None):
                n0, d0 = first_block[STAGES[s_no]], u * FBLOCKS

                def mul(jc, t, g):
                    dve.wait_ge(silu_done, g(2 * (d0 + jc) + t + 1, 2))
                    r = rstd_base[f"pre{s_no}"] + t
                    dve.scalar_tensor_tensor(h[:, t, :], ps[:, 4 + t, FB:2 * FB], rstd[:, r:r + 1], h[:, t, :],
                                             ALU.mult, ALU.mult).then_inc(h_ready, 1)

                def turned_h(jc, g):
                    dve.wait_ge(ht_h, g(d0 + jc + 1, 1))
                    hi, lo = (xt_hi[:, 0:FC, :], xt_lo[:, 0:FC, :]) if jc == FBLOCKS - 1 else (ht_hi[:, :, :], ht_lo[:, :, :])
                    dve.tensor_tensor(lo, ps[:, 6, :].rearrange("p (c t) -> p c t", c=FC), hi.bitcast(F32), ALU.subtract)\
                       .then_inc(ht_l, 1)

                def down_rows(jc, part, g):
                    dve.wait_ge(d_hi, g(2 * (d0 + jc) + part + 1, 2))
                    dve.tensor_tensor(down_part(down_lo, part), down_part(raw_down, part),
                                      down_part(down_hi, part).bitcast(F32), ALU.subtract).then_inc(d_lo, 1)

                def behind(jc, g):
                    turned_h(jc, g)
                    for part in range(2):
                        down_rows(jc, part, g)

                def step(jc, g, ahead):
                    if jc >= 1:
                        behind(jc - 1, g)
                    mul(jc, 0, g)
                    if ahead:
                        split_main(n0 + jc + 1, hi=g(2 * (n0 + jc + 1) + 1, 2))
                    mul(jc, 1, g)

                def fixed(c, k):
                    return c
                step(0, fixed, True)
                if aside:
                    aside()
                step(1, fixed, True)
                with dve.Fori(0, (FBLOCKS - PEEL) // 2) as i:
                    for q in range(2):
                        step(2 + q, lambda c, k, i=i: c + 2 * k * i, True)
                step(FBLOCKS - 1, fixed, n0 + FBLOCKS < total_blocks)
                down_rows(FBLOCKS - 1, 0, fixed)
                turned_h(FBLOCKS - 1, fixed)
                down_rows(FBLOCKS - 1, 1, fixed)

            def link(ins):
                shares[0] += 1
                ins.then_inc(share_step, 1)
                dve.wait_ge(share_step, shares[0])

            def attention(*parts):
                base = UNITS * ATT[parts[0][0]]
                count = UNITS * len(parts)

                def logits(u):
                    name, bias_of, _ = parts[(u - base) // UNITS]
                    t, hh = u % UNITS // HEADS, u % HEADS
                    keys = P * (t + 1)
                    dve.wait_ge(scores_ready, u + 1)
                    if u >= 6:
                        dve.wait_ge(pt_ready, u - 5)
                    first = neg_sinks[:, hh:hh + 1] if name == "swa" else 3.0e38
                    dve.tensor_tensor_reduce(prob_slot(u)[:, 0:keys], score_bank(u)[:, 0:keys],
                                             bias_of(hh)[:, SEQ - keys:SEQ], 1.0, first, ALU.add, ALU.min,
                                             low[:, u:u + 1]).then_inc(logits_ready, 1)
                    if name == "swa" and hh == HEADS - 1:
                        dve.wait_ge(logits_ready, u + 1)
                        cols = slice(u + 1 - HEADS, u + 1)
                        dve.tensor_tensor(sink_exp[:, cols], low[:, cols], sinks[:, :], ALU.add).then_inc(sink_added, 1)

                def copy(u):
                    keys = P * (u % UNITS // HEADS + 1)
                    dve.wait_ge(pt_ready, u + 1)
                    if u >= 4:
                        dve.wait_ge(pv_ready, u - 3)
                    dve.tensor_copy(probt_slot(u)[:, 0:keys], turned_bank(u)[:, 0:keys]).then_inc(pt_copied, 1)

                for n in range(count + LAG_V + 1):
                    if n < count:
                        logits(base + n)
                    if LAG_T <= n < count + LAG_T:
                        copy(base + n - LAG_T)
                    done = n - LAG_V
                    if done > 0 and done % HEADS == 0:
                        t = (done // HEADS - 1) % TILES
                        dve.wait_ge(pv_ready, base + done)
                        parts[(done - 1) // UNITS][2](t)

            def head_bank(t):
                return ps[:, 6 + t, :].rearrange("p (h d) -> p h d", h=HEADS)

            def finish_plain(name, col, extra=None, gate_no=None, add=False):
                def finish(t):
                    cols = slice(UNITS * ATT[name] + HEADS * t, UNITS * ATT[name] + HEADS * (t + 1))
                    dve.wait_ge(probs_ready, UNITS * ATT[name] + HEADS * (t + 1))
                    source = total[:, cols]
                    if extra is not None:
                        dve.wait_ge(sink_done, t + 1)
                        link(dve.tensor_tensor(share[:, cols], source, sink_exp[:, HEADS * t:HEADS * (t + 1)], ALU.add))
                        source = share[:, cols]
                    link(dve.reciprocal(share[:, cols], source))
                    if gate_no is not None:
                        link(dve.tensor_tensor(share[:, cols], share[:, cols],
                                               gate[:, t, HEADS * gate_no:HEADS * (gate_no + 1)], ALU.mult))
                    weights = spread(share[:, cols], [P, HEADS, HEAD])
                    dst = attn[:, t, col:col + 512].rearrange("p (h d) -> p h d", h=HEADS)
                    outs[0] += 1
                    if add:
                        ins = dve.tensor_tensor(branch, head_bank(t), weights, ALU.mult)
                        ins.then_inc(head_out, 1)
                        dve.wait_ge(head_out, outs[0])
                        link(dve.tensor_tensor(dst, dst, branch, ALU.add))
                    else:
                        dve.tensor_tensor(dst, head_bank(t), weights, ALU.mult).then_inc(head_out, 1)
                return finish

            dve.wait_ge(prep_ready, 1)
            dve.tensor_copy(gcol[:, 0:8], ps[:, 3, 0:8]).then_inc(prep_done, 1)

            def make_rows():
                dve.wait_ge(prep_ready, 2)
                dve.tensor_copy(gcol[:, 8:G_ROWS], ps[:, 7, 8:G_ROWS]).then_inc(prep_done, 1)
                dve.tensor_scalar(neg_table[:, :], ps[0:SLOTS, 7, P:P + BUCKETS], -1.0, None, ALU.mult)\
                   .then_inc(prep_done, 1)
                dve.wait_ge(prep_done, 3)
                dve.memset(bias_rows, BIG).then_inc(rows_step, 1)
                dve.wait_ge(rows_step, 1)
                for b, first, last in BUCKET_RANGES:
                    width = last - first + 1
                    dve.tensor_copy(bias_rows[:, SEQ - 1 - last:SEQ - first],
                                    neg_table[:, b:b + 1].to_broadcast([SLOTS, width])).then_inc(rows_step, 1)
                dve.wait_ge(rows_step, N_ROWS - 1)
                dve.memset(bias_rows[0:HEADS, 0:P], BIG).then_inc(rows_step, 1)
                dve.tensor_scalar(neg_sinks[:, :], sinks[:, :], -1.0, None, ALU.mult).then_inc(neg_sinks_ready, 1)
            pre_norm(0, 0)
            split_main(0)
            pre_norm(0, 1)
            ffn(0, 0, make_rows)
            post_norm(0)

            n0 = first_block["l0_mix"]
            split_main(n0 + 1)
            split_main(n0 + 2)
            turned_plain("ka", 1, lambda k: qk[:, 8, :])
            for k in range(3):
                job = job_base["lat"] + k
                dve.wait_ge(t_hi, k + 1)
                dve.scalar_tensor_tensor(lat_lo[:, k, :], t_bank(job), gcol[:, G_Q + k:G_Q + k + 1],
                                         lat_hi[:, k, :].bitcast(F32), ALU.mult, ALU.subtract).then_inc(t_done, 1)
            split_main(n0 + 3)
            dve.wait_ge(q_zeroed, 2)
            turned_by_group("qa")
            dve.wait_ge(neg_sinks_ready, 1)
            dve.wait_ge(bias_landed, 16)
            dve.wait_ge(d_lo, 2 * FBLOCKS)
            attention(("swa", lambda hh: bias[:, hh, :], finish_plain("swa", 0, extra=True)))
            for i, (dst, scale) in enumerate(((mla_qt, -MLA_K ** -0.5), (mla_kt, 1.0))):
                if i == 0:
                    split_main(n0 + 4, which=(0,))
                for hh in range(0, HEADS, 2):
                    job = job_base["mla"] + (HEADS * i + hh) // 2
                    dve.wait_ge(t_ready, job + 1)
                    dve.tensor_scalar(dst[0:MLA_K, hh:hh + 2, :], t_bank_two(job)[0:MLA_K, :, :], scale, None, ALU.mult)\
                       .then_inc(t_done, 1)
            attention(("mla", lambda hh: causal[:, :], finish_plain("mla", 512)))
            turned_lo("out0", 0)
            turned_lo("out0", 1, chunks=range(1))
            split_main(n0 + 4, which=(1,))
            turned_lo("out0", 1, chunks=range(1, KD))
            split_main(n0 + 5)
            split_main(n0 + 6)
            post_norm(1)

            ffn(1, 2)
            post_norm(2)
            ffn(2, 3)
            post_norm(3)

            n0 = first_block["l1_mix"]
            split_main(n0 + 1)
            split_main(n0 + 2)
            for i, z in enumerate((zk, zv)):
                job = job_base["kvc"] + i
                dve.wait_ge(t_ready, job + 1)
                pe_cols = gcol[:, (G_PEK, G_PEV)[i]:(G_PEK, G_PEV)[i] + 16]
                for par in range(2):
                    for g in range(2):
                        rows = slice(64 * par, 64 * par + 64)
                        src = t_bank(job)[64 * g:64 * g + 64, :]
                        src = bass.AP(tensor=src.tensor, offset=src.offset + par,
                                      ap=[list(src.ap[0]), [2, 16], [CMP_STRIDE, NCMP]])
                        ins = dve.tensor_tensor(z[rows, :, g, :], src, spread(pe_cols[rows, :], [64, 16, NCMP]), ALU.add)
                ins.then_inc(t_done, 1)
            turned_plain("ks", 1, lambda k: qk[:, 8, :])
            for i, z in enumerate((zk, zv)):
                dve.wait_ge(z_hi, i + 1)
                dve.tensor_tensor(z_part(down_lo, i), z, z_part(down_hi, i).bitcast(F32), ALU.subtract).then_inc(z_lo, 1)
            split_main(n0 + 3)
            turned_plain("kw", 1, lambda k: qk[:, 9, :])
            split_main(n0 + 4)
            dve.wait_ge(q_zeroed, 4)
            turned_by_group("qc")
            dve.wait_ge(gate_exp, 2)
            dve.tensor_scalar(gate[:, :, :], gate[:, :, :], 1.0, None, ALU.add).then_inc(gate_done, 1)
            dve.wait_ge(gate_done, 1)
            dve.reciprocal(gate[:, :, :], gate[:, :, :]).then_inc(gate_done, 1)
            dve.memset(vcmp, 0.0).then_inc(vcmp_zero, 1)
            split_main(n0 + 5)
            split_main(n0 + 6)
            dve.wait_ge(hid_turned, 1)
            dve.tensor_copy(hid[:, :, :], ps[:, 4, 0:4 * NCMP].rearrange("p (c r) -> p c r", c=2)).then_inc(hid_spread, 1)
            dve.wait_ge(hid_zero, 1)
            dve.wait_ge(hid_turned, 2)
            for c in range(2):
                for g in range(2):
                    at = (2 * c + g) * NCMP
                    dve.tensor_copy(hid_rows[:, c, g, :, 0:NCMP],
                                    ps[:, 5, at:at + NCMP].unsqueeze(1).to_broadcast([P, 4, NCMP])).then_inc(hid_spread, 1)
            dve.wait_ge(cmp_kv_ready, 1)
            for g in range(2):
                rows = slice(64 * g, 64 * g + 64)
                dve.tensor_copy(kcmp[rows, 0:NCMP], ps[rows, 6, g * NCMP:(g + 1) * NCMP]).then_inc(cmp_kv_done, 1)
            dve.wait_ge(cmp_kv_ready, 2)
            dve.wait_ge(vcmp_zero, 1)
            for j in range(4):
                rows = slice(32 * j, 32 * j + 32)
                dve.tensor_copy(vcmp[rows, :, j, :], ps[rows, 7, 0:2 * HEAD].rearrange("p (g d) -> p g d", g=2))\
                   .then_inc(cmp_kv_done, 1)
            split_main(n0 + 7)
            dve.wait_ge(const_step, N_CONST)
            for t in range(TILES):
                dve.wait_ge(cmp_s_ready, t + 1)
                off = cmp_off[:, t, :].unsqueeze(1).to_broadcast([P, HEADS, CPAD])
                dve.tensor_tensor(cmp_view(t), ps[:, 4 + t, 0:HEADS * CPAD].rearrange("p (q c) -> p q c", c=CPAD), off,
                                  ALU.add).then_inc(cmp_step, 1)
                dve.wait_ge(cmp_step, 3 * t + 1)
                dve.tensor_reduce(cmp_low[:, t, :], cmp_view(t), AX, ALU.min).then_inc(cmp_step, 1)
                dve.wait_ge(cmp_step, 3 * t + 2)
                dve.tensor_tensor(cmp_view(t), cmp_view(t), spread(cmp_low[:, t, :], [P, HEADS, CPAD]), ALU.subtract)\
                   .then_inc(cmp_step, 1)
            dve.wait_ge(gate_done, 2)
            for t in range(TILES):
                dve.wait_ge(cmp_e, t + 1)
                link(dve.tensor_reduce(cmp_sum[:, t, :], cmp_view(t), AX, ALU.add))
                ok = cmp_ok[:, t, :].unsqueeze(1).to_broadcast([P, HEADS, CPAD])
                dve.tensor_tensor(cmp_view(t), cmp_view(t), ok, ALU.mult).then_inc(cmp_p_ready, 1)
                link(dve.reciprocal(cmp_sum[:, t, :], cmp_sum[:, t, :]))
                link(dve.tensor_tensor(cmp_sum[:, t, :], cmp_sum[:, t, :], gate[:, t, 0:HEADS], ALU.mult))
            split_main(n0 + 8)
            for t in range(TILES):
                dve.wait_ge(cmp_t_ready, t + 1)
                dve.tensor_copy(probt[:, t, :], ps[:, 2 + t, 0:SEQ]).then_inc(cmp_t_done, 1)
            dve.wait_ge(d_lo, 6 * FBLOCKS)
            for t in range(TILES):
                dve.wait_ge(cmp_o_ready, t + 1)
                outs[0] += 1
                dve.tensor_tensor(attn[:, t, 0:512].rearrange("p (h d) -> p h d", h=HEADS), head_bank(t),
                                  spread(cmp_sum[:, t, :], [P, HEADS, HEAD]), ALU.mult).then_inc(head_out, 1)
            dve.wait_ge(q_zeroed, 6)
            turned_q("qd", lambda i, par: par, lambda i, par: moba_q[:, 4 * par + 2 * i:4 * par + 2 * i + 2, :])
            for i in range(2):
                job = job_base["kd"] + i
                dve.wait_ge(t_ready, job + 1)
                dve.tensor_copy(moba_k[:, 2 * i:2 * i + 2, :], t_bank_two(job)).then_inc(t_done, 1)
            dve.wait_ge(head_out, outs[0])
            dve.wait_ge(bias_landed, 32)
            attention(("slc", lambda hh: bias[:, hh, :], finish_plain("slc", 0, gate_no=1, add=True)),
                      ("win", lambda hh: bias[:, hh, :], finish_plain("win", 0, gate_no=2, add=True)),
                      ("moba", lambda hh: bias[:, HEADS + hh, :], finish_plain("moba", 512)))
            for t in range(TILES):
                turned_lo("out1", t)
            split_main(n0 + 9)
            split_main(n0 + 10)
            post_norm(4)

            ffn(3, 5)
            post_norm(5)


def rope_tables():
    inv = (np.float32(10000.0) ** (-np.arange(0, ROPE, 2, dtype=np.float32) / np.float32(ROPE))).astype(np.float32)
    angle = np.arange(SEQ, dtype=np.float32)[:, None] * inv[None, :]
    return np.concatenate([np.cos(angle), np.sin(angle)], axis=1).astype(np.float32)


_INS = ["x", "rel_bias_table"]
for _s in STAGES:
    _INS += [f"{_s}_pre", f"{_s}_post"]
    if _s in FFNS:
        _INS += [f"{_s}_wg", f"{_s}_wu", f"{_s}_wd"]
_INS += ["l0_w_in", "l0_sinks", "l0_mla_q_norm", "l0_mla_w_uq", "l0_mla_kv_norm", "l0_mla_w_ukv", "l0_w_out",
         "l1_w_in", "l1_nsa_pe_k", "l1_nsa_pe_v", "l1_nsa_wk1", "l1_nsa_wk2", "l1_nsa_wv1", "l1_nsa_wv2", "l1_w_out"]


def kernel(**inputs):
    import concourse.bacc as bacc
    from concourse.bass_utils import run_bass_kernel_spmd

    nc = bacc.Bacc("TRN2", target_bir_lowering=False, num_devices=1)
    arrays, args = {}, {}
    given = {name: np.ascontiguousarray(inputs[name]) for name in _INS}
    given["rope_tables"] = rope_tables()
    for name, value in given.items():
        arrays[f"in_{name}"] = value
        args[name] = nc.dram_tensor(f"in_{name}", value.shape, mybir.dt.from_np(value.dtype), kind="ExternalInput").ap()
    out = nc.dram_tensor("out_0", (1, SEQ, D), F32, kind="ExternalOutput").ap()
    trunk(nc, args, out)
    result = run_bass_kernel_spmd(nc, [arrays], core_ids=[0])
    return result.results[0]["out_0"]
```
